# Optimizing a Trainium2 kernel written in Bass

```python
import jax, jax.numpy as jnp
from jax import lax
import numpy as np

D_MODEL = 1024
BATCH = 1
SEQ = 256
DEPTH = 2

GRID_W = 64
N_META = 16
HEAD_DIM = 64
ATTN_HEADS = 8
ATTN_KV_HEADS = 2
ATTN_GROUP = ATTN_HEADS // ATTN_KV_HEADS
ATTN_WIDTH = ATTN_HEADS * HEAD_DIM
ATTN_KV_WIDTH = ATTN_KV_HEADS * HEAD_DIM
NA_HEADS = 8
NA_WIDTH = NA_HEADS * HEAD_DIM
NA_KH_MAX = 8
NA_KW = 16
Q_BLOCK = 128
ROPE_THETA = 10000.0
EPS = 1e-6
IN_SPLITS = (ATTN_WIDTH, ATTN_KV_WIDTH, ATTN_KV_WIDTH, ATTN_WIDTH,
             NA_WIDTH, NA_WIDTH, NA_WIDTH, NA_WIDTH, D_MODEL, D_MODEL)
IN_COLS = ATTN_WIDTH * 2 + ATTN_KV_WIDTH * 2 + NA_WIDTH * 4 + D_MODEL * 2


def rms_norm(x, g):
    xf = x.astype(jnp.float32)
    y = xf * lax.rsqrt(jnp.mean(xf * xf, axis=-1, keepdims=True) + EPS)
    return (y * g.astype(jnp.float32)).astype(x.dtype)

def split_cols(p):
    outs, off = [], 0
    for w in IN_SPLITS:
        outs.append(p[..., off:off + w])
        off += w
    return outs

def axial_rope_tables(n_real):
    t = jnp.arange(n_real, dtype=jnp.int32)
    zeros = jnp.zeros((N_META,), jnp.int32)
    row = jnp.concatenate([zeros, t // GRID_W]).astype(jnp.float32)
    col = jnp.concatenate([zeros, t % GRID_W]).astype(jnp.float32)
    axis_dim = HEAD_DIM // 2
    inv = ROPE_THETA ** (-jnp.arange(0, axis_dim, 2, dtype=jnp.float32) / axis_dim)
    ang_r = row[:, None] * inv[None]
    ang_c = col[:, None] * inv[None]
    ang = jnp.concatenate([ang_r, ang_r, ang_c, ang_c], axis=-1)
    return jnp.cos(ang), jnp.sin(ang)

def apply_axial_rope(x, cos, sin):
    axis_dim = HEAD_DIM // 2
    q4 = axis_dim // 2
    xf = x.astype(jnp.float32)
    xr, xc = xf[..., :axis_dim], xf[..., axis_dim:]
    rot = jnp.concatenate([-xr[..., q4:], xr[..., :q4], -xc[..., q4:], xc[..., :q4]], axis=-1)
    return (xf * cos[None, :, None, :] + rot * sin[None, :, None, :]).astype(x.dtype)

def gqa_attention(q, k, v):
    b, l = q.shape[:2]
    n = l - N_META
    scale = HEAD_DIM ** -0.5

    def attend(qb):
        s = jnp.einsum('bqkgd,bskd->bkgqs', qb, k).astype(jnp.float32) * scale
        p = jax.nn.softmax(s, axis=-1).astype(v.dtype)
        return jnp.einsum('bkgqs,bskd->bqkgd', p, v)

    qg = q.reshape(b, l, ATTN_KV_HEADS, ATTN_GROUP, HEAD_DIM)
    o_meta = attend(qg[:, :N_META])
    q_blocks = qg[:, N_META:].reshape(b, n // Q_BLOCK, Q_BLOCK, ATTN_KV_HEADS, ATTN_GROUP, HEAD_DIM)
    q_blocks = q_blocks.transpose(1, 0, 2, 3, 4, 5)
    o_real = lax.map(attend, q_blocks).transpose(1, 0, 2, 3, 4, 5)
    o_real = o_real.reshape(b, n, ATTN_KV_HEADS, ATTN_GROUP, HEAD_DIM)
    return jnp.concatenate([o_meta, o_real], axis=1).reshape(b, l, ATTN_WIDTH)

def neighbourhood_attention(q, k, v, rpb):
    b, l = q.shape[:2]
    n = l - N_META
    rows = n // GRID_W
    kh = min(NA_KH_MAX, rows)
    scale = HEAD_DIM ** -0.5
    qm, km, vm = q[:, :N_META], k[:, :N_META], v[:, :N_META]

    s_mm = jnp.einsum('bqhd,bmhd->bhqm', qm, km).astype(jnp.float32) * scale
    o_meta = jnp.einsum('bhqm,bmhd->bqhd', jax.nn.softmax(s_mm, axis=-1).astype(v.dtype), vm)

    qg = q[:, N_META:].reshape(b, rows, GRID_W, NA_HEADS, HEAD_DIM)
    kg = k[:, N_META:].reshape(b, rows, GRID_W, NA_HEADS, HEAD_DIM)
    vg = v[:, N_META:].reshape(b, rows, GRID_W, NA_HEADS, HEAD_DIM)

    r = jnp.arange(rows)
    row_start = jnp.clip(r - kh // 2, 0, rows - kh)
    row_bias_idx = row_start[:, None] + jnp.arange(kh)[None] - r[:, None] + NA_KH_MAX - 1
    c = jnp.arange(GRID_W)
    col_start = jnp.clip(c - NA_KW // 2, 0, GRID_W - NA_KW)
    col_idx = col_start[:, None] + jnp.arange(NA_KW)[None]
    col_bias_idx = col_idx - c[:, None] + NA_KW - 1
    rpb_cols = rpb[:, :, col_bias_idx]

    def row_step(args):
        q_row, rs, rbi = args
        k_band = lax.dynamic_slice_in_dim(kg, rs, kh, axis=1)
        v_band = lax.dynamic_slice_in_dim(vg, rs, kh, axis=1)
        k_win = k_band[:, :, col_idx]
        v_win = v_band[:, :, col_idx]
        s_win = jnp.einsum('bchd,bicjhd->bhcij', q_row, k_win).astype(jnp.float32) * scale
        bias = rpb_cols[:, rbi].transpose(0, 2, 1, 3)
        s_win = s_win + bias[None].astype(jnp.float32)
        s_meta = jnp.einsum('bchd,bmhd->bhcm', q_row, km).astype(jnp.float32) * scale
        s = jnp.concatenate([s_win.reshape(b, NA_HEADS, GRID_W, kh * NA_KW), s_meta], axis=-1)
        p = jax.nn.softmax(s, axis=-1).astype(v.dtype)
        p_win = p[..., :kh * NA_KW].reshape(b, NA_HEADS, GRID_W, kh, NA_KW)
        p_meta = p[..., kh * NA_KW:]
        return (jnp.einsum('bhcij,bicjhd->bchd', p_win, v_win)
                + jnp.einsum('bhcm,bmhd->bchd', p_meta, vm))

    o_rows = lax.map(row_step, (qg.transpose(1, 0, 2, 3, 4), row_start, row_bias_idx))
    o_real = o_rows.transpose(1, 0, 2, 3, 4).reshape(b, n, NA_WIDTH)
    return jnp.concatenate([o_meta.reshape(b, N_META, NA_WIDTH), o_real], axis=1)

def hybrid_layer(x, norm_g, w_in, q_norm_g, k_norm_g, rpb, w_o_attn, w_o_na, w_out, cos, sin):
    b, l, _ = x.shape
    h = rms_norm(x, norm_g)
    proj = jnp.einsum('bld,de->ble', h, w_in)
    qa, ka, va, za, qb, kb, vb, zb, ga, gb = split_cols(proj)

    qa = apply_axial_rope(rms_norm(qa.reshape(b, l, ATTN_HEADS, HEAD_DIM), q_norm_g), cos, sin)
    ka = apply_axial_rope(rms_norm(ka.reshape(b, l, ATTN_KV_HEADS, HEAD_DIM), k_norm_g), cos, sin)
    va = va.reshape(b, l, ATTN_KV_HEADS, HEAD_DIM)
    oa = gqa_attention(qa, ka, va) * jax.nn.silu(za)

    qb = qb.reshape(b, l, NA_HEADS, HEAD_DIM)
    kb = kb.reshape(b, l, NA_HEADS, HEAD_DIM)
    vb = vb.reshape(b, l, NA_HEADS, HEAD_DIM)
    ob = neighbourhood_attention(qb, kb, vb, rpb) * jax.nn.silu(zb)

    ya = jnp.einsum('ble,ed->bld', oa, w_o_attn)
    yb = jnp.einsum('ble,ed->bld', ob, w_o_na)
    mixed = jax.nn.sigmoid(ga) * ya + jax.nn.sigmoid(gb) * yb
    return x + jnp.einsum('bld,de->ble', mixed, w_out)

def first_inputs(seed: int = 0) -> dict:
    key = jax.random.key(seed)
    ks = jax.random.split(key, 12)
    f32 = jnp.float32
    x = jax.random.normal(ks[0], (BATCH, SEQ, D_MODEL), f32)
    meta_tokens = jax.random.normal(ks[1], (N_META, D_MODEL), f32)
    norm_g = 1.0 + 0.05 * jax.random.normal(ks[2], (DEPTH, D_MODEL), f32)
    w_in = jax.random.normal(ks[3], (DEPTH, D_MODEL, IN_COLS), f32) * D_MODEL ** -0.5
    q_norm_g = 1.0 + 0.05 * jax.random.normal(ks[4], (DEPTH, HEAD_DIM), f32)
    k_norm_g = 1.0 + 0.05 * jax.random.normal(ks[5], (DEPTH, HEAD_DIM), f32)
    na_rpb = 0.1 * jax.random.normal(ks[6], (DEPTH, NA_HEADS, 2 * NA_KH_MAX - 1, 2 * NA_KW - 1), f32)
    w_o_attn = jax.random.normal(ks[7], (DEPTH, ATTN_WIDTH, D_MODEL), f32) * ATTN_WIDTH ** -0.5
    w_o_na = jax.random.normal(ks[8], (DEPTH, NA_WIDTH, D_MODEL), f32) * NA_WIDTH ** -0.5
    w_out = jax.random.normal(ks[9], (DEPTH, D_MODEL, D_MODEL), f32) * D_MODEL ** -0.5
    final_norm_g = 1.0 + 0.05 * jax.random.normal(ks[10], (D_MODEL,), f32)
    return {"x": x, "meta_tokens": meta_tokens, "norm_g": norm_g, "w_in": w_in,
            "q_norm_g": q_norm_g, "k_norm_g": k_norm_g, "na_rpb": na_rpb,
            "w_o_attn": w_o_attn, "w_o_na": w_o_na, "w_out": w_out,
            "final_norm_g": final_norm_g}

def first_block(x, meta_tokens, norm_g, w_in, q_norm_g, k_norm_g, na_rpb, w_o_attn, w_o_na, w_out, final_norm_g):
    b, s, _ = x.shape
    meta = jnp.broadcast_to(meta_tokens[None].astype(x.dtype), (b, N_META, D_MODEL))
    h = jnp.concatenate([meta, x], axis=1)
    cos, sin = axial_rope_tables(s)
    for i in range(DEPTH):
        h = hybrid_layer(h, norm_g[i], w_in[i], q_norm_g[i], k_norm_g[i], na_rpb[i],
                         w_o_attn[i], w_o_na[i], w_out[i], cos, sin)
    h = rms_norm(h, final_norm_g)
    return h[:, N_META:]


N_A = DEPTH // 2
N_B = DEPTH - N_A
M_HEADS = 4
M_DQK = 128
M_DV = D_MODEL // M_HEADS
M_CHUNK = 64
M_SPLITS = [M_HEADS * M_DQK, 2 * M_HEADS * M_DQK, 2 * M_HEADS * M_DQK + M_HEADS * M_DV,
            2 * M_HEADS * M_DQK + 2 * M_HEADS * M_DV, 2 * M_HEADS * M_DQK + 2 * M_HEADS * M_DV + M_HEADS]
M_IN = 2 * M_HEADS * M_DQK + 2 * M_HEADS * M_DV + 2 * M_HEADS
A_HEADS = 8
A_DH = D_MODEL // A_HEADS
ROT_DIM = A_DH // 4
ROPE_THETA_2 = 500000.0
MOBA_BLOCK = 256
MOBA_TOPK = 3
D_FF = 2816
CONV_W = 3


def rmsnorm(x, g):
    xf = x.astype(jnp.float32)
    y = xf * lax.rsqrt(jnp.mean(xf * xf, axis=-1, keepdims=True) + EPS)
    return (y * g.astype(jnp.float32)).astype(x.dtype)

def rope_tables(s_len):
    pos = jnp.arange(s_len, dtype=jnp.float32)
    inv = ROPE_THETA_2 ** (-jnp.arange(0, ROT_DIM, 2, dtype=jnp.float32) / ROT_DIM)
    ang = pos[:, None] * inv[None, :]
    return jnp.cos(ang), jnp.sin(ang)

def apply_partial_rope(t, cos, sin):
    half = ROT_DIM // 2
    t1, t2, rest = t[..., :half], t[..., half:ROT_DIM], t[..., ROT_DIM:]
    c = cos[None, :, None, :].astype(t.dtype)
    s = sin[None, :, None, :].astype(t.dtype)
    return jnp.concatenate([t1 * c - t2 * s, t2 * c + t1 * s, rest], axis=-1)

def mlstm_chunkwise(q, k, v, i_pre, f_pre):
    b_, s_, h_, dk = q.shape
    nc = s_ // M_CHUNK

    def to_chunks(t):
        t = t.astype(jnp.float32).reshape((b_, nc, M_CHUNK, h_) + t.shape[3:])
        return jnp.moveaxis(jnp.moveaxis(t, 1, 0), 3, 2)

    qc, kc, vc = to_chunks(q), to_chunks(k), to_chunks(v)
    ic = to_chunks(i_pre)
    lfc = to_chunks(jax.nn.log_sigmoid(f_pre.astype(jnp.float32)))
    tri = jnp.tril(jnp.ones((M_CHUNK, M_CHUNK), dtype=bool))

    def step(carry, inp):
        c_st, n_st, m_st = carry
        qb, kb, vb, ib, lfb = inp
        bcum = jnp.cumsum(lfb, axis=-1)
        dmat = jnp.where(tri, bcum[..., :, None] - bcum[..., None, :] + ib[..., None, :], -jnp.inf)
        inter = bcum + m_st[..., None]
        m_t = jnp.maximum(inter, jnp.max(dmat, axis=-1))
        w_inter = jnp.exp(inter - m_t)
        s = jnp.einsum('bhtd,bhsd->bhts', qb, kb) * jnp.exp(dmat - m_t[..., None])
        num = w_inter[..., None] * jnp.einsum('bhtd,bhde->bhte', qb, c_st) + jnp.einsum('bhts,bhse->bhte', s, vb)
        den = w_inter * jnp.einsum('bhtd,bhd->bht', qb, n_st) + jnp.sum(s, axis=-1)
        h = num / jnp.maximum(jnp.abs(den), jnp.exp(-m_t))[..., None]
        b_last = bcum[..., -1]
        g = b_last[..., None] - bcum + ib
        m_new = jnp.maximum(b_last + m_st, jnp.max(g, axis=-1))
        decay = jnp.exp(b_last + m_st - m_new)
        wk = jnp.exp(g - m_new[..., None])[..., None] * kb
        c_new = decay[..., None, None] * c_st + jnp.einsum('bhsd,bhse->bhde', wk, vb)
        n_new = decay[..., None] * n_st + jnp.sum(wk, axis=-2)
        return (c_new, n_new, m_new), h

    dv = v.shape[-1]
    init = (jnp.zeros((b_, h_, dk, dv), jnp.float32), jnp.zeros((b_, h_, dk), jnp.float32),
            jnp.zeros((b_, h_), jnp.float32))
    _, hs = lax.scan(step, init, (qc, kc, vc, ic, lfc))
    return jnp.transpose(hs, (1, 0, 3, 2, 4)).reshape(b_, s_, h_, dv)

def mlstm_mixer(x, norm_g, w_in, b_gates, h_norm_g, w_out):
    b_, s_, _ = x.shape
    u = rmsnorm(x, norm_g) @ w_in
    q, k, v, o, gi, gf = jnp.split(u, M_SPLITS, axis=-1)
    q = q.reshape(b_, s_, M_HEADS, M_DQK) * (M_DQK ** -0.5)
    k = k.reshape(b_, s_, M_HEADS, M_DQK)
    v = v.reshape(b_, s_, M_HEADS, M_DV)
    i_pre = gi.astype(jnp.float32) + b_gates[0]
    f_pre = gf.astype(jnp.float32) + b_gates[1]
    h = mlstm_chunkwise(q, k, v, i_pre, f_pre)
    h = rmsnorm(h, h_norm_g.reshape(M_HEADS, M_DV)).reshape(b_, s_, M_HEADS * M_DV)
    h = h * jax.nn.sigmoid(o.astype(jnp.float32))
    return h.astype(x.dtype) @ w_out

def conv_ffn(x, norm_g, w_up, conv_w, conv_b, w_down):
    s_ = x.shape[1]
    u = rmsnorm(x, norm_g) @ w_up
    up = jnp.pad(u, ((0, 0), (CONV_W - 1, 0), (0, 0)))
    c = conv_b + up[:, 0:s_] * conv_w[0]
    for j in range(1, CONV_W):
        c = c + up[:, j:j + s_] * conv_w[j]
    val, gate = jnp.split(c, 2, axis=-1)
    return (jax.nn.silu(gate) * val) @ w_down

def shared_kv(x, norm_g, w_kv, k_norm_g, cos, sin):
    b_, s_, _ = x.shape
    kv = rmsnorm(x, norm_g) @ w_kv
    k, v = jnp.split(kv, 2, axis=-1)
    k = apply_partial_rope(rmsnorm(k.reshape(b_, s_, A_HEADS, A_DH), k_norm_g), cos, sin)
    v = v.reshape(b_, s_, A_HEADS, A_DH)
    nb = -(-s_ // MOBA_BLOCK)
    pad = nb * MOBA_BLOCK - s_
    k = jnp.pad(k, ((0, 0), (0, pad), (0, 0), (0, 0)))
    v = jnp.pad(v, ((0, 0), (0, pad), (0, 0), (0, 0)))
    kb = k.reshape(b_, nb, MOBA_BLOCK, A_HEADS, A_DH).transpose(0, 3, 1, 2, 4)
    vb = v.reshape(b_, nb, MOBA_BLOCK, A_HEADS, A_DH).transpose(0, 3, 1, 2, 4)
    kmean = jnp.mean(kb.astype(jnp.float32), axis=3).astype(kb.dtype)
    return kb, vb, kmean

def moba_mixer(x, norm_g, w_q, q_norm_g, w_o, kb, vb, kmean, cos, sin):
    b_, s_, _ = x.shape
    q = (rmsnorm(x, norm_g) @ w_q).reshape(b_, s_, A_HEADS, A_DH)
    q = apply_partial_rope(rmsnorm(q, q_norm_g), cos, sin) * (A_DH ** -0.5)
    q = q.transpose(0, 2, 1, 3)
    nb = kb.shape[2]
    n_topk = min(MOBA_TOPK, nb)
    bidx = jnp.arange(b_)[:, None, None, None]
    hidx = jnp.arange(A_HEADS)[None, :, None, None]
    n_sel = n_topk * MOBA_BLOCK

    def attend_block(qi):
        start = qi * Q_BLOCK
        cur = start // MOBA_BLOCK
        qb = lax.dynamic_slice_in_dim(q, start, Q_BLOCK, axis=2)
        gate = jnp.einsum('bhqd,bhnd->bhqn', qb, kmean).astype(jnp.float32)
        gate = jnp.where(jnp.arange(nb) < cur, gate, -jnp.inf)
        _, sel = lax.top_k(gate, n_topk)
        sel_valid = jnp.arange(n_topk) < cur
        kg = kb[bidx, hidx, sel]
        vg = vb[bidx, hidx, sel]
        l_sel = jnp.einsum('bhqd,bhqjkd->bhqjk', qb, kg).astype(jnp.float32)
        l_sel = jnp.where(sel_valid[:, None], l_sel, -jnp.inf).reshape(b_, A_HEADS, Q_BLOCK, n_sel)
        ko = lax.dynamic_index_in_dim(kb, cur, axis=2, keepdims=False)
        vo = lax.dynamic_index_in_dim(vb, cur, axis=2, keepdims=False)
        l_own = jnp.einsum('bhqd,bhkd->bhqk', qb, ko).astype(jnp.float32)
        qpos = start + jnp.arange(Q_BLOCK)
        kpos = cur * MOBA_BLOCK + jnp.arange(MOBA_BLOCK)
        l_own = jnp.where(kpos[None, :] <= qpos[:, None], l_own, -jnp.inf)
        p = jax.nn.softmax(jnp.concatenate([l_sel, l_own], axis=-1), axis=-1).astype(vb.dtype)
        p_sel = p[..., :n_sel].reshape(b_, A_HEADS, Q_BLOCK, n_topk, MOBA_BLOCK)
        p_own = p[..., n_sel:]
        return jnp.einsum('bhqjk,bhqjkd->bhqd', p_sel, vg) + jnp.einsum('bhqk,bhkd->bhqd', p_own, vo)

    o = lax.map(attend_block, jnp.arange(s_ // Q_BLOCK))
    o = o.transpose(1, 0, 3, 2, 4).reshape(b_, s_, A_HEADS * A_DH)
    return o @ w_o

def second_inputs(seed: int = 0) -> dict:
    key = jax.random.key(seed)
    ks = jax.random.split(key, 20)
    f32 = jnp.float32

    def w(k, shape, fan_in, scale=1.0):
        return jax.random.normal(k, shape, f32) * (scale * fan_in ** -0.5)

    def gain(k, shape):
        return 1.0 + 0.05 * jax.random.normal(k, shape, f32)

    res_scale = (2 * DEPTH) ** -0.5
    gate_base = jnp.stack([jnp.zeros((M_HEADS,), f32), jnp.linspace(3.0, 6.0, M_HEADS, dtype=f32)])
    return {
        'x': jax.random.normal(ks[0], (BATCH, SEQ, D_MODEL), f32),
        'a_norm': gain(ks[1], (N_A, D_MODEL)),
        'a_w_in': w(ks[2], (N_A, D_MODEL, M_IN), D_MODEL),
        'a_b_gates': gate_base[None] + 0.1 * jax.random.normal(ks[3], (N_A, 2, M_HEADS), f32),
        'a_h_norm': gain(ks[4], (N_A, M_HEADS * M_DV)),
        'a_w_out': w(ks[5], (N_A, D_MODEL, D_MODEL), D_MODEL, res_scale),
        'kv_norm': gain(ks[6], (D_MODEL,)),
        'w_kv': w(ks[7], (D_MODEL, 2 * D_MODEL), D_MODEL),
        'k_norm': gain(ks[8], (A_DH,)),
        'b_norm': gain(ks[9], (N_B, D_MODEL)),
        'b_w_q': w(ks[10], (N_B, D_MODEL, D_MODEL), D_MODEL),
        'b_q_norm': gain(ks[11], (N_B, A_DH)),
        'b_w_o': w(ks[12], (N_B, D_MODEL, D_MODEL), D_MODEL, res_scale),
        'f_norm': gain(ks[13], (DEPTH, D_MODEL)),
        'f_w_up': w(ks[14], (DEPTH, D_MODEL, 2 * D_FF), D_MODEL),
        'f_conv_w': w(ks[15], (DEPTH, CONV_W, 2 * D_FF), CONV_W),
        'f_conv_b': 0.02 * jax.random.normal(ks[16], (DEPTH, 2 * D_FF), f32),
        'f_w_down': w(ks[17], (DEPTH, D_FF, D_MODEL), D_FF, res_scale),
    }

def second_block(x, a_norm, a_w_in, a_b_gates, a_h_norm, a_w_out, kv_norm, w_kv, k_norm,
              b_norm, b_w_q, b_q_norm, b_w_o, f_norm, f_w_up, f_conv_w, f_conv_b, f_w_down):
    cos, sin = rope_tables(x.shape[1])
    h = x
    kb = vb = kmean = None
    for l in range(DEPTH):
        if l < N_A:
            h = h + mlstm_mixer(h, a_norm[l], a_w_in[l], a_b_gates[l], a_h_norm[l], a_w_out[l])
        else:
            j = l - N_A
            h = h + moba_mixer(h, b_norm[j], b_w_q[j], b_q_norm[j], b_w_o[j], kb, vb, kmean, cos, sin)
        h = h + conv_ffn(h, f_norm[l], f_w_up[l], f_conv_w[l], f_conv_b[l], f_w_down[l])
        if l == N_A - 1:
            kb, vb, kmean = shared_kv(h, kv_norm, w_kv, k_norm, cos, sin)
    return h


def setup_inputs(seed=0):
    out = dict(first_inputs(seed))
    for name, value in second_inputs(seed + 1).items():
        if name != "x":
            out[name + "_2"] = value
    return out


def reference(
    x, meta_tokens, norm_g, w_in, q_norm_g, k_norm_g, na_rpb, w_o_attn, w_o_na, w_out,
    final_norm_g, a_norm_2, a_w_in_2, a_b_gates_2, a_h_norm_2, a_w_out_2, kv_norm_2, w_kv_2,
    k_norm_2, b_norm_2, b_w_q_2, b_q_norm_2, b_w_o_2, f_norm_2, f_w_up_2, f_conv_w_2,
    f_conv_b_2, f_w_down_2,
):
    x = first_block(
        x, meta_tokens, norm_g, w_in, q_norm_g, k_norm_g, na_rpb, w_o_attn, w_o_na, w_out,
        final_norm_g,
    )
    return second_block(
        x, a_norm_2, a_w_in_2, a_b_gates_2, a_h_norm_2, a_w_out_2, kv_norm_2, w_kv_2, k_norm_2,
        b_norm_2, b_w_q_2, b_q_norm_2, b_w_o_2, f_norm_2, f_w_up_2, f_conv_w_2, f_conv_b_2,
        f_w_down_2,
    )


_drawn_inputs = setup_inputs


def setup_inputs(seed=0):
    import zlib

    import numpy as np

    out = dict(_drawn_inputs(seed))
    spreads = {}
    factors = {'norm_g': 4.826,
     'q_norm_g': 8.0,
     'k_norm_g': 8.0,
     'na_rpb': 6.885,
     'a_h_norm_2': 4.104,
     'kv_norm_2': 8.0,
     'k_norm_2': 8.0,
     'b_norm_2': 8.0,
     'b_q_norm_2': 8.0,
     'f_conv_b_2': 5.003}
    for name, (base, spread) in spreads.items():
        noise = np.random.default_rng([zlib.crc32(name.encode()), seed]).standard_normal(out[name].shape)
        drawn = base * np.exp(spread * noise) if base else spread * noise
        out[name] = __import__('jax').numpy.asarray(drawn.astype(out[name].dtype))
    for name, factor in factors.items():
        out[name] = (out[name] * factor).astype(out[name].dtype)
    return out
```

```python
from contextlib import ExitStack

import numpy as np

import concourse.bass as bass
from concourse import mybir

F32 = mybir.dt.float32
PART = mybir.dt.float32r
ALU = mybir.AluOpType
ACT = mybir.ActivationFunctionType
AX_X = mybir.AxisListType.X

P = 128
D = 1024
DT = D // P
SEQ = 256
META = 16
L1 = SEQ + META
LAYERS = 2
EPS = 1e-6
NEG = -1e30

GRID_W, NA_KW, RPB_H, RPB_W = 64, 16, 15, 31
HD = 64
GROUP = 4
KV = 2
NA_HEADS = 8
VCOLS = KV * HD + NA_HEADS * HD
M_HEADS = 4
A_HEADS = 8
ROT = 32
FFT = 2816 // P

TT1 = [(0, 128), (128, 128), (256, META)]
TT2 = TT1[:2]

CH = 8
RAW_SLOTS = 4
PART_SLOTS = 4

CONSTS = {}
_at = 0
for _name, _n in [("ident", 128), ("rot1", 128), ("jrev", 128), ("cos1", L1), ("sin1", L1), ("window", GRID_W),
                  ("causal", 128), ("tri_neg", 512), ("eye2", 512), ("causal_t", 256), ("head_sum", 2), ("ones", 2),
                  ("sel4", 512), ("sel10", 5 * 128), ("cos2", 256), ("sin2", 256), ("rot2", 32)]:
    CONSTS[_name] = (_at, _n)
    _at += _n
NCONST = _at
VECS = {}
_at = 0
for _name, _n in [("norm_g", 16), ("qg", 2), ("kg", 2), ("final_g", 8), ("a_norm", 8), ("a_h_norm", 8), ("kv_norm", 8),
                  ("k_norm", 1), ("b_norm", 8), ("b_q_norm", 1), ("f_norm", 16), ("conv_w", 2 * 3 * 2 * FFT),
                  ("conv_b", 2 * 2 * FFT), ("b_gates", 8), ("w_gates", 64)]:
    VECS[_name] = (_at, _n)
    _at += _n
NVEC = _at


class Signal:

    def __init__(self, sem, known):
        self.sem, self.known, self.marks, self.n = sem, known, {}, 0

    def inc(self, key, by=1):
        assert key not in self.marks, key
        self.n += by
        self.marks[key] = self.n
        return self.sem, by

    def at(self, key):
        assert not self.known or key in self.known, key
        return self.sem, self.known.get(key, 1)


def tile_list():
    tiles, at = [], 0

    def add(name, engine, blocks):
        nonlocal at
        tiles.append((name, engine, at, blocks))
        at += blocks

    def rows(names, blocks):
        nonlocal at
        for name in names:
            tiles.append((name, "dve", at, blocks))
        at += blocks

    for i in range(LAYERS):
        add(("ka", i), "act", DT)
        for m in range(4):
            add(("qa", i, m), "act", DT)
        for m in range(4):
            add(("qb", i, m), "act", DT)
        for m in range(4):
            add(("kb", i, m), "act", DT)
        rows([("va", i, t) for t in range(3)], DT)
        rows([("vb", i, t) for t in range(3)], 4 * DT)
        for n in range(24):
            add(("gate", i, n), "dve" if n % 2 else "act", DT)
        for m in range(DT):
            add(("ya", i, m), "dve", 4)
            add(("yb", i, m), "dve", 4)
        for m in range(DT):
            add(("out", i, m), "dve", DT)
    for m in range(4):
        add(("mq", m), "act", DT)
    for m in range(4):
        add(("mk", m), "act", DT)
    rows([("mv", t, s) for t in range(2) for s in range(2)], 8 * DT)
    for m in range(DT):
        add(("mo", m), "dve", DT)
    for m in range(DT):
        add(("mout", m), "dve", DT)
    for l in range(2):
        for j in range(FFT):
            add(("uv", l, j), "dve", DT)
            add(("ug", l, j), "dve", DT)
        for m in range(DT):
            add(("down", l, m), "dve", FFT)
        if l == 0:
            for m in range(DT):
                add(("kk", m), "act", DT)
            for m in range(DT):
                add(("qq", m), "act", DT)
            rows([("vv", t, s) for t in range(2) for s in range(2)], 8 * DT)
            for m in range(DT):
                add(("aout", m), "dve", DT)
    return tiles, at // CH


def program(nc, x_t, consts_d, vecs_d, rpb, weights, out, known):
    ctx = ExitStack()
    with ctx:
        signals = {}

        def sb(name, shape, dt=F32, stack=ctx):
            return stack.enter_context(nc.sbuf_tensor(name, shape, dt))

        def signal(name):
            signals[name] = Signal(ctx.enter_context(nc.semaphore(name)), known.get(name, {}))
            return signals[name]

        acc = ctx.enter_context(nc.psum_tensor("acc", [P, 4, 512], F32))
        misc = ctx.enter_context(nc.psum_tensor("misc", [P, 4, 512], F32))
        raw = sb("raw", [P, RAW_SLOTS, CH * P])
        w_hi = sb("w_hi", [P, PART_SLOTS, CH * P], PART)
        w_lo = sb("w_lo", [P, PART_SLOTS, CH * P], PART)
        cst = sb("cst", [P, NCONST])
        vec = sb("vec", [P, NVEC])
        h = sb("h", [P, DT, L1])
        xt = sb("xt", [P, DT, L1])
        xs_hi = sb("xs_hi", [P, DT, L1], PART)
        xs_lo = sb("xs_lo", [P, DT, L1], PART)
        ys_hi = sb("ys_hi", [P, DT, L1], PART)
        ys_lo = sb("ys_lo", [P, DT, L1], PART)
        var = sb("var", [P, 32])
        rstd = sb("rstd", [P, 32])
        mhalf = sb("mhalf", [P, 32])
        nmax = sb("nmax", [P, 2])
        rsum = sb("rsum", [P, 2])
        rinv = sb("rinv", [P, 2])
        qscale = sb("qscale", [P, 3])
        gw_hi = sb("gw_hi", [P, 64], PART)
        gw_lo = sb("gw_lo", [P, 64], PART)

        with ExitStack() as first:
            rq = sb("rq", [P, 5, L1], F32, first)
            xg = sb("xg", [P, 5, L1], F32, first)
            qf = sb("qf", [P, 5, L1], F32, first)
            rrow = sb("rrow", [10, L1], F32, first)
            t2 = sb("t2", [P, L1], F32, first)
            qn = sb("qn", [P, 4, L1], F32, first)
            kn = sb("kn", [P, 4, L1], F32, first)
            v_sb = sb("v_sb", [P, 3, VCOLS], F32, first)
            gates = sb("gates", [P, 24, L1], F32, first)
            o_raw = sb("o_raw", [P, 8, L1], F32, first)
            bias = sb("bias", [P, NA_HEADS, 6 * GRID_W], F32, first)
            probs = sb("probs", [P, 2, L1], F32, first)
            pt = sb("pt", [P, 2, 384], F32, first)
            pm = sb("pm", [META, 128], F32, first)
            pmt = sb("pmt", [META, 128], F32, first)
            ms = sb("ms", [META, 16], F32, first)
        with ExitStack() as mixers:
            qk2 = sb("qk2", [P, 16, SEQ], F32, mixers)
            v2 = sb("v2", [P, 2, D], F32, mixers)
            og = sb("og", [P, DT, SEQ], F32, mixers)
            num = sb("num", [P, DT, SEQ], F32, mixers)
            dmat = sb("dmat", [P, M_HEADS, 384], F32, mixers)
            g8 = sb("g8", [P, 2, 8], F32, mixers)
            ab = sb("ab", [P, 2, 4], F32, mixers)
            ln1 = sb("ln1", [P, 2, 4], F32, mixers)
            lf = sb("lf", [P, 2, 4], F32, mixers)
            nf = sb("nf", [P, 2, 4], F32, mixers)
            a_tok = sb("a_tok", [P, 2, 4], F32, mixers)
            floor = sb("floor", [P, 2, 4], F32, mixers)
            den = sb("den", [P, 2, 4], F32, mixers)
            fac = sb("fac", [P, 8], F32, mixers)
            cmax = sb("cmax", [M_HEADS, 2, 128 + SEQ], F32, mixers)
            probs2 = sb("probs2", [P, 2, SEQ], F32, mixers)
            pt2 = sb("pt2", [P, 2, SEQ], F32, mixers)
            rope_t = sb("rope_t", [ROT, 2, 2 * SEQ], F32, mixers)
        with ExitStack() as ffn_mem:
            a_hi = sb("a_hi", [P, FFT, SEQ], PART, ffn_mem)
            a_lo = sb("a_lo", [P, FFT, SEQ], PART, ffn_mem)
            cv = sb("cv", [P, 2, SEQ], F32, ffn_mem)
            cg = sb("cg", [P, 2, SEQ], F32, ffn_mem)

        def const(name, rows=P):
            a, n = CONSTS[name]
            return cst[0:rows, a:a + n]

        def v(name, i=0, n=1):
            a = VECS[name][0] + i
            return vec[:, a:a + n]

        ident = const("ident")

        inputs_loaded = signal("inputs_loaded")
        bias_loaded = signal("bias_loaded")
        raw_landed = [signal(f"raw_landed{i}") for i in range(RAW_SLOTS)]
        hi_ready = signal("hi_ready")
        lo_ready = signal("lo_ready")
        chunk_used = signal("chunk_used")
        tile_done = signal("tile_done")
        act_evac = signal("act_evac")
        dve_evac = signal("dve_evac")
        sq_ready = signal("sq_ready")
        stats_done = signal("stats_done")
        var_ready = signal("var_ready")
        rstd_ready = signal("rstd_ready")
        bcast_done = signal("bcast_done")
        x_ready = signal("x_ready")
        xhi_ready = signal("xhi_ready")
        xlo_ready = signal("xlo_ready")
        scores_done = signal("scores_done")
        max_ready = signal("max_ready")
        exp_ready = signal("exp_ready")
        probs_ready = signal("probs_ready")
        turned = signal("turned")
        turned_copied = signal("turned_copied")
        mixed_done = signal("mixed_done")
        mixed_copied = signal("mixed_copied")
        act_step = signal("act_step")
        dve_step = signal("dve_step")
        pool_step = signal("pool_step")
        pe_step = signal("pe_step")
        stored = signal("stored")

        tiles, n_chunks = tile_list()
        assert n_chunks == weights.shape[0]
        index = {name: n for n, (name, *_) in enumerate(tiles)}
        last_chunk = {name: (b + k - 1) // CH for name, _, b, k in tiles}
        ends_tile = {b + k: name for name, _, b, k in tiles}

        def bank(name):
            return acc[:, index[name] % 4, :]

        def chunk_free(eng, c):
            name = ends_tile.get((c + 1) * CH)
            eng.wait_ge(*(tile_done.at(name) if name else chunk_used.at(c)))

        block = ctx.enter_context(nc.Block())

        @block.sync
        def _(sp):
            sp.dma_start(cst[:], consts_d).then_inc(*inputs_loaded.inc("cst", 16))
            sp.dma_start(vec[:], vecs_d).then_inc(*inputs_loaded.inc("vec", 16))
            sp.dma_start(h[:], x_t).then_inc(*inputs_loaded.inc("h", 16))
            for c in range(n_chunks):
                if c >= RAW_SLOTS:
                    sp.wait_ge(*lo_ready.at(c - RAW_SLOTS))
                sp.dma_start(raw[:, c % RAW_SLOTS, :], weights[c]).then_inc(*raw_landed[c % RAW_SLOTS].inc(c, 16))
            for m in range(DT):
                sp.wait_ge(*dve_evac.at(("down", 1, m)))
                sp.dma_start(out[:, m], h[:, m, 0:SEQ]).then_inc(*stored.inc(m, 16))
            sp.wait_ge(*stored.at(DT - 1))

        units = [("na", hd, a) for hd in range(NA_HEADS) for a in range(2)]
        for g in range(KV):
            units += [("ga", g, c0, min(128, 4 * L1 - c0)) for c0 in range(0, 4 * L1, 128)]
        units2 = [(hd, t) for hd in range(A_HEADS) for t in range(2)]

        def meta_at(hd):
            return 64 * (hd % 2) + META * (hd // 2)

        def qflat(g):
            return qf[HD * g:HD * g + HD, 1:5, :].rearrange("p j t -> p (j t)")

        @block.tensor
        def _(pe):
            seen = set()

            def once(signal_, key):
                if (id(signal_), key) not in seen:
                    seen.add((id(signal_), key))
                    pe.wait_ge(*signal_.at(key))

            def weight(b, n=P):
                c, j = divmod(b, CH)
                once(lo_ready, c)
                s = c % PART_SLOTS
                return w_hi[:, s, j * P:j * P + n], w_lo[:, s, j * P:j * P + n]

            def acc_free(name):
                n = index[name] - 4
                if n >= 0:
                    before, engine, *_ = tiles[n]
                    pe.wait_ge(*(act_evac if engine == "act" else dve_evac).at(before))

            def parts(o, lhs, rhs, first, last):
                pe.matmul(o, lhs[0], rhs[0], start=first, stop=False)
                pe.matmul(o, lhs[0], rhs[1], start=False, stop=False)
                return pe.matmul(o, lhs[1], rhs[0], start=False, stop=last)

            def tile(name, x_hi, x_lo, key, k0=0, cols=SEQ):
                _, _, b0, blocks = tiles[index[name]]
                acc_free(name)
                o = bank(name)[:, 0:cols]
                for i in range(blocks):
                    w = weight(b0 + i)
                    once(xlo_ready, (key, k0 + i))
                    mm = parts(o, w, (x_hi[:, k0 + i, 0:cols], x_lo[:, k0 + i, 0:cols]), i == 0, i == blocks - 1)
                    if i == blocks - 1:
                        mm.then_inc(*tile_done.inc(name))
                    elif (b0 + i) % CH == CH - 1:
                        mm.then_inc(*chunk_used.inc((b0 + i) // CH))

            def row_tiles(names, x_hi, x_lo, key, tts, width, halves=1):
                b0 = tiles[index[names[0]]][2]
                for name in names:
                    acc_free(name)
                bk = width // P * halves
                for c0 in range(0, DT * bk, CH):
                    for n, name in enumerate(names):
                        t, s = divmod(n, halves)
                        tok, tn = tts[t]
                        for k in range(c0 // bk, (c0 + CH) // bk):
                            w = weight(b0 + k * bk + s * (width // P), width)
                            once(xlo_ready, (key, k))
                            x = (x_hi[:, k, tok:tok + tn], x_lo[:, k, tok:tok + tn])
                            o = bank(name)[0:tn, 0:width]
                            mm = parts(o, x, w, k == 0, k == DT - 1)
                        if c0 + CH == DT * bk:
                            mm.then_inc(*tile_done.inc(name))
                    if c0 + CH < DT * bk:
                        mm.then_inc(*chunk_used.inc((b0 + c0) // CH))

            def stats(key, tts):
                for m in range(DT):
                    pe.wait_ge(*sq_ready.at((key, m)))
                    for t, (t0, tn) in enumerate(tts):
                        mm = pe.matmul(misc[0:tn, 3, t:t + 1], xt[:, m, t0:t0 + tn], const("ones")[:, 0:1],
                                       start=(m == 0 and t == 0), stop=(m == DT - 1), skip_group_check=True)
                mm.then_inc(*stats_done.inc(key))

            def spread(key, tts):
                pe.wait_ge(*rstd_ready.at(key))
                for t, (t0, tn) in enumerate(tts):
                    mm = pe.matmul(misc[:, 2, t0:t0 + tn], rstd[0:tn, t:t + 1].to_broadcast([tn, P]),
                                   ident[0:tn, 0:tn], start=True, stop=True)
                mm.then_inc(*bcast_done.inc(key))

            pe.wait_ge(*inputs_loaded.at("h"))
            for i in range(LAYERS):
                key = ("x", i)
                stats(key, TT1)
                spread(key, TT1)

                def proj(name):
                    tile(name, xs_hi, xs_lo, key, cols=L1)

                def rot(j):
                    pe.wait_ge(*dve_step.at(("xg", i)))
                    if j >= 2:
                        pe.wait_ge(*dve_step.at(("t2", i, j - 2)))
                    pe.matmul(misc[:, j % 2, 0:L1], const("rot1"), xg[:, j, :], start=True,
                              stop=True).then_inc(*pe_step.inc(("rot", i, j)))

                def rb(j):
                    pe.wait_ge(*dve_step.at(("rrow", i)))
                    if j >= 2:
                        pe.wait_ge(*dve_step.at(("qf", i, j - 2)))
                    a, _ = CONSTS["sel10"]
                    pe.matmul(misc[:, 2 + j % 2, 0:L1], cst[0:10, a + j * P:a + (j + 1) * P], rrow[:, :], start=True,
                              stop=True).then_inc(*pe_step.inc(("rb", i, j)))

                proj(("ka", i))
                for m in range(4):
                    proj(("qa", i, m))
                proj(("qb", i, 0))
                for j in range(5):
                    pe.wait_ge(*dve_step.at(("qsq", i, j)))
                    for t, (t0, tn) in enumerate(TT1):
                        mm = pe.matmul(misc[0:tn, 3, 10 * t + 2 * j:10 * t + 2 * j + 2], qf[:, j, t0:t0 + tn],
                                       const("head_sum"), start=True, stop=True)
                mm.then_inc(*stats_done.inc(("qk", i)))
                proj(("qb", i, 1))
                rot(0)
                rot(1)
                for m in (2, 3):
                    proj(("qb", i, m))
                proj(("kb", i, 0))
                pe.wait_ge(*rstd_ready.at(("qk", i)))
                for t, (t0, tn) in enumerate(TT1):
                    mm = pe.matmul(misc[0:10, 3, t0:t0 + tn], rstd[0:tn, 10 * t:10 * t + 10], ident[0:tn, 0:tn],
                                   start=True, stop=True)
                mm.then_inc(*pe_step.inc(("rt", i)))
                proj(("kb", i, 1))
                rb(0)
                rb(1)
                proj(("kb", i, 2))
                for j in range(2, 5):
                    rot(j)
                    rb(j)
                proj(("kb", i, 3))
                pe.wait_ge(*act_evac.at(("kb", i, 3)))
                pe.wait_ge(*dve_step.at(("t2", i, 4)))
                for hd in range(NA_HEADS):
                    a = HD * (hd % 2)
                    mm = pe.matmul(misc[0:META, hd % 2, META * (hd // 2):META * (hd // 2) + META], qn[a:a + HD, hd // 2, SEQ:L1],
                                   kn[a:a + HD, hd // 2, SEQ:L1], start=True, stop=True)
                mm.then_inc(*pe_step.inc(("meta_s", i)))
                row_tiles([("va", i, t) for t in range(3)], xs_hi, xs_lo, key, TT1, P)
                row_tiles([("vb", i, t) for t in range(3)], xs_hi, xs_lo, key, TT1, 512)
                pe.wait_ge(*dve_step.at(("meta_p", i)))
                pe.wait_ge(*dve_step.at(("qf", i, 4)))
                for hd in range(NA_HEADS):
                    mm = pe.matmul(misc[0:META, 2, META * hd:META * hd + META], pm[:, meta_at(hd):meta_at(hd) + META],
                                   ident[0:META, 0:META], start=True, stop=True)
                mm.then_inc(*pe_step.inc(("meta_t", i)))

                def scores(u):
                    n = len(units) * i + u
                    if u >= 2:
                        pe.wait_ge(*exp_ready.at(n - 2))
                    o = misc[:, u % 2, 0:L1]
                    if units[u][0] == "na":
                        _, hd, a = units[u]
                        p0 = HD * (hd % 2)
                        if u == 0:
                            pe.wait_ge(*pool_step.at(("bias", i)))
                        pe.matmul(o, qn[p0:p0 + HD, hd // 2, a * P:(a + 1) * P], kn[p0:p0 + HD, hd // 2, :],
                                  start=True, stop=False)
                        b0 = 2 * (1 - a) * GRID_W
                        mm = pe.matmul(o[:, 0:SEQ], const("jrev"), bias[:, hd, b0:b0 + 4 * GRID_W], start=False,
                                       stop=True)
                    else:
                        _, g, c0, cn = units[u]
                        mm = pe.matmul(o[0:cn], qflat(g)[:, c0:c0 + cn], qf[HD * g:HD * g + HD, 0, :], start=True,
                                       stop=True)
                    mm.then_inc(*scores_done.inc(n))

                def turn(u):
                    n = len(units) * i + u
                    pe.wait_ge(*probs_ready.at(n))
                    if u >= 1:
                        pe.wait_ge(*turned_copied.at(n - 1))
                    q = P if units[u][0] == "na" else units[u][3]
                    for t, (t0, tn) in enumerate(TT1):
                        mm = pe.matmul(misc[0:tn, 2, t * P:t * P + q], probs[0:q, u % 2, t0:t0 + tn], ident[0:q, 0:q],
                                       start=True, stop=True)
                    mm.then_inc(*turned.inc(n))

                def mix(u):
                    n = len(units) * i + u
                    pe.wait_ge(*turned_copied.at(n))
                    if u >= 1:
                        pe.wait_ge(*mixed_copied.at(n - 1))
                    if units[u][0] == "na":
                        _, hd, _ = units[u]
                        q, half, v0 = P, hd % 2, KV * HD + hd * HD
                    else:
                        _, half, _, q = units[u]
                        v0 = half * HD
                    for t, (t0, tn) in enumerate(TT1):
                        mm = pe.matmul(misc[HD * half:HD * half + HD, 3, (u % 2) * P:(u % 2) * P + q],
                                       v_sb[0:tn, t, v0:v0 + HD], pt[0:tn, u % 2, t * P:t * P + q],
                                       start=(t == 0), stop=(t == 2))
                    mm.then_inc(*mixed_done.inc(n))

                scores(0)
                proj(("gate", i, 0))
                pe.wait_ge(*dve_step.at(("meta_pt", i)))
                for hd in range(NA_HEADS):
                    a = HD * (hd % 2)
                    c0 = KV * HD + hd * HD
                    mm = pe.matmul(misc[a:a + HD, 3, META * (hd // 2):META * (hd // 2) + META],
                                   v_sb[0:META, 2, c0:c0 + HD], pmt[:, META * hd:META * hd + META], start=True, stop=True)
                mm.then_inc(*pe_step.inc(("meta_o", i)))
                pe.wait_ge(*act_step.at(("meta_o", i)))
                for u in range(1, len(units) + 2):
                    if u < len(units):
                        scores(u)
                    if u < 24:
                        proj(("gate", i, u))
                    if u - 1 < len(units):
                        turn(u - 1)
                    if u >= 2:
                        mix(u - 2)
                for m in range(DT):
                    tile(("ya", i, m), ys_hi, ys_lo, ("o", i), 0, L1)
                    tile(("yb", i, m), ys_hi, ys_lo, ("o", i), 4, L1)
                for m in range(DT):
                    tile(("out", i, m), xs_hi, xs_lo, ("mix", i), 0, L1)
            stats("final", TT1[:2])
            spread("final", TT1[:2])

            stats("a", TT2)
            spread("a", TT2)
            for k in range(DT):
                once(xlo_ready, ("a", k))
            pe.wait_ge(*dve_step.at("gw_lo"))
            for t, (t0, tn) in enumerate(TT2):
                for k in range(DT):
                    mm = parts(misc[:, 0, 8 * t:8 * t + 8], (xs_hi[:, k, t0:t0 + tn], xs_lo[:, k, t0:t0 + tn]),
                               (gw_hi[:, 8 * k:8 * k + 8], gw_lo[:, 8 * k:8 * k + 8]), k == 0, k == DT - 1)
            mm.then_inc(*pe_step.inc("gates"))
            tri, eye2 = const("tri_neg"), const("eye2")
            for m in range(4):
                tile(("mq", m), xs_hi, xs_lo, "a")
            pe.wait_ge(*dve_step.at("lf"))
            pe.matmul(misc[:, 1, 16:20], tri[:, 0:P], lf[:, 0, :], start=True, stop=True)
            pe.matmul(misc[:, 1, 20:24], tri[:, P:2 * P], lf[:, 0, :], start=True, stop=False)
            pe.matmul(misc[:, 1, 20:24], tri[:, 3 * P:4 * P], lf[:, 1, :], start=False, stop=True)
            for t in range(2):
                pe.matmul(misc[0:M_HEADS, 0, 0:SEQ], lf[:, t, :], tri[:, t * SEQ:(t + 1) * SEQ], start=(t == 0), stop=False)
            for t in range(2):
                mm = pe.matmul(misc[0:M_HEADS, 0, 0:SEQ], g8[:, t, 0:4], eye2[:, t * SEQ:(t + 1) * SEQ], start=False,
                               stop=(t == 1))
            mm.then_inc(*pe_step.inc("a_row"))
            for m in range(4):
                tile(("mk", m), xs_hi, xs_lo, "a")
            pe.wait_ge(*dve_step.at("cmax"))
            top = cmax[:, 0, P:P + SEQ]
            for t in range(2):
                mm = pe.matmul(misc[:, 1, 24 + 4 * t:28 + 4 * t], cmax[:, 0, P + t * P:P + (t + 1) * P],
                               ident[0:M_HEADS, 0:M_HEADS], start=True, stop=True)
            mm.then_inc(*pe_step.inc("m_tok"))
            row_tiles([("mv", t, s) for t in range(2) for s in range(2)], xs_hi, xs_lo, "a", TT2, 512, 2)
            a4, _ = CONSTS["sel4"]
            pe.wait_ge(*act_evac.at(("mk", 3)))
            for s in range(2 * M_HEADS):
                hd = s // 2
                tile(("mo", s), xs_hi, xs_lo, "a")
                if s % 2 == 0:
                    if hd:
                        pe.wait_ge(*dve_step.at(("d1", hd - 1)))
                    pe.matmul(misc[:, 2, 0:SEQ], cst[0:M_HEADS, a4 + hd * P:a4 + (hd + 1) * P], top, start=True,
                              stop=True).then_inc(*pe_step.inc(("mb", hd)))
                    if hd:
                        pe.wait_ge(*dve_step.at(("sd", hd - 1)))
                    pe.matmul(misc[:, 0, 0:SEQ], qk2[:, 4 + hd, 0:P], qk2[:, hd, :], start=True, stop=True)
                    pe.matmul(misc[:, 0, SEQ:384], qk2[:, 4 + hd, P:SEQ], qk2[:, hd, P:SEQ], start=True,
                              stop=True).then_inc(*pe_step.inc(("mst", hd)))
                else:
                    pe.wait_ge(*dve_step.at(("sd", hd)))
                    if hd:
                        pe.wait_ge(*act_step.at(("num", hd - 1)))
                    for j in range(2):
                        c0 = hd * SEQ + j * P
                        pe.matmul(misc[:, 3, j * SEQ:(j + 1) * SEQ], v2[:, 0, c0:c0 + P], dmat[:, hd, 0:SEQ],
                                  start=True, stop=False)
                        mm = pe.matmul(misc[:, 3, j * SEQ + P:(j + 1) * SEQ], v2[:, 1, c0:c0 + P],
                                       dmat[:, hd, SEQ:384], start=False, stop=True)
                    mm.then_inc(*pe_step.inc(("num", hd)))
                    one = const("ones")[:, 0:1]
                    pe.matmul(misc[:, 1, hd:hd + 1], dmat[:, hd, 0:P], one, start=True, stop=True)
                    pe.matmul(misc[:, 1, 4 + hd:5 + hd], dmat[:, hd, P:SEQ], one, start=True, stop=False)
                    pe.matmul(misc[:, 1, 4 + hd:5 + hd], dmat[:, hd, SEQ:384], one, start=False, stop=True)
            for hd in range(M_HEADS):
                pe.wait_ge(*dve_step.at(("nsq", hd)))
                for t in range(2):
                    for j in range(2):
                        mm = pe.matmul(misc[:, 1, 8 + 4 * t + hd:9 + 4 * t + hd], xt[:, 2 * hd + j, t * P:(t + 1) * P],
                                       one, start=(j == 0), stop=(j == 1))
            mm.then_inc(*pe_step.inc("nss"))
            pe.wait_ge(*dve_step.at("fac"))
            for hd in range(M_HEADS):
                if hd >= 2:
                    pe.wait_ge(*dve_step.at(("hn", 2 * hd - 3)))
                b = (2, 0)[hd % 2]
                for t in range(2):
                    mm = pe.matmul(misc[:, b, t * P:(t + 1) * P], fac[:, 4 * t + hd:4 * t + hd + 1].to_broadcast([P, P]),
                                   ident, start=True, stop=True)
                mm.then_inc(*pe_step.inc(("fb", hd)))
            for m in range(DT):
                tile(("mout", m), ys_hi, ys_lo, "mlstm")

            def ffn(l):
                stats(("f", l), TT2)
                spread(("f", l), TT2)
                for j in range(FFT):
                    tile(("uv", l, j), xs_hi, xs_lo, ("f", l))
                    tile(("ug", l, j), xs_hi, xs_lo, ("f", l))
                for m in range(DT):
                    tile(("down", l, m), a_hi, a_lo, ("act", l))

            ffn(0)

            stats("kv", TT2)
            spread("kv", TT2)
            r2 = cst[0:ROT, CONSTS["rot2"][0]:CONSTS["rot2"][0] + ROT]

            def head_stats(m):
                pe.wait_ge(*dve_step.at(("sq2", m)))
                for t in range(2):
                    mm = pe.matmul(misc[:, 3, 16 * t + m:16 * t + m + 1], xt[:, m % 8, t * P:(t + 1) * P], one,
                                   start=True, stop=True)
                mm.then_inc(*pe_step.inc(("st2", m)))

            def head_rot(j):
                if j >= 1:
                    pe.wait_ge(*dve_step.at(("rope2", j - 1)))
                for s in range(2):
                    pe.matmul(misc[0:ROT, 0, s * SEQ:(s + 1) * SEQ], r2, qk2[0:ROT, 2 * j + s, :], start=True, stop=True)
                for s in range(2):
                    for t in range(2):
                        c = 16 * t + 2 * j + s
                        mm = pe.matmul(misc[:, 1, s * SEQ + t * P:s * SEQ + (t + 1) * P],
                                       rstd[:, c:c + 1].to_broadcast([P, P]), ident, start=True, stop=True)
                mm.then_inc(*pe_step.inc(("rot2", j)))

            for m in range(DT):
                tile(("kk", m), xs_hi, xs_lo, "kv")
                if m >= 1:
                    head_stats(m - 1)
            for m in range(DT):
                tile(("qq", m), ys_hi, ys_lo, "b")
                head_stats(m + 7)
            head_stats(15)
            row_tiles([("vv", t, s) for t in range(2) for s in range(2)], xs_hi, xs_lo, "kv", TT2, 512, 2)
            pe.wait_ge(*rstd_ready.at("qk2"))
            pe.wait_ge(*dve_step.at("xg2"))
            for j in range(8):
                head_rot(j)

            def scores2(u):
                hd, t = units2[u]
                n = 2 * len(units) + u
                if u >= 2:
                    pe.wait_ge(*exp_ready.at(n - 2))
                keys = (t + 1) * P
                o = misc[:, u % 2, 0:keys]
                pe.matmul(o, qk2[:, 8 + hd, t * P:(t + 1) * P], qk2[:, hd, 0:keys], start=True, stop=False)
                pe.matmul(o[:, t * P:keys], ident, const("causal"), start=False,
                          stop=True).then_inc(*scores_done.inc(n))

            def turn2(u):
                n = 2 * len(units) + u
                pe.wait_ge(*probs_ready.at(n))
                if u >= 1:
                    pe.wait_ge(*turned_copied.at(n - 1))
                for k in range(units2[u][1] + 1):
                    mm = pe.matmul(misc[:, 2, k * P:(k + 1) * P], probs2[:, u % 2, k * P:(k + 1) * P], ident,
                                   start=True, stop=True)
                mm.then_inc(*turned.inc(n))

            def mix2(u):
                hd, t = units2[u]
                n = 2 * len(units) + u
                pe.wait_ge(*turned_copied.at(n))
                if u >= 1:
                    pe.wait_ge(*mixed_copied.at(n - 1))
                for k in range(t + 1):
                    mm = pe.matmul(misc[:, 3, (u % 2) * P:(u % 2 + 1) * P], v2[:, k, hd * P:(hd + 1) * P],
                                   pt2[:, u % 2, k * P:(k + 1) * P], start=(k == 0), stop=(k == t))
                mm.then_inc(*mixed_done.inc(n))

            pe.wait_ge(*dve_step.at(("rope2", 7)))
            for u in range(len(units2) + 2):
                if u < len(units2):
                    scores2(u)
                if 1 <= u <= len(units2):
                    turn2(u - 1)
                if u >= 2:
                    mix2(u - 2)
            for m in range(DT):
                tile(("aout", m), ys_hi, ys_lo, "attn")
            ffn(1)

        @block.scalar
        def _(act):
            at = {"next": 0}

            def split(upto):
                for c in range(at["next"], min(upto + 1, n_chunks)):
                    act.wait_ge(*raw_landed[c % RAW_SLOTS].at(c))
                    if c >= PART_SLOTS:
                        chunk_free(act, c - PART_SLOTS)
                    nc.scalar.activation(w_hi[:, c % PART_SLOTS, :], raw[:, c % RAW_SLOTS, :],
                                         ACT.Copy).then_inc(*hi_ready.inc(c))
                    at["next"] = c + 1

            def done(name):
                split(last_chunk[name] + PART_SLOTS - 1)
                act.wait_ge(*tile_done.at(name))

            def squares(key, before, after, cols):
                for m in range(DT):
                    act.wait_ge(*after(m))
                    if before is not None:
                        act.wait_ge(*xlo_ready.at((before, m)))
                    nc.scalar.activation(xt[:, m, 0:cols], h[:, m, 0:cols], ACT.Square).then_inc(*sq_ready.inc((key, m)))

            def upper(key, dst, cols):
                for m in range(DT):
                    act.wait_ge(*x_ready.at((key, m)))
                    nc.scalar.activation(dst[:, m, 0:cols], xt[:, m, 0:cols], ACT.Copy).then_inc(*xhi_ready.inc((key, m)))

            act.wait_ge(*inputs_loaded.at("h"))
            a, n = VECS["w_gates"]
            nc.scalar.activation(gw_hi[:, :], vec[:, a:a + n], ACT.Copy).then_inc(*act_step.inc("gw_hi"))
            for i in range(LAYERS):
                if i == 0:
                    squares(("x", 0), None, lambda m: inputs_loaded.at("h"), L1)
                    split(PART_SLOTS - 1)
                upper(("x", i), xs_hi, L1)
                for j, name in enumerate([("ka", i)] + [("qa", i, m) for m in range(4)]):
                    done(name)
                    nc.scalar.activation(rq[:, j, :], bank(name)[:, 0:L1], ACT.Copy).then_inc(*act_evac.inc(name))
                for kind, dst, scale in (("qb", qn, HD ** -0.5), ("kb", kn, 1.0)):
                    for m in range(4):
                        done((kind, i, m))
                        nc.scalar.activation(dst[:, m, :], bank((kind, i, m))[:, 0:L1], ACT.Copy,
                                             scale=scale).then_inc(*act_evac.inc((kind, i, m)))
                act.wait_ge(*dve_step.at(("meta_x", i)))
                nc.scalar.activation(pm[:, :], pm[:, :], ACT.Exp).then_inc(*act_step.inc(("meta_e", i)))

                def exp(u):
                    n = len(units) * i + u
                    q = P if units[u][0] == "na" else units[u][3]
                    act.wait_ge(*max_ready.at(n))
                    if u >= 2:
                        act.wait_ge(*turned.at(n - 2))
                    nc.scalar.activation(probs[0:q, u % 2, :], misc[0:q, u % 2, 0:L1], ACT.Exp, bias=nmax[0:q, u % 2:u % 2 + 1],
                                         accum_out=rsum[0:q, u % 2:u % 2 + 1]).then_inc(*exp_ready.inc(n))

                def turn(u):
                    n = len(units) * i + u
                    q = P if units[u][0] == "na" else units[u][3]
                    act.wait_ge(*turned.at(n))
                    if u >= 2:
                        act.wait_ge(*mixed_done.at(n - 2))
                    pv = pt[:, u % 2, 0:SEQ].rearrange("p (t q) -> p t q", t=2)[:, :, 0:q]
                    nc.scalar.activation(pv, misc[:, 2, 0:SEQ].rearrange("p (t q) -> p t q", t=2)[:, :, 0:q], ACT.Copy)
                    nc.scalar.activation(pt[0:META, u % 2, SEQ:SEQ + q], misc[0:META, 2, SEQ:SEQ + q],
                                         ACT.Copy).then_inc(*turned_copied.inc(n))

                def mixed(u):
                    n = len(units) * i + u
                    act.wait_ge(*mixed_done.at(n))
                    if units[u][0] == "na":
                        _, hd, a = units[u]
                        half, q = hd % 2, P
                        dst = o_raw[HD * half:HD * half + HD, 4 + hd // 2, a * P:(a + 1) * P]
                    else:
                        _, half, c0, q = units[u]
                        dst = o_raw[HD * half:HD * half + HD, 0:4, :].rearrange("p j t -> p (j t)")[:, c0:c0 + q]
                    nc.scalar.activation(dst, misc[HD * half:HD * half + HD, 3, (u % 2) * P:(u % 2) * P + q],
                                         ACT.Copy).then_inc(*mixed_copied.inc(n))

                split(last_chunk[("vb", i, 2)] + PART_SLOTS - 1)
                for u in range(len(units) + 2):
                    if u < len(units):
                        exp(u)
                    if u < 24:
                        split(last_chunk[("gate", i, u)] + PART_SLOTS - 1)
                        if u % 2 == 0:
                            done(("gate", i, u))
                            nc.scalar.activation(gates[:, u, :], bank(("gate", i, u))[:, 0:L1],
                                                 ACT.Copy).then_inc(*act_evac.inc(("gate", i, u)))
                    if u == 0:
                        act.wait_ge(*pe_step.at(("meta_o", i)))
                        nc.scalar.activation(o_raw[:, 4:8, SEQ:L1], misc[:, 3, 0:4 * META].rearrange("p (j t) -> p j t", j=4),
                                             ACT.Copy).then_inc(*act_step.inc(("meta_o", i)))
                    if 1 <= u <= len(units):
                        turn(u - 1)
                    if u >= 2:
                        mixed(u - 2)
                act.wait_ge(*dve_evac.at(("gate", i, 23)))
                act.wait_ge(*act_evac.at(("gate", i, 22)))
                for m in range(8):
                    nc.scalar.activation(gates[:, m, :], gates[:, m, :], ACT.Silu).then_inc(*act_step.inc(("silu", i, m)))
                upper(("o", i), ys_hi, L1)
                for m in range(8, 24, 4):
                    nc.scalar.activation(gates[:, m:m + 4, :], gates[:, m:m + 4, :],
                                         ACT.Sigmoid).then_inc(*act_step.inc(("sigm", i, m)))
                for m in range(DT):
                    split(last_chunk[("yb", i, m)] + PART_SLOTS - 1)
                    act.wait_ge(*x_ready.at((("mix", i), m)))
                    nc.scalar.activation(xs_hi[:, m, :], xt[:, m, :], ACT.Copy).then_inc(*xhi_ready.inc((("mix", i), m)))
                last = i == LAYERS - 1
                for m in range(DT):
                    split(last_chunk[("out", i, m)] + PART_SLOTS - 1)
                    act.wait_ge(*dve_evac.at(("out", i, m)))
                    act.wait_ge(*xlo_ready.at((("mix", i), m)))
                    nc.scalar.activation(xt[:, m, :], h[:, m, :],
                                         ACT.Square).then_inc(*sq_ready.inc(("final" if last else ("x", i + 1), m)))
            for m in range(DT):
                act.wait_ge(*x_ready.at(("final", m)))
                nc.scalar.activation(xt[:, m, 0:SEQ], h[:, m, 0:SEQ], ACT.Square).then_inc(*sq_ready.inc(("a", m)))
            upper("a", xs_hi, SEQ)
            for m in range(4):
                done(("mq", m))
                nc.scalar.activation(qk2[:, m, :], bank(("mq", m))[:, 0:SEQ], ACT.Copy,
                                     scale=P ** -0.5).then_inc(*act_evac.inc(("mq", m)))
                if m == 0:
                    act.wait_ge(*dve_step.at("ab"))
                    nc.scalar.activation(ln1[:], ab[:], ACT.Exp, scale=-1.0).then_inc(*act_step.inc("e1"))
                    act.wait_ge(*act_step.at("e1"))
                    nc.scalar.activation(ln1[:], ln1[:], ACT.Ln, bias=1.0).then_inc(*act_step.inc("ln1"))
            for m in range(4):
                done(("mk", m))
                nc.scalar.activation(qk2[:, 4 + m, :], bank(("mk", m))[:, 0:SEQ], ACT.Copy).then_inc(*act_evac.inc(("mk", m)))
            split(last_chunk[("mv", 0, 0)] - CH + PART_SLOTS)
            act.wait_ge(*dve_step.at("fm"))
            nc.scalar.activation(floor[:], floor[:], ACT.Exp).then_inc(*act_step.inc("floor"))
            split(last_chunk[("mv", 1, 1)] + PART_SLOTS - 1)
            for s in range(2 * M_HEADS):
                hd = s // 2
                split(last_chunk[("mo", s)] + PART_SLOTS - 1)
                if s % 2 == 0:
                    act.wait_ge(*dve_step.at(("d1", hd)))
                    nc.scalar.activation(dmat[:, hd, 0:SEQ], dmat[:, hd, 0:SEQ], ACT.Exp, bias=a_tok[:, 0, hd:hd + 1])
                    nc.scalar.activation(dmat[:, hd, SEQ:384], dmat[:, hd, SEQ:384], ACT.Exp,
                                         bias=a_tok[:, 1, hd:hd + 1]).then_inc(*act_step.inc(("dexp", hd)))
                else:
                    act.wait_ge(*pe_step.at(("num", hd)))
                    nc.scalar.activation(num[:, 2 * hd:2 * hd + 2, :], misc[:, 3, :].rearrange("p (j t) -> p j t", j=2),
                                         ACT.Copy).then_inc(*act_step.inc(("num", hd)))
            for m in range(DT):
                act.wait_ge(*dve_evac.at(("mo", m)))
                nc.scalar.activation(og[:, m, :], og[:, m, :], ACT.Sigmoid).then_inc(*act_step.inc(("so", m)))
            upper("mlstm", ys_hi, SEQ)

            def residual(kind, before, key):
                for m in range(DT):
                    split(last_chunk[kind + (m,)] + PART_SLOTS - 1)
                    act.wait_ge(*dve_evac.at(kind + (m,)))
                    if before is not None:
                        act.wait_ge(*xlo_ready.at((before, m)))
                    nc.scalar.activation(xt[:, m, 0:SEQ], h[:, m, 0:SEQ], ACT.Square).then_inc(*sq_ready.inc((key, m)))

            def ffn(l):
                upper(("f", l), xs_hi, SEQ)
                for j in range(FFT + 1):
                    if j < FFT:
                        for c, (kind, dst) in enumerate((("uv", cv), ("ug", cg))):
                            done((kind, l, j))
                            if j >= 2:
                                act.wait_ge(*xlo_ready.at((("act", l), j - 2)))
                            w = v("conv_w", ((l * 3 + 2) * 2 + c) * FFT + j)
                            b = v("conv_b", (l * 2 + c) * FFT + j)
                            nc.scalar.activation(dst[:, j % 2, :], bank((kind, l, j))[:, 0:SEQ], ACT.Identity, bias=b,
                                                 scale=w).then_inc(*act_step.inc((kind, l, j)))
                    if j >= 1:
                        k = j - 1
                        act.wait_ge(*dve_evac.at(("ug", l, k)))
                        nc.scalar.activation(cg[:, k % 2, :], cg[:, k % 2, :], ACT.Silu).then_inc(*act_step.inc(("sg", l, k)))
                        act.wait_ge(*pool_step.at(("prod", l, k)))
                        nc.scalar.activation(a_hi[:, k, :], cv[:, k % 2, :], ACT.Copy).then_inc(*xhi_ready.inc((("act", l), k)))
                if l == 0:
                    residual(("down", 0), ("f", 0), "kv")
                else:
                    for m in range(DT):
                        split(last_chunk[("down", 1, m)] + PART_SLOTS - 1)

            residual(("mout",), "mlstm", ("f", 0))
            ffn(0)
            upper("kv", xs_hi, SEQ)
            upper("b", ys_hi, SEQ)
            for kind, base in (("kk", 0), ("qq", 8)):
                for m in range(DT):
                    done((kind, m))
                    nc.scalar.activation(qk2[:, base + m, :], bank((kind, m))[:, 0:SEQ],
                                         ACT.Copy).then_inc(*act_evac.inc((kind, m)))
            split(last_chunk[("vv", 1, 1)] + PART_SLOTS - 1)
            for u in range(len(units2) + 2):
                n = 2 * len(units) + u
                if u < len(units2):
                    keys = (units2[u][1] + 1) * P
                    act.wait_ge(*max_ready.at(n))
                    if u >= 2:
                        act.wait_ge(*turned.at(n - 2))
                    nc.scalar.activation(probs2[:, u % 2, 0:keys], misc[:, u % 2, 0:keys], ACT.Exp,
                                         bias=nmax[:, u % 2:u % 2 + 1],
                                         accum_out=rsum[:, u % 2:u % 2 + 1]).then_inc(*exp_ready.inc(n))
                if 1 <= u <= len(units2):
                    keys = (units2[u - 1][1] + 1) * P
                    act.wait_ge(*turned.at(n - 1))
                    if u >= 3:
                        act.wait_ge(*mixed_done.at(n - 3))
                    nc.scalar.activation(pt2[:, (u - 1) % 2, 0:keys], misc[:, 2, 0:keys],
                                         ACT.Copy).then_inc(*turned_copied.inc(n - 1))
                if u >= 2:
                    hd, t = units2[u - 2]
                    act.wait_ge(*mixed_done.at(n - 2))
                    nc.scalar.activation(xt[:, hd, t * P:(t + 1) * P], misc[:, 3, (u % 2) * P:(u % 2 + 1) * P],
                                         ACT.Copy).then_inc(*mixed_copied.inc(n - 2))
                    if t == 1:
                        act.wait_ge(*mixed_copied.at(n - 2))
                        nc.scalar.activation(ys_hi[:, hd, 0:SEQ], xt[:, hd, 0:SEQ],
                                             ACT.Copy).then_inc(*xhi_ready.inc(("attn", hd)))
            residual(("aout",), "attn", ("f", 1))
            ffn(1)

        @block.vector
        def _(dve):
            at = {"next": 0}

            def split(upto):
                for c in range(at["next"], min(upto + 1, n_chunks)):
                    dve.wait_ge(*hi_ready.at(c))
                    nc.vector.tensor_tensor(w_lo[:, c % PART_SLOTS, :], raw[:, c % RAW_SLOTS, :],
                                            w_hi[:, c % PART_SLOTS, :].bitcast(F32),
                                            ALU.subtract).then_inc(*lo_ready.inc(c))
                    at["next"] = c + 1

            def done(name):
                split(last_chunk[name] + PART_SLOTS - 1)
                dve.wait_ge(*tile_done.at(name))

            def step(ins, key):
                ins.then_inc(*dve_step.inc(key))
                dve.wait_ge(*dve_step.at(key))

            def variance(key, tts, n=D):
                dve.wait_ge(*stats_done.at(key))
                if len(tts) == 3:
                    step(nc.vector.tensor_scalar(var[0:META, 2:3], misc[0:META, 3, 2:3], 1.0 / n, EPS, ALU.mult, ALU.add),
                         ("var", key))
                nc.vector.tensor_scalar(var[:, 0:2], misc[:, 3, 0:2], 1.0 / n, EPS, ALU.mult,
                                        ALU.add).then_inc(*var_ready.inc(key))

            def normalise(key, gain, cols, again=None, bkey=None, dst=xt):
                dve.wait_ge(*bcast_done.at(bkey or key))
                for m in range(DT):
                    if again is not None:
                        dve.wait_ge(*xlo_ready.at((again, m)))
                    nc.vector.scalar_tensor_tensor(dst[:, m, 0:cols], h[:, m, 0:cols], gain(m), misc[:, 2, 0:cols],
                                                   ALU.mult, ALU.mult).then_inc(*x_ready.inc((key, m)))

            nc.vector.memset(mhalf[:], -0.5).then_inc(*dve_step.inc("mhalf"))
            dve.wait_ge(*inputs_loaded.at("h"))
            for i in range(LAYERS):
                nc.vector.tensor_scalar(qscale[:, i:i + 1], v("qg", i), HD ** -0.5, None,
                                        ALU.mult).then_inc(*dve_step.inc(("qscale", i)))
            nc.vector.tensor_scalar(qscale[:, 2:3], v("b_q_norm"), P ** -0.5, None, ALU.mult).then_inc(*dve_step.inc("qscale2"))
            dve.wait_ge(*act_step.at("gw_hi"))
            a, n = VECS["w_gates"]
            nc.vector.tensor_tensor(gw_lo[:, :], vec[:, a:a + n], gw_hi[:, :].bitcast(F32),
                                    ALU.subtract).then_inc(*dve_step.inc("gw_lo"))
            for i in range(LAYERS):
                key = ("x", i)
                variance(key, TT1)
                if i == 0:
                    split(PART_SLOTS - 1)
                normalise(key, lambda m: v("norm_g", 8 * i + m), L1)
                for j, name in enumerate([("ka", i)] + [("qa", i, m) for m in range(4)]):
                    split(last_chunk[name] + PART_SLOTS - 1)
                    dve.wait_ge(*act_evac.at(name))
                    nc.vector.tensor_tensor(qf[:, j, :], rq[:, j, :], rq[:, j, :], ALU.mult).then_inc(*dve_step.inc(("qsq", i, j)))
                nc.vector.tensor_scalar(xg[:, 0, :], rq[:, 0, :], v("kg", i), None, ALU.mult)
                nc.vector.tensor_scalar(xg[:, 1:5, :], rq[:, 1:5, :], qscale[:, i:i + 1], None,
                                        ALU.mult).then_inc(*dve_step.inc(("xg", i)))
                split(last_chunk[("qb", i, 0)] + PART_SLOTS - 1)
                dve.wait_ge(*stats_done.at(("qk", i)))
                step(nc.vector.tensor_scalar(var[0:META, 20:30], misc[0:META, 3, 20:30], 1.0 / HD, EPS, ALU.mult, ALU.add),
                     ("var", "qk", i))
                nc.vector.tensor_scalar(var[:, 0:20], misc[:, 3, 0:20], 1.0 / HD, EPS, ALU.mult,
                                        ALU.add).then_inc(*var_ready.inc(("qk", i)))
                split(last_chunk[("kb", i, 0)] + PART_SLOTS - 1)
                dve.wait_ge(*pe_step.at(("rt", i)))
                nc.vector.tensor_copy(rrow[:, :], misc[0:10, 3, 0:L1]).then_inc(*dve_step.inc(("rrow", i)))
                for j in range(5):
                    split(last_chunk[("kb", i, 1 if j < 2 else 2)] + PART_SLOTS - 1)
                    dve.wait_ge(*pe_step.at(("rot", i, j)))
                    step(nc.vector.tensor_tensor(t2[:, :], misc[:, j % 2, 0:L1], const("sin1"), ALU.mult), ("t2", i, j))
                    dve.wait_ge(*pool_step.at(("t1", i, j)))
                    step(nc.vector.tensor_tensor(t2[:, :], rq[:, j, :], t2[:, :], ALU.add), ("t3", i, j))
                    dve.wait_ge(*pe_step.at(("rb", i, j)))
                    step(nc.vector.tensor_tensor(qf[:, j, :], t2[:, :], misc[:, 2 + j % 2, 0:L1], ALU.mult), ("qf", i, j))
                split(last_chunk[("kb", i, 3)] + PART_SLOTS - 1)
                dve.wait_ge(*pe_step.at(("meta_s", i)))
                s3 = misc[0:META, 0:2, 0:64].rearrange("p b (h k) -> p b h k", h=4)
                p3 = pm[:, :].rearrange("p (b h k) -> p b h k", b=2, h=4)
                m3, z3 = (ms[:, c:c + 8].rearrange("p (b h) -> p b h", b=2) for c in (0, 8))
                step(nc.vector.tensor_reduce(m3, s3, AX_X, ALU.max), ("meta_m", i))
                nc.vector.tensor_tensor(p3, s3, m3.unsqueeze(3).to_broadcast([META, 2, 4, META]),
                                        ALU.subtract).then_inc(*dve_step.inc(("meta_x", i)))
                for t in range(3):
                    done(("va", i, t))
                    tn = TT1[t][1]
                    nc.vector.tensor_copy(v_sb[0:tn, t, 0:P], bank(("va", i, t))[0:tn, 0:P]).then_inc(*dve_evac.inc(("va", i, t)))
                dve.wait_ge(*act_step.at(("meta_e", i)))
                step(nc.vector.tensor_reduce(z3, p3, AX_X, ALU.add), ("meta_z", i))
                step(nc.vector.reciprocal(ms[:, 0:8], ms[:, 8:16]), ("meta_r", i))
                nc.vector.tensor_tensor(p3, p3, m3.unsqueeze(3).to_broadcast([META, 2, 4, META]),
                                        ALU.mult).then_inc(*dve_step.inc(("meta_p", i)))
                for t in range(3):
                    done(("vb", i, t))
                    tn = TT1[t][1]
                    nc.vector.tensor_copy(v_sb[0:tn, t, P:VCOLS], bank(("vb", i, t))[0:tn, :]).then_inc(*dve_evac.inc(("vb", i, t)))
                dve.wait_ge(*pe_step.at(("meta_t", i)))
                nc.vector.tensor_copy(pmt[:, :], misc[0:META, 2, 0:128]).then_inc(*dve_step.inc(("meta_pt", i)))
                for u in range(len(units)):
                    n = len(units) * i + u
                    q = P if units[u][0] == "na" else units[u][3]
                    b = u % 2
                    dve.wait_ge(*scores_done.at(n))
                    nc.vector.tensor_reduce(nmax[0:q, b:b + 1], misc[0:q, b, 0:L1], AX_X, ALU.max,
                                            negate=True).then_inc(*max_ready.inc(n))
                    if u < 24:
                        split(last_chunk[("gate", i, u)] + PART_SLOTS - 1)
                    dve.wait_ge(*exp_ready.at(n))
                    step(nc.vector.reciprocal(rinv[0:q, b:b + 1], rsum[0:q, b:b + 1]), ("rinv", n))
                    nc.vector.tensor_scalar(probs[0:q, b, :], probs[0:q, b, :], rinv[0:q, b:b + 1], None,
                                            ALU.mult).then_inc(*probs_ready.inc(n))
                    if u < 24 and u % 2:
                        done(("gate", i, u))
                        nc.vector.tensor_copy(gates[:, u, :], bank(("gate", i, u))[:, 0:L1]).then_inc(*dve_evac.inc(("gate", i, u)))
                dve.wait_ge(*mixed_copied.at(len(units) * (i + 1) - 1))
                for m in range(8):
                    dve.wait_ge(*act_step.at(("silu", i, m)))
                    dve.wait_ge(*xlo_ready.at((key, m)))
                    nc.vector.tensor_tensor(xt[:, m, :], o_raw[:, m, :], gates[:, m, :],
                                            ALU.mult).then_inc(*x_ready.inc((("o", i), m)))
                for m in range(DT):
                    split(last_chunk[("ya", i, m)] + PART_SLOTS - 1)
                    dve.wait_ge(*act_step.at(("sigm", i, 20)))
                    for s, kind in ((8, "ya"), (16, "yb")):
                        dve.wait_ge(*tile_done.at((kind, i, m)))
                        nc.vector.tensor_tensor(gates[:, s + m, :], gates[:, s + m, :], bank((kind, i, m))[:, 0:L1],
                                                ALU.mult).then_inc(*dve_evac.inc((kind, i, m)))
                    dve.wait_ge(*dve_evac.at(("yb", i, m)))
                    dve.wait_ge(*xlo_ready.at((("o", i), m)))
                    nc.vector.tensor_tensor(xt[:, m, :], gates[:, 8 + m, :], gates[:, 16 + m, :],
                                            ALU.add).then_inc(*x_ready.inc((("mix", i), m)))
                for m in range(DT):
                    done(("out", i, m))
                    nc.vector.tensor_tensor(h[:, m, :], h[:, m, :], bank(("out", i, m))[:, 0:L1],
                                            ALU.add).then_inc(*dve_evac.inc(("out", i, m)))
            variance("final", TT2)
            normalise("final", lambda m: v("final_g", m), SEQ, dst=h)
            variance("a", TT2)
            normalise("a", lambda m: v("a_norm", m), SEQ)

            dve.wait_ge(*pe_step.at("gates"))
            step(nc.vector.tensor_tensor(g8[:], misc[:, 0, 0:16].rearrange("p (t g) -> p t g", t=2),
                                         v("b_gates", 0, 8).unsqueeze(1).to_broadcast([P, 2, 8]), ALU.add), "g8")
            nc.vector.scalar_tensor_tensor(ab[:], g8[:, :, 4:8], -1.0, g8[:, :, 4:8], ALU.mult, ALU.max).then_inc(*dve_step.inc("ab"))
            split(last_chunk[("mq", 0)] + PART_SLOTS - 1)
            nc.vector.memset(cmax[:], 0.0).then_inc(*dve_step.inc("cmax0"))
            dve.wait_ge(*act_step.at("ln1"))
            nc.vector.scalar_tensor_tensor(lf[:], g8[:, :, 4:8], 0.0, ln1[:], ALU.min,
                                           ALU.subtract).then_inc(*dve_step.inc("lf"))
            split(last_chunk[("mq", 3)] + PART_SLOTS - 1)
            dve.wait_ge(*pe_step.at("a_row"))
            step(nc.vector.tensor_copy(nf[:], misc[:, 1, 16:24].rearrange("p (t g) -> p t g", t=2)), "nf")
            nc.vector.tensor_tensor(a_tok[:], g8[:, :, 0:4], nf[:], ALU.add).then_inc(*dve_step.inc("a_tok"))
            step(nc.vector.tensor_scalar(cmax[:, 0, P:], misc[0:M_HEADS, 0, 0:SEQ], 0.0, None, ALU.max), "m0")
            b = 0
            for r in range(8):
                d = 1 << r
                step(nc.vector.tensor_tensor(cmax[:, 1 - b, P:], cmax[:, b, P:], cmax[:, b, P - d:P + SEQ - d], ALU.max),
                     ("m", r) if r < 7 else "cmax")
                b = 1 - b
                if r % 2:
                    split(last_chunk[("mk", r // 2)] + PART_SLOTS - 2)
            dve.wait_ge(*pe_step.at("m_tok"))
            nc.vector.tensor_tensor(floor[:], nf[:], misc[:, 1, 24:32].rearrange("p (t g) -> p t g", t=2),
                                    ALU.subtract).then_inc(*dve_step.inc("fm"))
            split(last_chunk[("mk", 3)] + PART_SLOTS - 1)
            for t in range(2):
                for s in range(2):
                    done(("mv", t, s))
                    nc.vector.tensor_copy(v2[:, t, 512 * s:512 * s + 512], bank(("mv", t, s))).then_inc(*dve_evac.inc(("mv", t, s)))
            ct = const("causal_t")
            for s in range(2 * M_HEADS):
                hd = s // 2
                done(("mo", s))
                nc.vector.tensor_copy(og[:, s, :], bank(("mo", s))[:, 0:SEQ]).then_inc(*dve_evac.inc(("mo", s)))
                if s % 2 == 0:
                    dve.wait_ge(*pe_step.at(("mb", hd)))
                    nc.vector.scalar_tensor_tensor(dmat[:, hd, 0:SEQ], misc[:, 2, 0:SEQ], -1.0, ct, ALU.mult, ALU.add)
                    nc.vector.scalar_tensor_tensor(dmat[:, hd, SEQ:384], misc[:, 2, P:SEQ], -1.0, ct[:, 0:P], ALU.mult,
                                                   ALU.add).then_inc(*dve_step.inc(("d1", hd)))
                    split(last_chunk[("mo", s)] + PART_SLOTS - 1)
                    dve.wait_ge(*act_step.at(("dexp", hd)))
                    dve.wait_ge(*pe_step.at(("mst", hd)))
                    nc.vector.tensor_tensor(dmat[:, hd, :], dmat[:, hd, :], misc[:, 0, 0:384],
                                            ALU.mult).then_inc(*dve_step.inc(("sd", hd)))
                else:
                    split(last_chunk[("mo", s)] + PART_SLOTS - 1)
                    dve.wait_ge(*act_step.at(("num", hd)))
                    nc.vector.tensor_tensor(xt[:, 2 * hd:2 * hd + 2, 0:SEQ], num[:, 2 * hd:2 * hd + 2, :],
                                            num[:, 2 * hd:2 * hd + 2, :], ALU.mult).then_inc(*dve_step.inc(("nsq", hd)))
            dve.wait_ge(*pe_step.at("nss"))
            dve.wait_ge(*act_step.at("floor"))
            sums = misc[:, 1, 0:8].rearrange("p (t g) -> p t g", t=2)
            step(nc.vector.scalar_tensor_tensor(den[:], sums, -1.0, floor[:], ALU.mult, ALU.max), "-den")
            step(nc.vector.tensor_tensor(den[:], sums, den[:], ALU.max), "den")
            step(nc.vector.reciprocal(den[:], den[:]), "rden")
            f3 = fac[:, :].rearrange("p (t g) -> p t g", t=2)
            v3 = var[:, 0:8].rearrange("p (t g) -> p t g", t=2)
            step(nc.vector.tensor_tensor(f3, den[:], den[:], ALU.mult), "rden2")
            step(nc.vector.tensor_tensor(f3, f3, misc[:, 1, 8:16].rearrange("p (t g) -> p t g", t=2), ALU.mult), "nvar")
            nc.vector.tensor_scalar(v3, f3, 1.0 / 256, EPS, ALU.mult, ALU.add).then_inc(*var_ready.inc("mlstm"))
            dve.wait_ge(*rstd_ready.at("mlstm"))
            nc.vector.tensor_tensor(f3, rstd[:, 0:8].rearrange("p (t g) -> p t g", t=2), den[:],
                                    ALU.mult).then_inc(*dve_step.inc("fac"))
            for m in range(DT):
                dve.wait_ge(*pe_step.at(("fb", m // 2)))
                step(nc.vector.scalar_tensor_tensor(num[:, m, :], num[:, m, :], v("a_h_norm", m),
                                                    misc[:, (2, 0)[m // 2 % 2], 0:SEQ], ALU.mult, ALU.mult), ("hn", m))
                dve.wait_ge(*act_step.at(("so", m)))
                nc.vector.tensor_tensor(xt[:, m, 0:SEQ], num[:, m, :], og[:, m, :], ALU.mult).then_inc(*x_ready.inc(("mlstm", m)))

            def residual(kind):
                for m in range(DT):
                    done(kind + (m,))
                    nc.vector.tensor_tensor(h[:, m, 0:SEQ], h[:, m, 0:SEQ], bank(kind + (m,))[:, 0:SEQ],
                                            ALU.add).then_inc(*dve_evac.inc(kind + (m,)))

            def ffn(l):
                variance(("f", l), TT2)
                normalise(("f", l), lambda m: v("f_norm", 8 * l + m), SEQ)
                for j in range(FFT):
                    for c, (kind, dst) in enumerate((("uv", cv), ("ug", cg))):
                        split(last_chunk[(kind, l, j)] + PART_SLOTS - 1)
                        dve.wait_ge(*act_step.at((kind, l, j)))
                        o = bank((kind, l, j))
                        w = [v("conv_w", ((l * 3 + s) * 2 + c) * FFT + j) for s in range(2)]
                        y = dst[:, j % 2, :]
                        step(nc.vector.scalar_tensor_tensor(y[:, 1:SEQ], o[:, 0:SEQ - 1], w[1], y[:, 1:SEQ], ALU.mult, ALU.add),
                             ("conv", kind, l, j))
                        nc.vector.scalar_tensor_tensor(y[:, 2:SEQ], o[:, 0:SEQ - 2], w[0], y[:, 2:SEQ], ALU.mult,
                                                       ALU.add).then_inc(*dve_evac.inc((kind, l, j)))
                residual(("down", l))

            residual(("mout",))
            ffn(0)
            variance("kv", TT2)
            normalise("kv", lambda m: v("kv_norm", m), SEQ)
            normalise("b", lambda m: v("b_norm", m), SEQ, again="kv", bkey="kv")
            for m in range(16):
                name = (("kk", "qq")[m // 8], m % 8)
                split(last_chunk[name] + PART_SLOTS - 1)
                dve.wait_ge(*act_evac.at(name))
                if m >= 8:
                    dve.wait_ge(*pe_step.at(("st2", m - 8)))
                elif m < 8:
                    dve.wait_ge(*xlo_ready.at(("b", m)))
                nc.vector.tensor_tensor(xt[:, m % 8, 0:SEQ], qk2[:, m, :], qk2[:, m, :], ALU.mult).then_inc(*dve_step.inc(("sq2", m)))
            dve.wait_ge(*dve_step.at(("sq2", 15)))
            nc.vector.tensor_scalar(qk2[:, 0:8, :], qk2[:, 0:8, :], v("k_norm"), None, ALU.mult)
            nc.vector.tensor_scalar(qk2[:, 8:16, :], qk2[:, 8:16, :], qscale[:, 2:3], None,
                                    ALU.mult).then_inc(*dve_step.inc("xg2"))
            dve.wait_ge(*pe_step.at(("st2", 15)))
            nc.vector.tensor_scalar(var[:, 0:32], misc[:, 3, 0:32], 1.0 / P, EPS, ALU.mult, ALU.add).then_inc(*var_ready.inc("qk2"))
            for t in range(2):
                for s in range(2):
                    done(("vv", t, s))
                    nc.vector.tensor_copy(v2[:, t, 512 * s:512 * s + 512], bank(("vv", t, s))).then_inc(*dve_evac.inc(("vv", t, s)))
            sin2 = const("sin2", ROT).unsqueeze(1).to_broadcast([ROT, 2, SEQ])
            cos2 = const("cos2", ROT).unsqueeze(1).to_broadcast([ROT, 2, SEQ])
            dve.wait_ge(*dve_step.at("xg2"))
            for j in range(8):
                x2 = qk2[0:ROT, 2 * j:2 * j + 2, :]
                ta = rope_t[:, 0, :].rearrange("p (s t) -> p s t", s=2)
                dve.wait_ge(*pe_step.at(("rot2", j)))
                step(nc.vector.tensor_tensor(ta, misc[0:ROT, 0, :].rearrange("p (s t) -> p s t", s=2), sin2, ALU.mult), ("ra", j))
                step(nc.vector.tensor_tensor(x2, x2, cos2, ALU.mult), ("rc", j))
                step(nc.vector.tensor_tensor(x2, x2, ta, ALU.add), ("rs", j))
                x2 = qk2[:, 2 * j:2 * j + 2, :]
                step(nc.vector.tensor_tensor(x2, x2, misc[:, 1, :].rearrange("p (s t) -> p s t", s=2), ALU.mult), ("rope2", j))
            for u in range(len(units2)):
                n = 2 * len(units) + u
                keys = (units2[u][1] + 1) * P
                b = u % 2
                dve.wait_ge(*scores_done.at(n))
                nc.vector.tensor_reduce(nmax[:, b:b + 1], misc[:, b, 0:keys], AX_X, ALU.max, negate=True).then_inc(*max_ready.inc(n))
                dve.wait_ge(*exp_ready.at(n))
                step(nc.vector.reciprocal(rinv[:, b:b + 1], rsum[:, b:b + 1]), ("rinv", n))
                nc.vector.tensor_scalar(probs2[:, b, 0:keys], probs2[:, b, 0:keys], rinv[:, b:b + 1], None,
                                        ALU.mult).then_inc(*probs_ready.inc(n))
            residual(("aout",))
            ffn(1)

        @block.gpsimd
        def _(pool):
            def root(key, cols):
                pool.wait_ge(*var_ready.at(key))
                for n, (rows, c0, c1) in enumerate(cols):
                    ins = nc.gpsimd.tensor_tensor(rstd[0:rows, c0:c1], var[0:rows, c0:c1], mhalf[0:rows, c0:c1], ALU.pow)
                ins.then_inc(*rstd_ready.inc(key))

            def lower(key, dst, upper_, cols, tiles_=DT, src=xt):
                for m in range(tiles_):
                    pool.wait_ge(*xhi_ready.at((key, m)))
                    nc.gpsimd.tensor_tensor(dst[:, m, 0:cols], src[:, m, 0:cols], upper_[:, m, 0:cols].bitcast(F32),
                                            ALU.subtract).then_inc(*xlo_ready.inc((key, m)))

            pool.wait_ge(*dve_step.at("mhalf"))
            pool.wait_ge(*inputs_loaded.at("h"))
            three, two = [(P, 0, 2), (META, 2, 3)], [(P, 0, 2)]
            for i in range(LAYERS):
                root(("x", i), three)
                if i:
                    pool.wait_ge(*scores_done.at(len(units) * (i - 1) + 2 * NA_HEADS - 1))
                for r in range(2):
                    for hd in range(NA_HEADS):
                        src = bass.AP(tensor=rpb.tensor, offset=((i * NA_HEADS + hd) * RPB_H + 5 - r) * RPB_W - 48,
                                      ap=[[1, GRID_W], [RPB_W, 6], [1, GRID_W]])
                        pool.dma_start(bias[GRID_W * r:GRID_W * r + GRID_W, hd, :].rearrange("p (d j) -> p d j", d=6),
                                       src).then_inc(*bias_loaded.inc((i, r, hd), 16))
                lower(("x", i), xs_lo, xs_hi, L1)
                root(("qk", i), [(P, 0, 20), (META, 20, 30)])
                pool.wait_ge(*dve_step.at(("xg", i)))
                for j in range(5):
                    nc.gpsimd.tensor_tensor(rq[:, j, :], xg[:, j, :], const("cos1"), ALU.mult).then_inc(*pool_step.inc(("t1", i, j)))
                pool.wait_ge(*bias_loaded.at((i, 1, NA_HEADS - 1)))
                b3 = bias[:, :, :].rearrange("p h (d j) -> p (h d) j", j=GRID_W)
                nc.gpsimd.tensor_tensor(b3, b3, const("window").unsqueeze(1).to_broadcast([P, 6 * NA_HEADS, GRID_W]),
                                        ALU.add).then_inc(*pool_step.inc(("bias", i)))
                lower(("o", i), ys_lo, ys_hi, L1)
                lower(("mix", i), xs_lo, xs_hi, L1)
            root("final", two)
            root("a", two)
            lower("a", xs_lo, xs_hi, SEQ)
            root("mlstm", [(P, 0, 8)])
            lower("mlstm", ys_lo, ys_hi, SEQ)

            def ffn(l):
                root(("f", l), two)
                lower(("f", l), xs_lo, xs_hi, SEQ)
                for j in range(FFT):
                    pool.wait_ge(*act_step.at(("sg", l, j)))
                    nc.gpsimd.tensor_tensor(cv[:, j % 2, :], cv[:, j % 2, :], cg[:, j % 2, :],
                                            ALU.mult).then_inc(*pool_step.inc(("prod", l, j)))
                    pool.wait_ge(*xhi_ready.at((("act", l), j)))
                    nc.gpsimd.tensor_tensor(a_lo[:, j, :], cv[:, j % 2, :], a_hi[:, j, :].bitcast(F32),
                                            ALU.subtract).then_inc(*xlo_ready.inc((("act", l), j)))

            ffn(0)
            root("kv", two)
            lower("kv", xs_lo, xs_hi, SEQ)
            lower("b", ys_lo, ys_hi, SEQ)
            root("qk2", [(P, 0, 32)])
            lower("attn", ys_lo, ys_hi, SEQ)
            ffn(1)
    return {name: s.marks for name, s in signals.items()}


def shape_constants():
    c = np.zeros((P, NCONST), np.float32)

    def put(name, value):
        a, n = CONSTS[name]
        value = np.asarray(value, np.float32)
        assert value.shape[1] == n, name
        c[:value.shape[0], a:a + n] = value

    put("ident", np.eye(P))
    rot = np.zeros((P, P))
    for q in range(P):
        rot[(q + 16, q) if q % 32 < 16 else (q - 16, q)] = -1.0 if q % 32 < 16 else 1.0
    put("rot1", rot)
    jrev = np.zeros((P, P))
    for q in range(P):
        jrev[GRID_W * (q // GRID_W) + GRID_W - 1 - q % GRID_W, q] = 1.0
    put("jrev", jrev)
    t = np.arange(SEQ)
    row = np.concatenate([t // GRID_W, np.zeros(META, int)]).astype(np.float32)
    col = np.concatenate([t % GRID_W, np.zeros(META, int)]).astype(np.float32)
    inv = np.float32(10000.0) ** (-np.arange(0, 32, 2, dtype=np.float32) / np.float32(32))
    ar, ac = (inv[:, None] * z[None, :] for z in (row, col))
    ang = np.concatenate([ar, ar, ac, ac] * 2, axis=0)
    put("cos1", np.cos(ang))
    put("sin1", np.sin(ang))
    cc = GRID_W - 1 - np.arange(P) % GRID_W
    start = np.clip(cc - NA_KW // 2, 0, GRID_W - NA_KW)[:, None]
    j = np.arange(GRID_W)[None, :]
    put("window", np.where((j >= start) & (j < start + NA_KW), 0.0, NEG))
    a, b = np.arange(P)[:, None], np.arange(P)[None, :]
    put("causal", np.where(b <= a, 0.0, NEG))
    put("causal_t", np.concatenate([np.where(a <= b, 0.0, NEG), np.zeros((P, P))], axis=1))
    s, u = np.arange(P)[:, None], np.arange(SEQ)[None, :]
    put("tri_neg", np.concatenate([-(s + P * k <= u).astype(np.float32) for k in range(2)], axis=1))
    put("eye2", np.concatenate([(s + P * k == u).astype(np.float32) for k in range(2)], axis=1))
    put("head_sum", np.stack([np.arange(P) < HD, np.arange(P) >= HD], axis=1))
    put("ones", np.ones((P, 2)))
    put("sel4", np.repeat(np.eye(M_HEADS), P, axis=1))
    put("sel10", np.repeat(np.eye(10), HD, axis=1))
    inv2 = np.float32(500000.0) ** (-np.arange(0, ROT, 2, dtype=np.float32) / np.float32(ROT))
    ang2 = inv2[:, None] * t[None, :].astype(np.float32)
    put("cos2", np.cos(np.concatenate([ang2, ang2])))
    put("sin2", np.sin(np.concatenate([ang2, ang2])))
    rot2 = np.zeros((ROT, ROT))
    for q in range(ROT):
        rot2[(q + 16, q) if q < 16 else (q - 16, q)] = -1.0 if q < 16 else 1.0
    put("rot2", rot2)
    return c


def cols(x):
    return np.ascontiguousarray(x).reshape(-1, P).T


def pair_heads(w, axis):
    w = np.moveaxis(w, axis, 0)
    w = w.reshape(KV, GROUP, HD, *w.shape[1:])
    w = np.swapaxes(w, 0, 1).reshape(KV * GROUP * HD, *w.shape[3:])
    return np.moveaxis(w, 0, axis)


def by_tile(w):
    k, m = w.shape
    return w.reshape(k // P, P, m // P, P).transpose(2, 0, 1, 3).reshape(-1, P, P)


def by_row(w):
    k, m = w.shape
    return w.reshape(k // P, P, m // P, P).transpose(0, 2, 1, 3).reshape(-1, P, P)


def weight_stream(inp):
    blocks = []
    for i in range(LAYERS):
        w = inp["w_in"][i]
        qa, ka, va, za, qb, kb, vb, zb, ga, gb = np.split(w, np.cumsum([512, 128, 128, 512, 512, 512, 512, 512, 1024]), axis=1)
        blocks += [by_tile(ka), by_tile(pair_heads(qa, 1)), by_tile(qb), by_tile(kb), by_row(va), by_row(vb),
                   by_tile(pair_heads(za, 1)), by_tile(zb), by_tile(ga), by_tile(gb)]
        wa, wn = by_tile(pair_heads(inp["w_o_attn"][i], 0)), by_tile(inp["w_o_na"][i])
        blocks += [np.stack([wa.reshape(DT, 4, P, P), wn.reshape(DT, 4, P, P)], axis=1).reshape(-1, P, P)]
        blocks += [by_tile(inp["w_out"][i])]
    w = inp["a_w_in_2"][0]
    blocks += [by_tile(w[:, 0:1024]), by_row(w[:, 1024:2048]), by_tile(w[:, 2048:3072]), by_tile(inp["a_w_out_2"][0])]
    for l in range(2):
        up = by_tile(inp["f_w_up_2"][l]).reshape(2, FFT, DT, P, P).swapaxes(0, 1)
        blocks += [up.reshape(-1, P, P), by_tile(inp["f_w_down_2"][l])]
        if l == 0:
            w = inp["w_kv_2"]
            blocks += [by_tile(w[:, 0:1024]), by_tile(inp["b_w_q_2"][0]), by_row(w[:, 1024:2048]), by_tile(inp["b_w_o_2"][0])]
    stream = np.concatenate(blocks)
    return np.ascontiguousarray(stream.reshape(-1, CH, P, P).transpose(0, 2, 1, 3)).reshape(-1, P, CH * P)


def parameter_vectors(inp):
    g = inp["a_b_gates_2"][0].reshape(1, 8)
    w = inp["a_w_in_2"][0][:, 3072:3080].reshape(DT, P, 8).transpose(1, 0, 2).reshape(P, 64)
    two = lambda x: np.concatenate([x, x], axis=1).T
    parts = {
        "norm_g": cols(inp["norm_g"]), "qg": two(inp["q_norm_g"]), "kg": two(inp["k_norm_g"]),
        "final_g": cols(inp["final_norm_g"]), "a_norm": cols(inp["a_norm_2"]), "a_h_norm": cols(inp["a_h_norm_2"]),
        "kv_norm": cols(inp["kv_norm_2"]), "k_norm": cols(inp["k_norm_2"]), "b_norm": cols(inp["b_norm_2"]),
        "b_q_norm": cols(inp["b_q_norm_2"]), "f_norm": cols(inp["f_norm_2"]), "conv_w": cols(inp["f_conv_w_2"]),
        "conv_b": cols(inp["f_conv_b_2"]), "b_gates": np.broadcast_to(g, (P, 8)), "w_gates": w,
    }
    assert all(parts[n].shape == (P, k) for n, (_, k) in VECS.items())
    return np.ascontiguousarray(np.concatenate([parts[n] for n in VECS], axis=1))


def kernel(**inputs):
    import concourse.bacc as bacc
    from concourse.bass_utils import run_bass_kernel_spmd

    inp = {k: np.asarray(v) for k, v in inputs.items()}
    tokens = np.concatenate([inp["x"][0], inp["meta_tokens"]], axis=0)
    arrays = {
        "x_t": np.ascontiguousarray(tokens.T.reshape(DT, P, L1).transpose(1, 0, 2)),
        "consts": shape_constants(),
        "vecs": parameter_vectors(inp),
        "rpb": np.ascontiguousarray(inp["na_rpb"]),
        "weights": weight_stream(inp),
    }

    def build(known):
        nc = bacc.Bacc("TRN2", target_bir_lowering=False, num_devices=1)
        args = [nc.dram_tensor(n, a.shape, F32, kind="ExternalInput").ap() for n, a in arrays.items()]
        out = nc.dram_tensor("out", (P, DT, SEQ), F32, kind="ExternalOutput").ap()
        return nc, program(nc, *args, out, known)

    _, marks = build({})
    nc, _ = build(marks)
    r = run_bass_kernel_spmd(nc, [arrays], core_ids=[0])
    got = r.results[0]["out"]
    return got.transpose(2, 1, 0).reshape(1, SEQ, D)
```

```python
from contextlib import ExitStack

import numpy as np

import concourse.bass as bass
from concourse import mybir

F32 = mybir.dt.float32
PART = mybir.dt.float32r
ALU = mybir.AluOpType
ACT = mybir.ActivationFunctionType
AX_X = mybir.AxisListType.X

P = 128
D = 1024
DT = D // P
SEQ = 256
META = 16
L1 = SEQ + META
LAYERS = 2
EPS = 1e-6
NEG = -1e30

GRID_W, NA_KW, RPB_H, RPB_W = 64, 16, 15, 31
HD = 64
GROUP = 4
KV = 2
NA_HEADS = 8
VCOLS = KV * HD + NA_HEADS * HD
M_HEADS = 4
A_HEADS = 8
ROT = 32
FFT = 2816 // P

TT1 = [(0, 128), (128, 128), (256, META)]
TT2 = TT1[:2]

CH = 8
RAW_SLOTS = 4
PART_SLOTS = 4

CONSTS = {}
_at = 0
for _name, _n in [("ident", 128), ("ones", 2), ("rot1", 128), ("jrev", 128), ("cos1", L1), ("sin1", L1), ("window", GRID_W),
                  ("causal", 128), ("tri_neg", 512), ("eye2", 512), ("causal_t", 256), ("head_sum", 2),
                  ("sel4", 512), ("sel10", 5 * 128), ("cos2", 256), ("sin2", 256), ("rot2", 32)]:
    CONSTS[_name] = (_at, _n)
    _at += _n
NCONST = _at
NFIRST = 130
VECS = {}
_at = 0
for _name, _n in [("norm_g", 16), ("qg", 2), ("kg", 2), ("final_g", 8), ("a_norm", 8), ("a_h_norm", 8), ("kv_norm", 8),
                  ("k_norm", 1), ("b_norm", 8), ("b_q_norm", 1), ("f_norm", 16), ("conv_w", 2 * 3 * 2 * FFT),
                  ("conv_b", 2 * 2 * FFT), ("b_gates", 8), ("w_gates", 64)]:
    VECS[_name] = (_at, _n)
    _at += _n
NVEC = _at


class Signal:

    def __init__(self, sem, known):
        self.sem, self.known, self.marks, self.n = sem, known, {}, 0

    def inc(self, key, by=1):
        assert key not in self.marks, key
        self.n += by
        self.marks[key] = self.n
        return self.sem, by

    def at(self, key):
        assert not self.known or key in self.known, key
        return self.sem, self.known.get(key, 1)


UNITS = 2 * NA_HEADS + 18


def filler(u):
    gates = [("gate", n) for n in range(24) if n * 27 // 24 == u]
    return gates + ([("yb", u - 27)] if 27 <= u < 27 + DT else [])


UNITS2 = 2 * A_HEADS


def attention_steps(m):
    return range(max(0, 2 * m - 6), 2 * m - 4 if m < DT - 1 else UNITS2 + 2) if m >= 3 else range(0)


def rope_at(m=None, step=None):
    if step is not None:
        return [6, 7] if step == 11 else []
    return [m - 2, m - 1] if m in (2, 4, 6) else []


def tile_list():
    tiles, at = [], 0

    def add(name, engine, blocks):
        nonlocal at
        tiles.append((name, engine, at, blocks))
        at += blocks

    def rows(names, blocks):
        nonlocal at
        for name in names:
            tiles.append((name, "dve", at, blocks))
        at += blocks

    for i in range(LAYERS):
        add(("ka", i), "act", DT)
        for m in range(4):
            add(("qa", i, m), "act", DT)
        for m in range(4):
            add(("qb", i, m), "dve", DT)
        for m in range(4):
            add(("kb", i, m), "dve", DT)
        rows([("va", i, t) for t in range(3)], DT)
        rows([("vb", i, t) for t in range(3)], 4 * DT)
        for u in range(UNITS + 2):
            for kind, n in filler(u):
                add((kind, i, n), "dve", DT if kind == "gate" else 4)
            if u >= 2:
                add(("mx", i, u - 2), "act", 0)
        for m in range(DT):
            add(("ya", i, m), "dve", 4)
        for m in range(DT):
            add(("out", i, m), "dve", DT)
    for m in range(4):
        add(("mq", m), "dve", DT)
    for m in range(4):
        add(("mk", m), "dve", DT)
    rows([("mv", t, s) for t in range(2) for s in range(2)], 8 * DT)
    for m in range(DT):
        add(("mo", m), "dve", DT)
    for m in range(DT):
        add(("mout", m), "dve", DT)
    for l in range(2):
        for j in range(FFT):
            add(("uv", l, j), "dve", DT)
            add(("ug", l, j), "dve", DT)
        for m in range(DT):
            add(("down", l, m), "dve", FFT)
        if l == 0:
            for m in range(DT):
                add(("kk", m), "act", DT)
            rows([("vv", t, s) for t in range(2) for s in range(2)], 8 * DT)
            for m in range(DT):
                add(("qq", m), "act", DT)
                for hd in rope_at(m):
                    add(("rope", hd), "dve", 0)
                for u in attention_steps(m):
                    for hd in rope_at(step=u):
                        add(("rope", hd), "dve", 0)
                    if u >= 2:
                        add(("mx2", u - 2), "dve", 0)
            for m in range(DT):
                add(("aout", m), "dve", DT)
    return tiles, at // CH


def program(nc, x_t, consts_d, vecs_d, rpb, weights, out, known):
    ctx = ExitStack()
    with ctx:
        signals = {}

        def sb(name, shape, dt=F32, stack=ctx):
            return stack.enter_context(nc.sbuf_tensor(name, shape, dt))

        def signal(name):
            signals[name] = Signal(ctx.enter_context(nc.semaphore(name)), known.get(name, {}))
            return signals[name]

        acc = ctx.enter_context(nc.psum_tensor("acc", [P, 4, 512], F32))
        misc = ctx.enter_context(nc.psum_tensor("misc", [P, 4, 512], F32))
        raw = sb("raw", [P, RAW_SLOTS, CH * P])
        w_hi = sb("w_hi", [P, PART_SLOTS, CH * P], PART)
        w_lo = sb("w_lo", [P, PART_SLOTS, CH * P], PART)
        cst = sb("cst", [P, NCONST])
        vec = sb("vec", [P, NVEC])
        h = sb("h", [P, DT, L1])
        xt = sb("xt", [P, DT, L1])
        xs_hi = sb("xs_hi", [P, DT, L1], PART)
        xs_lo = sb("xs_lo", [P, DT, L1], PART)
        ys_hi = sb("ys_hi", [P, DT, L1], PART)
        ys_lo = sb("ys_lo", [P, DT, L1], PART)
        var = sb("var", [P, 32])
        rstd = sb("rstd", [P, 32])
        mhalf = sb("mhalf", [P, 32])
        nmax = sb("nmax", [P, 2])
        rsum = sb("rsum", [P, 2])
        rinv = sb("rinv", [P, 2])
        rtok = sb("rtok", [P, 4])
        eps_var = sb("eps_var", [P, 4])
        sq_sum = sb("sq_sum", [P, L1])
        rb_sb = sb("rb_sb", [P, 2 * SEQ])
        fga = sb("fga", [P, DT])
        qscale = sb("qscale", [P, 3])
        gw_hi = sb("gw_hi", [P, 64], PART)
        gw_lo = sb("gw_lo", [P, 64], PART)

        with ExitStack() as first:
            rq = sb("rq", [P, 5, L1], F32, first)
            xg = sb("xg", [P, 5, L1], F32, first)
            qf = sb("qf", [P, 5, L1], F32, first)
            rrow = sb("rrow", [10, L1], F32, first)
            t2 = sb("t2", [P, L1], F32, first)
            qkn = sb("qkn", [P, 8, L1], F32, first)
            v_sb = sb("v_sb", [P, 3, VCOLS], F32, first)
            gates = sb("gates", [P, 24, L1], F32, first)
            o_raw = sb("o_raw", [P, 8, L1], F32, first)
            bias = sb("bias", [P, NA_HEADS, 6 * GRID_W], F32, first)
            probs = sb("probs", [P, 2, L1], F32, first)
            pt = sb("pt", [P, 2, 384], F32, first)
            pm = sb("pm", [META, 128], F32, first)
            pmt = sb("pmt", [META, 128], F32, first)
            z_tanh = xg
            ms = sb("ms", [META, 16], F32, first)
        with ExitStack() as mixers:
            qk2 = sb("qk2", [P, 16, SEQ], F32, mixers)
            v2 = sb("v2", [P, 2, D], F32, mixers)
            og = sb("og", [P, DT, SEQ], F32, mixers)
            num = sb("num", [P, DT, SEQ], F32, mixers)
            dmat = sb("dmat", [P, M_HEADS, 384], F32, mixers)
            sq_sum2 = sb("sq_sum2", [P, SEQ], F32, mixers)
            gate_rows = sb("gate_rows", [8, SEQ], F32, mixers)
            g8 = sb("g8", [P, 2, 8], F32, mixers)
            ab = sb("ab", [P, 2, 4], F32, mixers)
            ln1 = sb("ln1", [P, 2, 4], F32, mixers)
            lf = sb("lf", [P, 2, 4], F32, mixers)
            nf = sb("nf", [P, 2, 4], F32, mixers)
            a_tok = sb("a_tok", [P, 2, 4], F32, mixers)
            floor = sb("floor", [P, 2, 4], F32, mixers)
            den = sb("den", [P, 2, 4], F32, mixers)
            fac = sb("fac", [P, 8], F32, mixers)
            cmax = sb("cmax", [M_HEADS, 2, 128 + SEQ], F32, mixers)
            probs2 = sb("probs2", [P, 2, SEQ], F32, mixers)
            pt2 = sb("pt2", [P, 2, SEQ], F32, mixers)
            rope_t = sb("rope_t", [ROT, 2, SEQ], F32, mixers)
            x_cos = sb("x_cos", [ROT, 16, SEQ], F32, mixers)
        with ExitStack() as ffn_mem:
            a_hi = sb("a_hi", [P, FFT, SEQ], PART, ffn_mem)
            a_lo = sb("a_lo", [P, FFT, SEQ], PART, ffn_mem)
            up = sb("up", [P, 2, 2, SEQ], F32, ffn_mem)
            cv = sb("cv", [P, 2, SEQ], F32, ffn_mem)
            cg = sb("cg", [P, 2, SEQ], F32, ffn_mem)

        def const(name, rows=P):
            a, n = CONSTS[name]
            return cst[0:rows, a:a + n]

        def v(name, i=0, n=1):
            a = VECS[name][0] + i
            return vec[:, a:a + n]

        ident = const("ident")
        qn, kn = qkn[:, 0:4, :], qkn[:, 4:8, :]
        pair = ((xs_hi, xs_lo), (ys_hi, ys_lo))

        inputs_loaded = signal("inputs_loaded")
        h_loaded = signal("h_loaded")
        h2_loaded = signal("h2_loaded")
        first_loaded = signal("first_loaded")
        cst_loaded = signal("cst_loaded")
        bias_loaded = signal("bias_loaded")
        raw_landed = [signal(f"raw_landed{i}") for i in range(RAW_SLOTS)]
        hi_ready = signal("hi_ready")
        lo_ready = signal("lo_ready")
        chunk_used = signal("chunk_used")
        tile_done = signal("tile_done")
        act_evac = signal("act_evac")
        dve_evac = signal("dve_evac")
        sq_ready = signal("sq_ready")
        stats_done = signal("stats_done")
        var_ready = signal("var_ready")
        rstd_ready = signal("rstd_ready")
        bcast_done = signal("bcast_done")
        x_ready = signal("x_ready")
        xhi_ready = signal("xhi_ready")
        xlo_ready = signal("xlo_ready")
        xlo_ready_dve = signal("xlo_ready_dve")
        scores_done = signal("scores_done")
        max_ready = signal("max_ready")
        exp_ready = signal("exp_ready")
        probs_ready = signal("probs_ready")
        turned = signal("turned")
        turned_copied = signal("turned_copied")
        act_step = signal("act_step")
        dve_step = signal("dve_step")
        pool_step = signal("pool_step")
        pe_step = signal("pe_step")
        stored = signal("stored")

        tiles, n_chunks = tile_list()
        assert n_chunks == weights.shape[0]
        index = {name: n for n, (name, *_) in enumerate(tiles)}
        last_chunk = {name: (b + k - 1) // CH for name, _, b, k in tiles}
        ends_tile = {b + k: name for name, _, b, k in tiles if k}

        def bank(name):
            return acc[:, index[name] % 4, :]

        def chunk_free(eng, c):
            name = ends_tile.get((c + 1) * CH)
            eng.wait_ge(*(tile_done.at(name) if name else chunk_used.at(c)))

        block = ctx.enter_context(nc.Block())

        @block.sync
        def _(sp):
            def load_bias(i):
                for r in range(2):
                    for hd in range(NA_HEADS):
                        src = bass.AP(tensor=rpb.tensor, offset=((i * NA_HEADS + hd) * RPB_H + 5 - r) * RPB_W - 48,
                                      ap=[[1, GRID_W], [RPB_W, 6], [1, GRID_W]])
                        sp.dma_start(bias[GRID_W * r:GRID_W * r + GRID_W, hd, :].rearrange("p (d j) -> p d j", d=6),
                                     src).then_inc(*bias_loaded.inc((i, r, hd), 16))

            sp.dma_start(vec[:], vecs_d).then_inc(*inputs_loaded.inc("vec", 16))
            sp.dma_start(h[:, 0:4], x_t[:, 0:4]).then_inc(*h_loaded.inc("h0", 16))
            sp.dma_start(h[:, 4:8], x_t[:, 4:8]).then_inc(*h2_loaded.inc("h4", 16))
            for c in range(n_chunks):
                if c >= RAW_SLOTS:
                    sp.wait_ge(*lo_ready.at(c - RAW_SLOTS))
                sp.dma_start(raw[:, c % RAW_SLOTS, :], weights[c]).then_inc(*raw_landed[c % RAW_SLOTS].inc(c, 16))
                if c == 1:
                    sp.dma_start(cst[:, 0:NFIRST], consts_d[:, 0:NFIRST]).then_inc(*first_loaded.inc("first", 16))
                if c == 3:
                    sp.dma_start(cst[:, NFIRST:], consts_d[:, NFIRST:]).then_inc(*cst_loaded.inc("cst", 16))
                if c == 6:
                    load_bias(0)
                if c == last_chunk[("ya", 0, 0)]:
                    sp.wait_ge(*scores_done.at(2 * NA_HEADS - 1))
                    load_bias(1)
            for m in range(DT):
                sp.wait_ge(*dve_evac.at(("down", 1, m)))
                sp.dma_start(out[:, m], h[:, m, 0:SEQ]).then_inc(*stored.inc(m, 16))
            sp.wait_ge(*stored.at(DT - 1))

        units = [("na", hd, a) for hd in range(NA_HEADS) for a in range(2)]
        na0, ga0 = 0, len(units)
        units += [("ga", g, c0, min(128, 4 * L1 - c0)) for c0 in range(0, 4 * L1, 128) for g in range(KV)]
        assert len(units) == UNITS
        units2 = [(hd, t) for hd in range(A_HEADS) for t in range(2)]

        def gated_at(u):
            if u in (7, 11, 15, 19):
                return [4 + (u - 7) // 4]
            return [m for m in range(3) if u == ga0 + 2 * ((L1 * (m + 1) - 1) // P) + 1 + 3]

        def meta_at(hd):
            return 64 * (hd % 2) + META * (hd // 2)

        def qflat(g):
            return qf[HD * g:HD * g + HD, 1:5, :].rearrange("p j t -> p (j t)")

        @block.tensor
        def _(pe):
            seen = set()

            def once(signal_, key):
                if (id(signal_), key) not in seen:
                    seen.add((id(signal_), key))
                    pe.wait_ge(*signal_.at(key))

            def once_low(key, k):
                if key == "attn":
                    once(dve_evac, ("mx2", 2 * k + 1))
                else:
                    direct = (key[0] if isinstance(key, tuple) else key) in ("x", "a", "kv", "b", "f")
                    once(xlo_ready_dve if direct else xlo_ready, (key, k))

            def weight(b, n=P):
                c, j = divmod(b, CH)
                once(lo_ready, c)
                s = c % PART_SLOTS
                return w_hi[:, s, j * P:j * P + n], w_lo[:, s, j * P:j * P + n]

            def acc_free(name):
                n = index[name] - 4
                if n >= 0:
                    before, engine, *_ = tiles[n]
                    pe.wait_ge(*(act_evac if engine == "act" else dve_evac).at(before))

            def parts(o, lhs, rhs, first, last):
                pe.matmul(o, lhs[0], rhs[0], start=first, stop=False)
                pe.matmul(o, lhs[0], rhs[1], start=False, stop=False)
                return pe.matmul(o, lhs[1], rhs[0], start=False, stop=last)

            def tile(name, x_hi, x_lo, key, k0=0, cols=SEQ):
                _, _, b0, blocks = tiles[index[name]]
                acc_free(name)
                o = bank(name)[:, 0:cols]
                for i in range(blocks):
                    w = weight(b0 + i)
                    once_low(key, k0 + i)
                    mm = parts(o, w, (x_hi[:, k0 + i, 0:cols], x_lo[:, k0 + i, 0:cols]), i == 0, i == blocks - 1)
                    if i == blocks - 1:
                        mm.then_inc(*tile_done.inc(name))
                    elif (b0 + i) % CH == CH - 1:
                        mm.then_inc(*chunk_used.inc((b0 + i) // CH))

            def row_tiles(names, x_hi, x_lo, key, tts, width, halves=1, between=None):
                b0 = tiles[index[names[0]]][2]
                for name in names:
                    acc_free(name)
                bk = width // P * halves
                for c0 in range(0, DT * bk, CH):
                    for n, name in enumerate(names):
                        t, s = divmod(n, halves)
                        tok, tn = tts[t]
                        for k in range(c0 // bk, (c0 + CH) // bk):
                            w = weight(b0 + k * bk + s * (width // P), width)
                            once_low(key, k)
                            x = (x_hi[:, k, tok:tok + tn], x_lo[:, k, tok:tok + tn])
                            o = bank(name)[0:tn, 0:width]
                            mm = parts(o, x, w, k == 0, k == DT - 1)
                        if c0 + CH == DT * bk:
                            mm.then_inc(*tile_done.inc(name))
                    if c0 + CH < DT * bk:
                        mm.then_inc(*chunk_used.inc((b0 + c0) // CH))
                    if between:
                        between(c0 // CH)

            def stats(key, tts, n=0):
                pe.wait_ge(*pool_step.at(("sum", key, DT - 1)))
                for t, (t0, tn) in enumerate(tts):
                    c = 4 * n + t
                    mm = pe.matmul(misc[0:tn, 3, c:c + 1], (sq_sum, sq_sum2)[n][:, t0:t0 + tn], const("ones")[:, 0:1], start=True,
                                   stop=True)
                mm.then_inc(*stats_done.inc(key))

            def spread(key, tts, ready=None, col=0):
                pe.wait_ge(*rstd_ready.at(ready or key))
                c0 = SEQ * (col // 2)
                for t, (t0, tn) in enumerate(tts):
                    mm = pe.matmul(misc[:, 2, c0 + t0:c0 + t0 + tn], rtok[0:tn, col + t:col + t + 1].to_broadcast([tn, P]),
                                   ident[0:tn, 0:tn], start=True, stop=True)
                mm.then_inc(*bcast_done.inc(key))

            for i in range(LAYERS):
                key = ("x", i)
                xp, op = pair[i % 2], pair[1 - i % 2]

                def proj(name):
                    tile(name, *xp, key, cols=L1)

                def rot(j):
                    pe.wait_ge(*dve_step.at(("xg", i)))
                    if j >= 2:
                        pe.wait_ge(*dve_step.at(("t2", i, j - 2)))
                    pe.matmul(misc[:, j % 2, 0:L1], const("rot1"), xg[:, j, :], start=True,
                              stop=True).then_inc(*pe_step.inc(("rot", i, j)))

                def rb(j):
                    pe.wait_ge(*dve_step.at(("rrow", i)))
                    if j >= 2:
                        pe.wait_ge(*dve_step.at(("qf", i, j - 2)))
                    a, _ = CONSTS["sel10"]
                    pe.matmul(misc[:, 2 + j % 2, 0:L1], cst[0:10, a + j * P:a + (j + 1) * P], rrow[:, :], start=True,
                              stop=True).then_inc(*pe_step.inc(("rb", i, j)))

                proj(("ka", i))
                for m in range(4):
                    proj(("qa", i, m))
                    if m == 0:
                        if i == 0:
                            pe.wait_ge(*first_loaded.at("first"))
                        stats(key, TT1)
                    if m == 1:
                        spread(key, TT1)
                proj(("qb", i, 0))
                if i == 0:
                    pe.wait_ge(*cst_loaded.at("cst"))
                for j in range(5):
                    pe.wait_ge(*dve_step.at(("qsq", i, j)))
                    for t, (t0, tn) in enumerate(TT1):
                        mm = pe.matmul(misc[0:tn, 3, 10 * t + 2 * j:10 * t + 2 * j + 2], qf[:, j, t0:t0 + tn],
                                       const("head_sum"), start=True, stop=True)
                mm.then_inc(*stats_done.inc(("qk", i)))
                proj(("qb", i, 1))
                rot(0)
                rot(1)
                for m in (2, 3):
                    proj(("qb", i, m))
                proj(("kb", i, 0))
                pe.wait_ge(*rstd_ready.at(("qk", i)))
                for t, (t0, tn) in enumerate(TT1):
                    mm = pe.matmul(misc[0:10, 3, t0:t0 + tn], rstd[0:tn, 10 * t:10 * t + 10], ident[0:tn, 0:tn],
                                   start=True, stop=True)
                mm.then_inc(*pe_step.inc(("rt", i)))
                proj(("kb", i, 1))
                rb(0)
                rb(1)
                proj(("kb", i, 2))
                for j in range(2, 5):
                    rot(j)
                    rb(j)
                proj(("kb", i, 3))
                pe.wait_ge(*dve_evac.at(("kb", i, 3)))
                pe.wait_ge(*dve_step.at(("t2", i, 4)))
                for hd in range(NA_HEADS):
                    a = HD * (hd % 2)
                    mm = pe.matmul(misc[0:META, hd % 2, META * (hd // 2):META * (hd // 2) + META], qn[a:a + HD, hd // 2, SEQ:L1],
                                   kn[a:a + HD, hd // 2, SEQ:L1], start=True, stop=True)
                mm.then_inc(*pe_step.inc(("meta_s", i)))
                row_tiles([("va", i, t) for t in range(3)], *xp, key, TT1, P)
                row_tiles([("vb", i, t) for t in range(3)], *xp, key, TT1, 512)
                pe.wait_ge(*dve_step.at(("meta_p", i)))
                pe.wait_ge(*dve_step.at(("qf", i, 4)))
                for hd in range(NA_HEADS):
                    mm = pe.matmul(misc[0:META, 2, META * hd:META * hd + META], pm[:, meta_at(hd):meta_at(hd) + META],
                                   ident[0:META, 0:META], start=True, stop=True)
                mm.then_inc(*pe_step.inc(("meta_t", i)))

                def scores(u):
                    n = len(units) * i + u
                    if u >= 2:
                        pe.wait_ge(*exp_ready.at(n - 2))
                    o = misc[:, u % 2, 0:L1]
                    if units[u][0] == "na":
                        _, hd, a = units[u]
                        p0 = HD * (hd % 2)
                        if u == 0:
                            pe.wait_ge(*pool_step.at(("bias", i)))
                        pe.matmul(o, qn[p0:p0 + HD, hd // 2, a * P:(a + 1) * P], kn[p0:p0 + HD, hd // 2, :],
                                  start=True, stop=False)
                        b0 = 2 * (1 - a) * GRID_W
                        mm = pe.matmul(o[:, 0:SEQ], const("jrev"), bias[:, hd, b0:b0 + 4 * GRID_W], start=False,
                                       stop=True)
                    else:
                        _, g, c0, cn = units[u]
                        mm = pe.matmul(o[0:cn], qflat(g)[:, c0:c0 + cn], qf[HD * g:HD * g + HD, 0, :], start=True,
                                       stop=True)
                    mm.then_inc(*scores_done.inc(n))

                def turn(u):
                    n = len(units) * i + u
                    pe.wait_ge(*probs_ready.at(n))
                    if u >= 1:
                        pe.wait_ge(*turned_copied.at(n - 1))
                    q = P if units[u][0] == "na" else units[u][3]
                    for t, (t0, tn) in enumerate(TT1):
                        mm = pe.matmul(misc[0:tn, 2, t * P:t * P + q], probs[0:q, u % 2, t0:t0 + tn], ident[0:q, 0:q],
                                       start=True, stop=True)
                    mm.then_inc(*turned.inc(n))

                def mix(u):
                    n = len(units) * i + u
                    pe.wait_ge(*turned_copied.at(n))
                    acc_free(("mx", i, u))
                    if units[u][0] == "na":
                        _, hd, _ = units[u]
                        q, half, v0 = P, hd % 2, KV * HD + hd * HD
                    else:
                        _, half, _, q = units[u]
                        v0 = half * HD
                    for t, (t0, tn) in enumerate(TT1):
                        mm = pe.matmul(bank(("mx", i, u))[HD * half:HD * half + HD, 0:q],
                                       v_sb[0:tn, t, v0:v0 + HD], pt[0:tn, u % 2, t * P:t * P + q],
                                       start=(t == 0), stop=(t == 2))
                    mm.then_inc(*tile_done.inc(("mx", i, u)))

                scores(0)
                proj(("gate", i, 0))
                pe.wait_ge(*dve_step.at(("meta_pt", i)))
                for hd in range(NA_HEADS):
                    a = HD * (hd % 2)
                    c0 = KV * HD + hd * HD
                    mm = pe.matmul(misc[a:a + HD, 3, META * (hd // 2):META * (hd // 2) + META],
                                   v_sb[0:META, 2, c0:c0 + HD], pmt[:, META * hd:META * hd + META], start=True, stop=True)
                mm.then_inc(*pe_step.inc(("meta_o", i)))
                pe.wait_ge(*act_step.at(("meta_o", i)))
                for u in range(1, len(units) + 2):
                    if u < len(units):
                        scores(u)
                    for kind, m in filler(u):
                        if kind == "gate":
                            proj((kind, i, m))
                        else:
                            tile((kind, i, m), *op, ("o", i), 4, L1)
                    if u - 1 < len(units):
                        turn(u - 1)
                    if u >= 2:
                        mix(u - 2)
                for m in range(DT):
                    tile(("ya", i, m), *op, ("o", i), 0, L1)
                for m in range(DT):
                    tile(("out", i, m), *xp, ("mix", i), 0, L1)

            tile(("mq", 0), xs_hi, xs_lo, "a")
            stats("final", TT2)
            stats("a", TT2, 1)
            tile(("mq", 1), xs_hi, xs_lo, "a")
            pe.wait_ge(*dve_step.at("gw_lo"))
            for k in range(DT):
                mm = parts(misc[0:8, 0, 0:SEQ], (gw_hi[:, 8 * k:8 * k + 8], gw_lo[:, 8 * k:8 * k + 8]),
                           (xs_hi[:, k, 0:SEQ], xs_lo[:, k, 0:SEQ]), k == 0, k == DT - 1)
            mm.then_inc(*pe_step.inc("gate_rows"))
            tri, eye2 = const("tri_neg"), const("eye2")
            tile(("mq", 2), xs_hi, xs_lo, "a")
            pe.wait_ge(*dve_step.at("gate_rows"))
            for t in range(2):
                mm = pe.matmul(misc[:, 1, 32 + 8 * t:40 + 8 * t], gate_rows[:, t * P:(t + 1) * P], ident[0:8, 0:8],
                               start=True, stop=True)
            mm.then_inc(*pe_step.inc("gates"))
            spread("final", TT2)
            spread("a", TT2, "final", 2)
            tile(("mq", 3), xs_hi, xs_lo, "a")
            tile(("mk", 0), xs_hi, xs_lo, "a")
            tile(("mk", 1), xs_hi, xs_lo, "a")
            pe.wait_ge(*dve_step.at("lf"))
            pe.matmul(misc[:, 1, 16:20], tri[:, 0:P], lf[:, 0, :], start=True, stop=True)
            pe.matmul(misc[:, 1, 20:24], tri[:, P:2 * P], lf[:, 0, :], start=True, stop=False)
            pe.matmul(misc[:, 1, 20:24], tri[:, 3 * P:4 * P], lf[:, 1, :], start=False, stop=True)
            for t in range(2):
                pe.matmul(misc[0:M_HEADS, 0, 0:SEQ], lf[:, t, :], tri[:, t * SEQ:(t + 1) * SEQ], start=(t == 0), stop=False)
            for t in range(2):
                mm = pe.matmul(misc[0:M_HEADS, 0, 0:SEQ], g8[:, t, 0:4], eye2[:, t * SEQ:(t + 1) * SEQ], start=False,
                               stop=(t == 1))
            mm.then_inc(*pe_step.inc("a_row"))
            tile(("mk", 2), xs_hi, xs_lo, "a")
            tile(("mk", 3), xs_hi, xs_lo, "a")
            top = cmax[:, 0, P:P + SEQ]

            def running_maximum(c):
                if c == 1:
                    pe.wait_ge(*dve_step.at("cmax"))
                    for t in range(2):
                        mm = pe.matmul(misc[:, 1, 24 + 4 * t:28 + 4 * t], top[:, t * P:(t + 1) * P],
                                       ident[0:M_HEADS, 0:M_HEADS], start=True, stop=True)
                    mm.then_inc(*pe_step.inc("m_tok"))

            row_tiles([("mv", t, s) for t in range(2) for s in range(2)], xs_hi, xs_lo, "a", TT2, 512, 2, running_maximum)
            a4, _ = CONSTS["sel4"]
            pe.wait_ge(*dve_evac.at(("mk", 3)))
            for s in range(2 * M_HEADS):
                hd = s // 2
                if s % 2 == 0:
                    tile(("mo", hd), xs_hi, xs_lo, "a")
                    if hd:
                        pe.wait_ge(*dve_step.at(("d1", hd - 1)))
                    pe.matmul(misc[:, 2, 0:SEQ], cst[0:M_HEADS, a4 + hd * P:a4 + (hd + 1) * P], top, start=True,
                              stop=True).then_inc(*pe_step.inc(("mb", hd)))
                    if hd:
                        pe.wait_ge(*dve_step.at(("sd", hd - 1)))
                    pe.matmul(misc[:, 0, 0:SEQ], qk2[:, 4 + hd, 0:P], qk2[:, hd, :], start=True, stop=True)
                    pe.matmul(misc[:, 0, SEQ:384], qk2[:, 4 + hd, P:SEQ], qk2[:, hd, P:SEQ], start=True,
                              stop=True).then_inc(*pe_step.inc(("mst", hd)))
                else:
                    pe.wait_ge(*dve_step.at(("sd", hd)))
                    if hd:
                        pe.wait_ge(*act_step.at(("num", hd - 1)))
                    for j in range(2):
                        c0 = hd * SEQ + j * P
                        pe.matmul(misc[:, 3, j * SEQ:(j + 1) * SEQ], v2[:, 0, c0:c0 + P], dmat[:, hd, 0:SEQ],
                                  start=True, stop=False)
                        mm = pe.matmul(misc[:, 3, j * SEQ + P:(j + 1) * SEQ], v2[:, 1, c0:c0 + P],
                                       dmat[:, hd, SEQ:384], start=False, stop=True)
                    mm.then_inc(*pe_step.inc(("num", hd)))
                    one = const("ones")[:, 0:1]
                    pe.matmul(misc[:, 1, hd:hd + 1], dmat[:, hd, 0:P], one, start=True, stop=True)
                    pe.matmul(misc[:, 1, 4 + hd:5 + hd], dmat[:, hd, P:SEQ], one, start=True, stop=False)
                    pe.matmul(misc[:, 1, 4 + hd:5 + hd], dmat[:, hd, SEQ:384], one, start=False, stop=True)
            tile(("mo", 4), xs_hi, xs_lo, "a")
            for hd in range(M_HEADS):
                pe.wait_ge(*dve_step.at(("nsq", hd)))
                for t in range(2):
                    for j in range(2):
                        mm = pe.matmul(misc[:, 1, 8 + 4 * t + hd:9 + 4 * t + hd], xt[:, 2 * hd + j, t * P:(t + 1) * P],
                                       one, start=(j == 0), stop=(j == 1))
            mm.then_inc(*pe_step.inc("nss"))
            for m in (5, 6, 7):
                tile(("mo", m), xs_hi, xs_lo, "a")
            pe.wait_ge(*dve_step.at("fac"))
            for hd in range(M_HEADS):
                if hd >= 2:
                    pe.wait_ge(*dve_step.at(("hn", 2 * hd - 3)))
                b = (2, 0)[hd % 2]
                for t in range(2):
                    mm = pe.matmul(misc[:, b, t * P:(t + 1) * P], fac[:, 4 * t + hd:4 * t + hd + 1].to_broadcast([P, P]),
                                   ident, start=True, stop=True)
                mm.then_inc(*pe_step.inc(("fb", hd)))
            for m in range(DT):
                tile(("mout", m), ys_hi, ys_lo, "mlstm")

            def ffn(l):
                for j in range(FFT):
                    tile(("uv", l, j), *pair[l], ("f", l))
                    if j == 0:
                        stats(("f", l), TT2)
                    tile(("ug", l, j), *pair[l], ("f", l))
                    if j == 0:
                        spread(("f", l), TT2)
                for m in range(DT):
                    tile(("down", l, m), a_hi, a_lo, ("act", l))

            ffn(0)

            r2 = cst[0:ROT, CONSTS["rot2"][0]:CONSTS["rot2"][0] + ROT]

            def head_stats(g, c, name):
                pe.wait_ge(*dve_step.at(("sq2", g)))
                for t in range(2):
                    mm = pe.matmul(misc[:, 3, c[t]:c[t] + 1], xt[:, g % 8, t * P:(t + 1) * P], one,
                                   start=True, stop=True)
                mm.then_inc(*pe_step.inc(("st2", g)))

            def head_rope(g, o):
                pe.matmul(o[0:ROT, 0:SEQ], r2, qk2[0:ROT, g, :], start=True, stop=True)
                for t in range(2):
                    c = 8 * t + g if g < 8 else 16 + 8 * t + g - 8
                    mm = pe.matmul(o[:, SEQ + t * P:SEQ + (t + 1) * P], rstd[:, c:c + 1].to_broadcast([P, P]), ident,
                                   start=True, stop=True)
                return mm

            def key_ropes(c):
                if 3 <= c <= 6:
                    for g in (2 * c - 6, 2 * c - 5):
                        pe.wait_ge(*rstd_ready.at("k2"))
                        pe.wait_ge(*dve_step.at("xk"))
                        if g >= 2:
                            pe.wait_ge(*dve_step.at(("rope2", g - 2)))
                        head_rope(g, misc[:, g % 2, :]).then_inc(*pe_step.inc(("rope2", g)))

            def query_rope(hd):
                acc_free(("rope", hd))
                pe.wait_ge(*rstd_ready.at(("q2", hd // 2)))
                pe.wait_ge(*dve_step.at(("xq", hd // 2)))
                head_rope(8 + hd, bank(("rope", hd))).then_inc(*tile_done.inc(("rope", hd)))

            def scores2(u):
                hd, t = units2[u]
                n = 2 * len(units) + u
                if u >= 2:
                    pe.wait_ge(*exp_ready.at(n - 2))
                if u == 0:
                    pe.wait_ge(*dve_step.at(("rope2", 7)))
                if t == 0:
                    pe.wait_ge(*dve_evac.at(("rope", hd)))
                keys = (t + 1) * P
                o = misc[:, u % 2, 0:keys]
                pe.matmul(o, qk2[:, 8 + hd, t * P:(t + 1) * P], qk2[:, hd, 0:keys], start=True, stop=False)
                pe.matmul(o[:, t * P:keys], ident, const("causal"), start=False,
                          stop=True).then_inc(*scores_done.inc(n))

            def turn2(u):
                n = 2 * len(units) + u
                pe.wait_ge(*probs_ready.at(n))
                if u >= 1:
                    pe.wait_ge(*turned_copied.at(n - 1))
                for k in range(units2[u][1] + 1):
                    mm = pe.matmul(misc[:, 2, k * P:(k + 1) * P], probs2[:, u % 2, k * P:(k + 1) * P], ident,
                                   start=True, stop=True)
                mm.then_inc(*turned.inc(n))

            def mix2(u):
                hd, t = units2[u]
                n = 2 * len(units) + u
                pe.wait_ge(*turned_copied.at(n))
                acc_free(("mx2", u))
                for k in range(t + 1):
                    mm = pe.matmul(bank(("mx2", u))[:, 0:P], v2[:, k, hd * P:(hd + 1) * P],
                                   pt2[:, u % 2, k * P:(k + 1) * P], start=(k == 0), stop=(k == t))
                mm.then_inc(*tile_done.inc(("mx2", u)))

            for m in range(DT):
                tile(("kk", m), xs_hi, xs_lo, "kv")
                if m == 0:
                    stats("kv", TT2)
                elif m == 1:
                    pe.wait_ge(*var_ready.at("kv"))
                if m >= 1:
                    head_stats(m - 1, (m - 1, 8 + m - 1), "k")
            head_stats(7, (7, 15), "k")
            row_tiles([("vv", t, c) for t in range(2) for c in range(2)], xs_hi, xs_lo, "kv", TT2, 512, 2, key_ropes)
            for m in range(DT):
                tile(("qq", m), ys_hi, ys_lo, "b")
                if m == 0:
                    pe.wait_ge(*var_ready.at("k2"))
                elif m % 2:
                    for g in (m - 1, m):
                        if m > 1:
                            pe.wait_ge(*var_ready.at(("q2", m // 2 - 1)))
                        head_stats(8 + g, (16 + g, 24 + g), "q")
                for hd in rope_at(m):
                    query_rope(hd)
                for u in attention_steps(m):
                    for hd in rope_at(step=u):
                        query_rope(hd)
                    if u < UNITS2:
                        scores2(u)
                    if 1 <= u <= UNITS2:
                        turn2(u - 1)
                    if u >= 2:
                        mix2(u - 2)
            for m in range(DT):
                tile(("aout", m), xs_hi, xs_lo, "attn")
            ffn(1)

        @block.scalar
        def _(act):
            at = {"next": 0}

            def split(upto):
                for c in range(at["next"], min(upto + 1, n_chunks)):
                    act.wait_ge(*raw_landed[c % RAW_SLOTS].at(c))
                    if c >= PART_SLOTS:
                        chunk_free(act, c - PART_SLOTS)
                    nc.scalar.activation(w_hi[:, c % PART_SLOTS, :], raw[:, c % RAW_SLOTS, :],
                                         ACT.Copy).then_inc(*hi_ready.inc(c))
                    at["next"] = c + 1

            def done(name):
                split(last_chunk[name] + PART_SLOTS - 1)
                act.wait_ge(*tile_done.at(name))

            def upper(key, dst, cols):
                for m in range(DT):
                    act.wait_ge(*x_ready.at((key, m)))
                    nc.scalar.activation(dst[:, m, 0:cols], xt[:, m, 0:cols], ACT.Copy).then_inc(*xhi_ready.inc((key, m)))

            def input_parts(m, cols, key, gain, dst, sq_key=None):
                nc.scalar.activation(dst[:, m, 0:cols], h[:, m, 0:cols], ACT.Copy, scale=gain).then_inc(*xhi_ready.inc((key, m)))
                if sq_key:
                    nc.scalar.activation(xt[:, m, 0:cols], h[:, m, 0:cols], ACT.Square).then_inc(*sq_ready.inc((sq_key, m)))

            act.wait_ge(*inputs_loaded.at("vec"))
            a, n = VECS["w_gates"]
            nc.scalar.activation(gw_hi[:, :], vec[:, a:a + n], ACT.Copy).then_inc(*act_step.inc("gw_hi"))
            act.wait_ge(*h_loaded.at("h0"))
            for m in range(DT):
                if m == 4:
                    act.wait_ge(*h2_loaded.at("h4"))
                input_parts(m, L1, ("x", 0), v("norm_g", m), xs_hi)
                if m == 3:
                    split(0)
            split(1)
            for m in range(DT):
                nc.scalar.activation(xt[:, m, :], h[:, m, :], ACT.Square).then_inc(*sq_ready.inc((("x", 0), m)))
                if m == 3:
                    split(2)
            for i in range(LAYERS):
                xp, op = pair[i % 2], pair[1 - i % 2]
                for j, name in enumerate([("ka", i)] + [("qa", i, m) for m in range(4)]):
                    done(name)
                    nc.scalar.activation(rq[:, j, :], bank(name)[:, 0:L1], ACT.Copy).then_inc(*act_evac.inc(name))
                for kind in ("qb", "kb"):
                    for m in range(4):
                        split(last_chunk[(kind, i, m)] + PART_SLOTS - 1)
                act.wait_ge(*dve_step.at(("meta_x", i)))
                nc.scalar.activation(pm[:, :], pm[:, :], ACT.Exp).then_inc(*act_step.inc(("meta_e", i)))

                def exp(u):
                    n = len(units) * i + u
                    q = P if units[u][0] == "na" else units[u][3]
                    act.wait_ge(*max_ready.at(n))
                    if u >= 2:
                        act.wait_ge(*turned.at(n - 2))
                    nc.scalar.activation(probs[0:q, u % 2, :], misc[0:q, u % 2, 0:L1], ACT.Exp, bias=nmax[0:q, u % 2:u % 2 + 1],
                                         accum_out=rsum[0:q, u % 2:u % 2 + 1]).then_inc(*exp_ready.inc(n))

                def turn(u):
                    n = len(units) * i + u
                    q = P if units[u][0] == "na" else units[u][3]
                    act.wait_ge(*turned.at(n))
                    if u >= 2:
                        act.wait_ge(*tile_done.at(("mx", i, u - 2)))
                    pv = pt[:, u % 2, 0:SEQ].rearrange("p (t q) -> p t q", t=2)[:, :, 0:q]
                    nc.scalar.activation(pv, misc[:, 2, 0:SEQ].rearrange("p (t q) -> p t q", t=2)[:, :, 0:q], ACT.Copy)
                    nc.scalar.activation(pt[0:META, u % 2, SEQ:SEQ + q], misc[0:META, 2, SEQ:SEQ + q],
                                         ACT.Copy).then_inc(*turned_copied.inc(n))

                def mixed(u):
                    n = len(units) * i + u
                    act.wait_ge(*tile_done.at(("mx", i, u)))
                    if units[u][0] == "na":
                        _, hd, a = units[u]
                        half, q = hd % 2, P
                        dst = o_raw[HD * half:HD * half + HD, 4 + hd // 2, a * P:(a + 1) * P]
                    else:
                        _, half, c0, q = units[u]
                        dst = o_raw[HD * half:HD * half + HD, 0:4, :].rearrange("p j t -> p (j t)")[:, c0:c0 + q]
                    nc.scalar.activation(dst, bank(("mx", i, u))[HD * half:HD * half + HD, 0:q],
                                         ACT.Copy).then_inc(*act_evac.inc(("mx", i, u)))

                def gated_upper(m):
                    act.wait_ge(*x_ready.at((("o", i), m)))
                    nc.scalar.activation(op[0][:, m, :], xt[:, m, :], ACT.Copy).then_inc(*xhi_ready.inc((("o", i), m)))

                split(last_chunk[("vb", i, 2)] + PART_SLOTS - 1)
                for u in range(len(units) + 2):
                    if u < len(units):
                        exp(u)
                    for kind, m in filler(u):
                        split(last_chunk[(kind, i, m)] + PART_SLOTS - 1)
                    if u == 0:
                        act.wait_ge(*pe_step.at(("meta_o", i)))
                        nc.scalar.activation(o_raw[:, 4:8, SEQ:L1], misc[:, 3, 0:4 * META].rearrange("p (j t) -> p j t", j=4),
                                             ACT.Copy).then_inc(*act_step.inc(("meta_o", i)))
                    if 1 <= u <= len(units):
                        turn(u - 1)
                    if u >= 2:
                        mixed(u - 2)
                    for kind, m in filler(u - 1):
                        if kind == "gate":
                            act.wait_ge(*dve_evac.at((kind, i, m)))
                            if 2 <= m < DT:
                                act.wait_ge(*dve_step.at(("zg", i, m - 2)))
                            nc.scalar.activation(z_tanh[:, m % 2, :] if m < DT else gates[:, m, :], gates[:, m, :], ACT.Tanh,
                                                 scale=0.5).then_inc(*act_step.inc(("tanh", i, m)))
                    for m in gated_at(u):
                        gated_upper(m)
                gated_upper(3)
                for m in range(DT):
                    split(last_chunk[("ya", i, m)] + PART_SLOTS - 1)
                    act.wait_ge(*x_ready.at((("mix", i), m)))
                    nc.scalar.activation(xp[0][:, m, :], xt[:, m, :], ACT.Copy).then_inc(*xhi_ready.inc((("mix", i), m)))
                for m in range(DT):
                    split(last_chunk[("out", i, m)] + PART_SLOTS - 1)
                    act.wait_ge(*dve_evac.at(("out", i, m)))
                    act.wait_ge(*xlo_ready.at((("mix", i), m)))
                    if i == LAYERS - 1:
                        act.wait_ge(*dve_step.at("fga"))
                        input_parts(m, SEQ, "a", fga[:, m:m + 1], op[0], "final")
                        nc.scalar.activation(num[:, m, :], h[:, m, 0:SEQ], ACT.Square,
                                             scale=v("final_g", m)).then_inc(*sq_ready.inc(("a", m)))
                    else:
                        input_parts(m, L1, ("x", i + 1), v("norm_g", 8 * (i + 1) + m), op[0], ("x", i + 1))
            split(last_chunk[("mq", 1)] + PART_SLOTS - 1)
            act.wait_ge(*dve_step.at("ab"))
            nc.scalar.activation(ln1[:], ab[:], ACT.Exp, scale=-1.0).then_inc(*act_step.inc("e1"))
            act.wait_ge(*act_step.at("e1"))
            nc.scalar.activation(ln1[:], ln1[:], ACT.Ln, bias=1.0).then_inc(*act_step.inc("ln1"))
            split(last_chunk[("mk", 3)] + PART_SLOTS - 1)
            split(last_chunk[("mv", 0, 0)] - CH + PART_SLOTS)
            act.wait_ge(*dve_step.at("fm"))
            nc.scalar.activation(floor[:], floor[:], ACT.Exp).then_inc(*act_step.inc("floor"))
            split(last_chunk[("mv", 1, 1)] + PART_SLOTS - 1)
            for s in range(2 * M_HEADS):
                hd = s // 2
                split(last_chunk[("mo", hd)] + PART_SLOTS - 1)
                if s % 2 == 0:
                    act.wait_ge(*dve_step.at(("d1", hd)))
                    nc.scalar.activation(dmat[:, hd, 0:SEQ], dmat[:, hd, 0:SEQ], ACT.Exp, bias=a_tok[:, 0, hd:hd + 1])
                    nc.scalar.activation(dmat[:, hd, SEQ:384], dmat[:, hd, SEQ:384], ACT.Exp,
                                         bias=a_tok[:, 1, hd:hd + 1]).then_inc(*act_step.inc(("dexp", hd)))
                else:
                    act.wait_ge(*pe_step.at(("num", hd)))
                    nc.scalar.activation(num[:, 2 * hd:2 * hd + 2, :], misc[:, 3, :].rearrange("p (j t) -> p j t", j=2),
                                         ACT.Copy).then_inc(*act_step.inc(("num", hd)))
            for m in range(DT):
                split(last_chunk[("mo", m)] + PART_SLOTS - 1)
                act.wait_ge(*dve_evac.at(("mo", m)))
                nc.scalar.activation(og[:, m, :], og[:, m, :], ACT.Sigmoid).then_inc(*act_step.inc(("so", m)))
            upper("mlstm", ys_hi, SEQ)

            def residual(kind, before, sq_key, inputs):
                for m in range(DT):
                    split(last_chunk[kind + (m,)] + PART_SLOTS - 1)
                    act.wait_ge(*dve_evac.at(kind + (m,)))
                    if before is not None:
                        act.wait_ge(*xlo_ready.at((before, m)))
                    for key, gain, at, dst in inputs:
                        input_parts(m, SEQ, key, v(gain, at + m), dst, sq_key if key == sq_key else None)

            def ffn(l):
                for j in range(FFT + 2):
                    for c, (kind, dst) in enumerate((("uv", cv), ("ug", cg))):
                        if j < FFT:
                            split(last_chunk[(kind, l, j)] + PART_SLOTS - 1)
                        if 1 <= j <= FFT:
                            k = j - 1
                            act.wait_ge(*dve_evac.at((kind, l, k)))
                            if k >= 2:
                                act.wait_ge(*xlo_ready.at((("act", l), k - 2)))
                            w = v("conv_w", ((l * 3 + 2) * 2 + c) * FFT + k)
                            b = v("conv_b", (l * 2 + c) * FFT + k)
                            nc.scalar.activation(dst[:, k % 2, :], up[:, k % 2, c, :], ACT.Identity, bias=b,
                                                 scale=w).then_inc(*act_step.inc((kind, l, k)))
                    if j >= 2:
                        k = j - 2
                        act.wait_ge(*dve_step.at(("conv", "ug", l, k)))
                        nc.scalar.activation(cg[:, k % 2, :], cg[:, k % 2, :], ACT.Silu).then_inc(*act_step.inc(("sg", l, k)))
                        act.wait_ge(*pool_step.at(("prod", l, k)))
                        nc.scalar.activation(a_hi[:, k, :], cv[:, k % 2, :], ACT.Copy).then_inc(*xhi_ready.inc((("act", l), k)))
                if l == 0:
                    residual(("down", 0), None, "kv", (("kv", "kv_norm", 0, xs_hi), ("b", "b_norm", 0, ys_hi)))
                else:
                    for m in range(DT):
                        split(last_chunk[("down", 1, m)] + PART_SLOTS - 1)

            residual(("mout",), "mlstm", ("f", 0), ((("f", 0), "f_norm", 0, xs_hi),))
            ffn(0)

            def raw_head(kind, base, m):
                done((kind, m))
                nc.scalar.activation(qk2[:, base + m, :], bank((kind, m))[:, 0:SEQ],
                                     ACT.Copy).then_inc(*act_evac.inc((kind, m)))

            for m in range(DT):
                raw_head("kk", 0, m)
            split(last_chunk[("vv", 1, 1)] + PART_SLOTS - 1)

            def upper2(u):
                hd, t = units2[u]
                act.wait_ge(*tile_done.at(("mx2", u)))
                nc.scalar.activation(xs_hi[:, hd, t * P:(t + 1) * P], bank(("mx2", u))[:, 0:P],
                                     ACT.Copy).then_inc(*xhi_ready.inc(("attn", u)))

            for m in range(DT):
                raw_head("qq", 8, m)
                for u in attention_steps(m):
                    n = 2 * len(units) + u
                    if u < UNITS2:
                        keys = (units2[u][1] + 1) * P
                        act.wait_ge(*max_ready.at(n))
                        if u >= 2:
                            act.wait_ge(*turned.at(n - 2))
                        nc.scalar.activation(probs2[:, u % 2, 0:keys], misc[:, u % 2, 0:keys], ACT.Exp,
                                             bias=nmax[:, u % 2:u % 2 + 1],
                                             accum_out=rsum[:, u % 2:u % 2 + 1]).then_inc(*exp_ready.inc(n))
                    if 1 <= u <= UNITS2:
                        keys = (units2[u - 1][1] + 1) * P
                        act.wait_ge(*turned.at(n - 1))
                        if u >= 3:
                            act.wait_ge(*tile_done.at(("mx2", u - 3)))
                        nc.scalar.activation(pt2[:, (u - 1) % 2, 0:keys], misc[:, 2, 0:keys],
                                             ACT.Copy).then_inc(*turned_copied.inc(n - 1))
                    if u >= 2:
                        upper2(u - 2)
            residual(("aout",), None, ("f", 1), ((("f", 1), "f_norm", 8, ys_hi),))
            ffn(1)

        @block.vector
        def _(dve):
            at = {"next": 0}

            def split(upto):
                for c in range(at["next"], min(upto + 1, n_chunks)):
                    dve.wait_ge(*hi_ready.at(c))
                    nc.vector.tensor_tensor(w_lo[:, c % PART_SLOTS, :], raw[:, c % RAW_SLOTS, :],
                                            w_hi[:, c % PART_SLOTS, :].bitcast(F32),
                                            ALU.subtract).then_inc(*lo_ready.inc(c))
                    at["next"] = c + 1

            def done(name):
                split(last_chunk[name] + PART_SLOTS - 1)
                dve.wait_ge(*tile_done.at(name))

            def step(ins, key):
                ins.then_inc(*dve_step.inc(key))
                dve.wait_ge(*dve_step.at(key))

            def variance(key, tts):
                dve.wait_ge(*stats_done.at(key))
                if len(tts) == 3:
                    step(nc.vector.tensor_scalar(var[0:META, 2:3], misc[0:META, 3, 2:3], 1.0 / D, EPS, ALU.mult, ALU.add),
                         ("var", key))
                nc.vector.tensor_scalar(var[:, 0:2], misc[:, 3, 0:2], 1.0 / D, EPS, ALU.mult,
                                        ALU.add).then_inc(*var_ready.inc(key))
                dve.wait_ge(*var_ready.at(key))
                step(nc.vector.tensor_scalar(eps_var[:, 0:3], var[:, 0:3], EPS, None, ALU.mult), ("eps_var", key))

            def factors(key, n):
                dve.wait_ge(*bcast_done.at(key))
                step(nc.vector.tensor_copy(rb_sb[:, 0:n], misc[:, 2, 0:n]), ("rb_sb", key))

            def low_part(m, cols, key, gain, upper_, dst):
                dve.wait_ge(*xhi_ready.at((key, m)))
                nc.vector.scalar_tensor_tensor(dst[:, m, 0:cols], h[:, m, 0:cols], gain, upper_[:, m, 0:cols].bitcast(F32),
                                               ALU.mult, ALU.subtract).then_inc(*xlo_ready_dve.inc((key, m)))

            nc.vector.memset(mhalf[:], -0.5)
            nc.vector.memset(var[:], 1.0)
            nc.vector.memset(rstd[:], 1.0)
            nc.vector.memset(rtok[:], 1.0).then_inc(*dve_step.inc("mhalf"))
            dve.wait_ge(*inputs_loaded.at("vec"))
            for i in range(LAYERS):
                nc.vector.tensor_scalar(qscale[:, i:i + 1], v("qg", i), HD ** -0.5, None,
                                        ALU.mult).then_inc(*dve_step.inc(("qscale", i)))
            nc.vector.tensor_scalar(qscale[:, 2:3], v("b_q_norm"), P ** -0.5, None, ALU.mult).then_inc(*dve_step.inc("qscale2"))
            nc.vector.tensor_tensor(fga[:, :], v("final_g", 0, DT), v("a_norm", 0, DT), ALU.mult).then_inc(*dve_step.inc("fga"))
            dve.wait_ge(*act_step.at("gw_hi"))
            a, n = VECS["w_gates"]
            nc.vector.tensor_tensor(gw_lo[:, :], vec[:, a:a + n], gw_hi[:, :].bitcast(F32),
                                    ALU.subtract).then_inc(*dve_step.inc("gw_lo"))
            for m in range(DT):
                low_part(m, L1, ("x", 0), v("norm_g", m), xs_hi, xs_lo)
                if m == 4:
                    split(0)
            split(1)
            for i in range(LAYERS):
                key = ("x", i)
                op = pair[1 - i % 2]
                split(last_chunk[("ka", i)] + PART_SLOTS - 1)
                for j, name in enumerate([("ka", i)] + [("qa", i, m) for m in range(4)]):
                    split(last_chunk[name] + PART_SLOTS - 1)
                    dve.wait_ge(*act_evac.at(name))
                    nc.vector.tensor_tensor(qf[:, j, :], rq[:, j, :], rq[:, j, :], ALU.mult).then_inc(*dve_step.inc(("qsq", i, j)))
                    if j == 1:
                        variance(key, TT1)
                    if j == 2:
                        factors(key, L1)
                nc.vector.tensor_scalar(xg[:, 0, :], rq[:, 0, :], v("kg", i), None, ALU.mult)
                nc.vector.tensor_scalar(xg[:, 1:5, :], rq[:, 1:5, :], qscale[:, i:i + 1], None,
                                        ALU.mult).then_inc(*dve_step.inc(("xg", i)))

                def head_tile(kind, m):
                    done((kind, i, m))
                    dst, scale = (qn, HD ** -0.5) if kind == "qb" else (kn, 1.0)
                    nc.vector.scalar_tensor_tensor(dst[:, m, :], bank((kind, i, m))[:, 0:L1], scale, rb_sb[:, 0:L1],
                                                   ALU.mult, ALU.mult).then_inc(*dve_evac.inc((kind, i, m)))

                def rope(j):
                    dve.wait_ge(*pe_step.at(("rot", i, j)))
                    step(nc.vector.tensor_tensor(t2[:, :], misc[:, j % 2, 0:L1], const("sin1"), ALU.mult), ("t2", i, j))
                    dve.wait_ge(*pool_step.at(("t1", i, j)))
                    step(nc.vector.tensor_tensor(t2[:, :], rq[:, j, :], t2[:, :], ALU.add), ("t3", i, j))
                    dve.wait_ge(*pe_step.at(("rb", i, j)))
                    step(nc.vector.tensor_tensor(qf[:, j, :], t2[:, :], misc[:, 2 + j % 2, 0:L1], ALU.mult), ("qf", i, j))

                head_tile("qb", 0)
                dve.wait_ge(*stats_done.at(("qk", i)))
                step(nc.vector.tensor_scalar(var[0:META, 20:30], misc[0:META, 3, 20:30], 1.0 / HD, eps_var[0:META, 2:3],
                                             ALU.mult, ALU.add), ("var", "qk", i))
                for t in range(2):
                    ins = nc.vector.tensor_scalar(var[:, 10 * t:10 * t + 10], misc[:, 3, 10 * t:10 * t + 10], 1.0 / HD,
                                                  eps_var[:, t:t + 1], ALU.mult, ALU.add)
                ins.then_inc(*var_ready.inc(("qk", i)))
                for m in range(1, 4):
                    head_tile("qb", m)
                head_tile("kb", 0)
                dve.wait_ge(*pe_step.at(("rt", i)))
                nc.vector.tensor_copy(rrow[:, :], misc[0:10, 3, 0:L1]).then_inc(*dve_step.inc(("rrow", i)))
                head_tile("kb", 1)
                if i == 0:
                    dve.wait_ge(*cst_loaded.at("cst"))
                rope(0)
                rope(1)
                head_tile("kb", 2)
                for j in range(2, 5):
                    rope(j)
                head_tile("kb", 3)
                dve.wait_ge(*pe_step.at(("meta_s", i)))
                s3 = misc[0:META, 0:2, 0:64].rearrange("p b (h k) -> p b h k", h=4)
                p3 = pm[:, :].rearrange("p (b h k) -> p b h k", b=2, h=4)
                m3, z3 = (ms[:, c:c + 8].rearrange("p (b h) -> p b h", b=2) for c in (0, 8))
                step(nc.vector.tensor_reduce(m3, s3, AX_X, ALU.max), ("meta_m", i))
                nc.vector.tensor_tensor(p3, s3, m3.unsqueeze(3).to_broadcast([META, 2, 4, META]),
                                        ALU.subtract).then_inc(*dve_step.inc(("meta_x", i)))
                for t in range(3):
                    done(("va", i, t))
                    tn = TT1[t][1]
                    nc.vector.tensor_scalar(v_sb[0:tn, t, 0:P], bank(("va", i, t))[0:tn, 0:P], rtok[0:tn, t:t + 1], None,
                                            ALU.mult).then_inc(*dve_evac.inc(("va", i, t)))
                dve.wait_ge(*act_step.at(("meta_e", i)))
                step(nc.vector.tensor_reduce(z3, p3, AX_X, ALU.add), ("meta_z", i))
                step(nc.vector.reciprocal(ms[:, 0:8], ms[:, 8:16]), ("meta_r", i))
                nc.vector.tensor_tensor(p3, p3, m3.unsqueeze(3).to_broadcast([META, 2, 4, META]),
                                        ALU.mult).then_inc(*dve_step.inc(("meta_p", i)))
                for t in range(3):
                    done(("vb", i, t))
                    tn = TT1[t][1]
                    nc.vector.tensor_scalar(v_sb[0:tn, t, P:VCOLS], bank(("vb", i, t))[0:tn, :], rtok[0:tn, t:t + 1], None,
                                            ALU.mult).then_inc(*dve_evac.inc(("vb", i, t)))
                dve.wait_ge(*pe_step.at(("meta_t", i)))
                nc.vector.tensor_copy(pmt[:, :], misc[0:META, 2, 0:128]).then_inc(*dve_step.inc(("meta_pt", i)))

                def gated(m):
                    dve.wait_ge(*dve_step.at(("zg", i, m)))
                    dve.wait_ge(*act_step.at(("meta_o", i)))
                    dve.wait_ge(*act_evac.at(("mx", i, 4 * (m - 4) + 3 if m >= 4 else ga0 + 2 * ((L1 * (m + 1) - 1) // P) + 1)))
                    nc.vector.scalar_tensor_tensor(xt[:, m, :], o_raw[:, m, :], 0.25, gates[:, m, :], ALU.mult,
                                                   ALU.mult).then_inc(*x_ready.inc((("o", i), m)))

                def y_tile(kind, at_, m):
                    dve.wait_ge(*act_step.at(("tanh", i, at_ + m)))
                    dve.wait_ge(*tile_done.at((kind, i, m)))
                    nc.vector.scalar_tensor_tensor(gates[:, at_ + m, :], gates[:, at_ + m, :], 1.0,
                                                   bank((kind, i, m))[:, 0:L1], ALU.add,
                                                   ALU.mult).then_inc(*dve_evac.inc((kind, i, m)))

                for u in range(len(units) + 2):
                    if u < len(units):
                        n = len(units) * i + u
                        q = P if units[u][0] == "na" else units[u][3]
                        b = u % 2
                        dve.wait_ge(*scores_done.at(n))
                        nc.vector.tensor_reduce(nmax[0:q, b:b + 1], misc[0:q, b, 0:L1], AX_X, ALU.max,
                                                negate=True).then_inc(*max_ready.inc(n))
                    for kind, m in filler(u):
                        split(last_chunk[(kind, i, m)] + PART_SLOTS - 1)
                    if u < len(units):
                        dve.wait_ge(*exp_ready.at(n))
                        step(nc.vector.reciprocal(rinv[0:q, b:b + 1], rsum[0:q, b:b + 1]), ("rinv", n))
                        nc.vector.tensor_scalar(probs[0:q, b, :], probs[0:q, b, :], rinv[0:q, b:b + 1], None,
                                                ALU.mult).then_inc(*probs_ready.inc(n))
                    for kind, m in filler(u):
                        if kind == "gate":
                            done((kind, i, m))
                            nc.vector.tensor_tensor(gates[:, m, :], bank((kind, i, m))[:, 0:L1], rb_sb[:, 0:L1],
                                                    ALU.mult).then_inc(*dve_evac.inc((kind, i, m)))
                        else:
                            y_tile(kind, 16, m)
                    for kind, m in filler(u - 1):
                        if kind == "gate" and m < DT:
                            dve.wait_ge(*act_step.at(("tanh", i, m)))
                            nc.vector.scalar_tensor_tensor(gates[:, m, :], z_tanh[:, m % 2, :], 1.0, gates[:, m, :], ALU.add,
                                                           ALU.mult).then_inc(*dve_step.inc(("zg", i, m)))
                    for m in gated_at(u):
                        gated(m)
                gated(3)
                split(last_chunk[("ya", i, 0)] + PART_SLOTS - 2)
                for m in range(DT):
                    y_tile("ya", 8, m)
                    dve.wait_ge(*dve_evac.at(("ya", i, m)))
                    dve.wait_ge(*xlo_ready.at((("o", i), m)))
                    nc.vector.tensor_tensor(xt[:, m, :], gates[:, 8 + m, :], gates[:, 16 + m, :],
                                            ALU.add).then_inc(*x_ready.inc((("mix", i), m)))
                    if m % 2:
                        split(last_chunk[("ya", i, m)] + PART_SLOTS - 1)
                for m in range(DT):
                    dve.wait_ge(*tile_done.at(("out", i, m)))
                    nc.vector.tensor_tensor(h[:, m, :], h[:, m, :], bank(("out", i, m))[:, 0:L1],
                                            ALU.add).then_inc(*dve_evac.inc(("out", i, m)))
                    if m < DT - 1:
                        split(last_chunk[("out", i, m)] + PART_SLOTS - 1)
                    if i < LAYERS - 1:
                        low_part(m, L1, ("x", i + 1), v("norm_g", 8 * (i + 1) + m), *op)
                    else:
                        low_part(m, SEQ, "a", fga[:, m:m + 1], *op)
                split(last_chunk[("out", i, DT - 1)] + PART_SLOTS - 1)
            dve.wait_ge(*stats_done.at("a"))
            step(nc.vector.tensor_scalar(var[:, 0:2], misc[:, 3, 0:2], 1.0 / D, EPS, ALU.mult, ALU.add), "var1")
            step(nc.vector.tensor_scalar(eps_var[:, 0:2], var[:, 0:2], EPS, None, ALU.mult), "eps_var1")
            for t in range(2):
                ins = nc.vector.tensor_scalar(var[:, 2 + t:3 + t], misc[:, 3, 4 + t:5 + t], 1.0 / D, eps_var[:, t:t + 1],
                                              ALU.mult, ALU.add)
            ins.then_inc(*var_ready.inc("final"))

            split(last_chunk[("mq", 1)] + PART_SLOTS - 1)
            dve.wait_ge(*pe_step.at("gate_rows"))
            nc.vector.tensor_copy(gate_rows[:], misc[0:8, 0, 0:SEQ]).then_inc(*dve_step.inc("gate_rows"))
            dve.wait_ge(*rstd_ready.at("final"))
            dve.wait_ge(*pe_step.at("gates"))
            for t in range(2):
                step(nc.vector.scalar_tensor_tensor(g8[:, t, :], misc[:, 1, 32 + 8 * t:40 + 8 * t], rtok[:, 2 + t:3 + t],
                                                    v("b_gates", 0, 8), ALU.mult, ALU.add), ("g8", t))
            nc.vector.scalar_tensor_tensor(ab[:], g8[:, :, 4:8], -1.0, g8[:, :, 4:8], ALU.mult, ALU.max).then_inc(*dve_step.inc("ab"))
            nc.vector.memset(cmax[:], 0.0).then_inc(*dve_step.inc("cmax0"))
            dve.wait_ge(*act_step.at("ln1"))
            nc.vector.scalar_tensor_tensor(lf[:], g8[:, :, 4:8], 0.0, ln1[:], ALU.min,
                                           ALU.subtract).then_inc(*dve_step.inc("lf"))
            factors("a", 2 * SEQ)
            rb12 = rb_sb[:, SEQ:2 * SEQ]
            for m in range(4):
                done(("mq", m))
                nc.vector.scalar_tensor_tensor(qk2[:, m, :], bank(("mq", m))[:, 0:SEQ], P ** -0.5, rb12, ALU.mult,
                                               ALU.mult).then_inc(*dve_evac.inc(("mq", m)))

            def key_tile(m):
                done(("mk", m))
                nc.vector.tensor_tensor(qk2[:, 4 + m, :], bank(("mk", m))[:, 0:SEQ], rb12,
                                        ALU.mult).then_inc(*dve_evac.inc(("mk", m)))

            key_tile(0)
            key_tile(1)
            dve.wait_ge(*pe_step.at("a_row"))
            step(nc.vector.tensor_copy(nf[:], misc[:, 1, 16:24].rearrange("p (t g) -> p t g", t=2)), "nf")
            nc.vector.tensor_tensor(a_tok[:], g8[:, :, 0:4], nf[:], ALU.add).then_inc(*dve_step.inc("a_tok"))
            step(nc.vector.tensor_scalar(cmax[:, 0, P:], misc[0:M_HEADS, 0, 0:SEQ], 0.0, None, ALU.max), "m0")
            b = 0
            for r in range(8):
                d = 1 << r
                step(nc.vector.tensor_tensor(cmax[:, 1 - b, P:], cmax[:, b, P:], cmax[:, b, P - d:P + SEQ - d], ALU.max),
                     ("m", r) if r < 7 else "cmax")
                b = 1 - b
            key_tile(2)
            key_tile(3)
            dve.wait_ge(*pe_step.at("m_tok"))
            nc.vector.tensor_tensor(floor[:], nf[:], misc[:, 1, 24:32].rearrange("p (t g) -> p t g", t=2),
                                    ALU.subtract).then_inc(*dve_step.inc("fm"))
            dve.wait_ge(*xlo_ready_dve.at(("a", 7)))
            first_v = last_chunk[("mv", 0, 0)] - CH + 1
            for m in range(DT):
                nc.vector.scalar_tensor_tensor(h[:, m, 0:SEQ], h[:, m, 0:SEQ], v("final_g", m), rb_sb[:, 0:SEQ], ALU.mult,
                                               ALU.mult).then_inc(*dve_step.inc(("final", m)))
                split(first_v + m)
            for t in range(2):
                for s in range(2):
                    done(("mv", t, s))
                    nc.vector.tensor_scalar(v2[:, t, 512 * s:512 * s + 512], bank(("mv", t, s)), rtok[:, 2 + t:3 + t], None,
                                            ALU.mult).then_inc(*dve_evac.inc(("mv", t, s)))
            ct = const("causal_t")

            def o_tile(m):
                done(("mo", m))
                nc.vector.tensor_tensor(og[:, m, :], bank(("mo", m))[:, 0:SEQ], rb12, ALU.mult).then_inc(*dve_evac.inc(("mo", m)))

            for s in range(2 * M_HEADS):
                hd = s // 2
                if s % 2 == 0:
                    o_tile(hd)
                    dve.wait_ge(*pe_step.at(("mb", hd)))
                    nc.vector.scalar_tensor_tensor(dmat[:, hd, 0:SEQ], misc[:, 2, 0:SEQ], -1.0, ct, ALU.mult, ALU.add)
                    nc.vector.scalar_tensor_tensor(dmat[:, hd, SEQ:384], misc[:, 2, P:SEQ], -1.0, ct[:, 0:P], ALU.mult,
                                                   ALU.add).then_inc(*dve_step.inc(("d1", hd)))
                    dve.wait_ge(*act_step.at(("dexp", hd)))
                    dve.wait_ge(*pe_step.at(("mst", hd)))
                    nc.vector.tensor_tensor(dmat[:, hd, :], dmat[:, hd, :], misc[:, 0, 0:384],
                                            ALU.mult).then_inc(*dve_step.inc(("sd", hd)))
                else:
                    dve.wait_ge(*act_step.at(("num", hd)))
                    nc.vector.tensor_tensor(xt[:, 2 * hd:2 * hd + 2, 0:SEQ], num[:, 2 * hd:2 * hd + 2, :],
                                            num[:, 2 * hd:2 * hd + 2, :], ALU.mult).then_inc(*dve_step.inc(("nsq", hd)))
            o_tile(4)
            dve.wait_ge(*pe_step.at("nss"))
            dve.wait_ge(*act_step.at("floor"))
            sums = misc[:, 1, 0:8].rearrange("p (t g) -> p t g", t=2)
            step(nc.vector.scalar_tensor_tensor(den[:], sums, -1.0, floor[:], ALU.mult, ALU.max), "-den")
            step(nc.vector.tensor_tensor(den[:], sums, den[:], ALU.max), "den")
            step(nc.vector.reciprocal(den[:], den[:]), "rden")
            f3 = fac[:, :].rearrange("p (t g) -> p t g", t=2)
            v3 = var[:, 0:8].rearrange("p (t g) -> p t g", t=2)
            step(nc.vector.tensor_tensor(f3, den[:], den[:], ALU.mult), "rden2")
            step(nc.vector.tensor_tensor(f3, f3, misc[:, 1, 8:16].rearrange("p (t g) -> p t g", t=2), ALU.mult), "nvar")
            nc.vector.tensor_scalar(v3, f3, 1.0 / 256, EPS, ALU.mult, ALU.add).then_inc(*var_ready.inc("mlstm"))
            o_tile(5)
            dve.wait_ge(*rstd_ready.at("mlstm"))
            nc.vector.tensor_tensor(f3, rstd[:, 0:8].rearrange("p (t g) -> p t g", t=2), den[:],
                                    ALU.mult).then_inc(*dve_step.inc("fac"))
            o_tile(6)
            o_tile(7)
            for m in range(DT):
                dve.wait_ge(*pe_step.at(("fb", m // 2)))
                step(nc.vector.scalar_tensor_tensor(num[:, m, :], num[:, m, :], v("a_h_norm", m),
                                                    misc[:, (2, 0)[m // 2 % 2], 0:SEQ], ALU.mult, ALU.mult), ("hn", m))
                dve.wait_ge(*act_step.at(("so", m)))
                nc.vector.tensor_tensor(xt[:, m, 0:SEQ], num[:, m, :], og[:, m, :], ALU.mult).then_inc(*x_ready.inc(("mlstm", m)))

            def residual(kind, inputs, before=None):
                for m in range(DT):
                    split(last_chunk[kind + (m,)] + PART_SLOTS - 2)
                    dve.wait_ge(*tile_done.at(kind + (m,)))
                    if before:
                        dve.wait_ge(*dve_step.at((before, m)))
                    nc.vector.tensor_tensor(h[:, m, 0:SEQ], h[:, m, 0:SEQ], bank(kind + (m,))[:, 0:SEQ],
                                            ALU.add).then_inc(*dve_evac.inc(kind + (m,)))
                    if m < DT - 1:
                        split(last_chunk[kind + (m,)] + PART_SLOTS - 1)
                    for key, gain, at_, (hi, lo) in inputs:
                        low_part(m, SEQ, key, v(gain, at_ + m), hi, lo)
                split(last_chunk[kind + (DT - 1,)] + PART_SLOTS - 1)

            def ffn(l):
                split(last_chunk[("uv", l, 0)] + PART_SLOTS - 1)
                variance(("f", l), TT2)
                factors(("f", l), SEQ)
                for j in range(FFT + 1):
                    for c, (kind, dst) in enumerate((("uv", cv), ("ug", cg))):
                        if j < FFT:
                            done((kind, l, j))
                            if j >= 2:
                                dve.wait_ge(*dve_step.at(("conv", kind, l, j - 2)))
                                dve.wait_ge(*act_step.at((kind, l, j - 2)))
                            nc.vector.tensor_tensor(up[:, j % 2, c, :], bank((kind, l, j))[:, 0:SEQ], rb_sb[:, 0:SEQ],
                                                    ALU.mult).then_inc(*dve_evac.inc((kind, l, j)))
                        if j >= 1:
                            k = j - 1
                            dve.wait_ge(*act_step.at((kind, l, k)))
                            u, y = up[:, k % 2, c, :], dst[:, k % 2, :]
                            w = [v("conv_w", ((l * 3 + s) * 2 + c) * FFT + k) for s in range(2)]
                            step(nc.vector.scalar_tensor_tensor(y[:, 1:SEQ], u[:, 0:SEQ - 1], w[1], y[:, 1:SEQ], ALU.mult,
                                                                ALU.add), ("conv1", kind, l, k))
                            nc.vector.scalar_tensor_tensor(y[:, 2:SEQ], u[:, 0:SEQ - 2], w[0], y[:, 2:SEQ], ALU.mult,
                                                           ALU.add).then_inc(*dve_step.inc(("conv", kind, l, k)))
                if l == 0:
                    residual(("down", 0), (("kv", "kv_norm", 0, pair[0]), ("b", "b_norm", 0, pair[1])))
                else:
                    residual(("down", 1), ())

            residual(("mout",), ((("f", 0), "f_norm", 0, pair[0]),), "final")
            ffn(0)
            split(last_chunk[("kk", 0)] + PART_SLOTS - 1)
            variance("kv", TT2)

            def head_squares(kind, g):
                name = (kind, g % 8)
                split(last_chunk[name] + PART_SLOTS - 1)
                dve.wait_ge(*act_evac.at(name))
                nc.vector.tensor_tensor(xt[:, g % 8, 0:SEQ], qk2[:, g, :], qk2[:, g, :], ALU.mult).then_inc(*dve_step.inc(("sq2", g)))

            def head_variance(c, n, key):
                for t in range(2):
                    a = c + 8 * t
                    ins = nc.vector.tensor_scalar(var[:, a:a + n], misc[:, 3, a:a + n], 1.0 / P, eps_var[:, t:t + 1], ALU.mult,
                                                  ALU.add)
                ins.then_inc(*var_ready.inc(key))

            def rope2(g, o):
                ta = rope_t[:, g % 2, 0:SEQ]
                step(nc.vector.tensor_tensor(ta, o[0:ROT, 0:SEQ], const("sin2", ROT), ALU.mult), ("ra", g))
                dve.wait_ge(*pool_step.at(("xc", g)))
                x2 = qk2[0:ROT, g, :]
                step(nc.vector.tensor_tensor(x2, ta, x_cos[:, g, :], ALU.add), ("rs", g))
                return nc.vector.tensor_tensor(qk2[:, g, :], qk2[:, g, :], o[:, SEQ:2 * SEQ], ALU.mult)

            for m in range(DT):
                head_squares("kk", m)
            dve.wait_ge(*rstd_ready.at("kv"))
            dve.wait_ge(*pe_step.at(("st2", 7)))
            head_variance(0, 8, "k2")
            dve.wait_ge(*dve_step.at(("sq2", 7)))
            nc.vector.tensor_scalar(qk2[:, 0:8, :], qk2[:, 0:8, :], v("k_norm"), None, ALU.mult).then_inc(*dve_step.inc("xk"))
            dve.wait_ge(*dve_step.at("xk"))
            first_v = last_chunk[("vv", 0, 0)] - CH + 1
            for c in range(3, 7):
                split(first_v + c + PART_SLOTS - 1)
                for g in (2 * c - 6, 2 * c - 5):
                    dve.wait_ge(*pe_step.at(("rope2", g)))
                    step(rope2(g, misc[:, g % 2, :]), ("rope2", g))
            for t in range(2):
                for s in range(2):
                    done(("vv", t, s))
                    nc.vector.tensor_scalar(v2[:, t, 512 * s:512 * s + 512], bank(("vv", t, s)), rtok[:, t:t + 1], None,
                                            ALU.mult).then_inc(*dve_evac.inc(("vv", t, s)))

            def query_rope(hd):
                dve.wait_ge(*tile_done.at(("rope", hd)))
                rope2(8 + hd, bank(("rope", hd))).then_inc(*dve_evac.inc(("rope", hd)))

            for m in range(DT):
                head_squares("qq", 8 + m)
                if m % 2:
                    p = m // 2
                    dve.wait_ge(*dve_step.at(("sq2", 8 + m)))
                    x2 = qk2[:, 8 + 2 * p:10 + 2 * p, :]
                    nc.vector.tensor_scalar(x2, x2, qscale[:, 2:3], None, ALU.mult).then_inc(*dve_step.inc(("xq", p)))
                    dve.wait_ge(*pe_step.at(("st2", 8 + m)))
                    head_variance(16 + 2 * p, 2, ("q2", p))
                for hd in rope_at(m):
                    query_rope(hd)
                for u in attention_steps(m):
                    for hd in rope_at(step=u):
                        query_rope(hd)
                    if u < UNITS2:
                        n = 2 * len(units) + u
                        keys = (units2[u][1] + 1) * P
                        b = u % 2
                        dve.wait_ge(*scores_done.at(n))
                        nc.vector.tensor_reduce(nmax[:, b:b + 1], misc[:, b, 0:keys], AX_X, ALU.max,
                                                negate=True).then_inc(*max_ready.inc(n))
                        dve.wait_ge(*exp_ready.at(n))
                        step(nc.vector.reciprocal(rinv[:, b:b + 1], rsum[:, b:b + 1]), ("rinv", n))
                        nc.vector.tensor_scalar(probs2[:, b, 0:keys], probs2[:, b, 0:keys], rinv[:, b:b + 1], None,
                                                ALU.mult).then_inc(*probs_ready.inc(n))
                    if u >= 2:
                        hd, t = units2[u - 2]
                        part = slice(t * P, (t + 1) * P)
                        dve.wait_ge(*xhi_ready.at(("attn", u - 2)))
                        nc.vector.tensor_tensor(xs_lo[:, hd, part], bank(("mx2", u - 2))[:, 0:P], xs_hi[:, hd, part].bitcast(F32),
                                                ALU.subtract).then_inc(*dve_evac.inc(("mx2", u - 2)))
            residual(("aout",), ((("f", 1), "f_norm", 8, pair[1]),))
            ffn(1)

        @block.gpsimd
        def _(pool):
            def root(key, dst, c0, c1):
                pool.wait_ge(*var_ready.at(key))
                nc.gpsimd.tensor_tensor(dst[:, c0:c1], var[:, c0:c1], mhalf[:, c0:c1], ALU.pow).then_inc(*rstd_ready.inc(key))

            def lower(key, dst, upper_, cols, order=range(DT)):
                for m in order:
                    pool.wait_ge(*xhi_ready.at((key, m)))
                    nc.gpsimd.tensor_tensor(dst[:, m, 0:cols], xt[:, m, 0:cols], upper_[:, m, 0:cols].bitcast(F32),
                                            ALU.subtract).then_inc(*xlo_ready.inc((key, m)))

            def add_square(key, m, cols, src=xt, n=0):
                pool.wait_ge(*sq_ready.at((key, m)))
                if m >= 2:
                    pool.wait_ge(*pool_step.at(("sum", key, m - 1)))
                if m >= 1:
                    o = (sq_sum, sq_sum2)[n][:, 0:cols]
                    nc.gpsimd.tensor_tensor(o, src[:, 0, 0:cols] if m == 1 else o, src[:, m, 0:cols],
                                            ALU.add).then_inc(*pool_step.inc(("sum", key, m)))

            pool.wait_ge(*dve_step.at("mhalf"))
            for m in range(DT):
                add_square(("x", 0), m, L1)
            for i in range(LAYERS):
                xp, op = pair[i % 2], pair[1 - i % 2]
                root(("x", i), rtok, 0, 3)
                root(("qk", i), rstd, 0, 30)
                if i == 0:
                    pool.wait_ge(*cst_loaded.at("cst"))
                pool.wait_ge(*dve_step.at(("xg", i)))
                for j in range(5):
                    nc.gpsimd.tensor_tensor(rq[:, j, :], xg[:, j, :], const("cos1"), ALU.mult).then_inc(*pool_step.inc(("t1", i, j)))
                pool.wait_ge(*bias_loaded.at((i, 1, NA_HEADS - 1)))
                b3 = bias[:, :, :].rearrange("p h (d j) -> p (h d) j", j=GRID_W)
                nc.gpsimd.tensor_tensor(b3, b3, const("window").unsqueeze(1).to_broadcast([P, 6 * NA_HEADS, GRID_W]),
                                        ALU.add).then_inc(*pool_step.inc(("bias", i)))
                lower(("o", i), op[1], op[0], L1, (4, 5, 6, 7, 0, 1, 2, 3))
                lower(("mix", i), xp[1], xp[0], L1)
                for m in range(DT):
                    if i < LAYERS - 1:
                        add_square(("x", i + 1), m, L1)
                    else:
                        add_square("final", m, SEQ)
                        add_square("a", m, SEQ, num, 1)
            root("final", rtok, 0, 4)
            root("mlstm", rstd, 0, 8)
            lower("mlstm", ys_lo, ys_hi, SEQ)

            def ffn(l):
                for m in range(DT):
                    add_square(("f", l), m, SEQ)
                root(("f", l), rtok, 0, 2)
                for j in range(FFT):
                    pool.wait_ge(*act_step.at(("sg", l, j)))
                    nc.gpsimd.tensor_tensor(cv[:, j % 2, :], cv[:, j % 2, :], cg[:, j % 2, :],
                                            ALU.mult).then_inc(*pool_step.inc(("prod", l, j)))
                    pool.wait_ge(*xhi_ready.at((("act", l), j)))
                    nc.gpsimd.tensor_tensor(a_lo[:, j, :], cv[:, j % 2, :], a_hi[:, j, :].bitcast(F32),
                                            ALU.subtract).then_inc(*xlo_ready.inc((("act", l), j)))

            def times_cos(g):
                nc.gpsimd.tensor_tensor(x_cos[:, g, :], qk2[0:ROT, g, :], const("cos2", ROT),
                                        ALU.mult).then_inc(*pool_step.inc(("xc", g)))

            ffn(0)
            for m in range(DT):
                add_square("kv", m, SEQ)
            root("kv", rtok, 0, 2)
            root("k2", rstd, 0, 16)
            pool.wait_ge(*dve_step.at("xk"))
            for g in range(8):
                times_cos(g)
            for p in range(4):
                pool.wait_ge(*var_ready.at(("q2", p)))
                for t in range(2):
                    a = 16 + 8 * t + 2 * p
                    ins = nc.gpsimd.tensor_tensor(rstd[:, a:a + 2], var[:, a:a + 2], mhalf[:, a:a + 2], ALU.pow)
                ins.then_inc(*rstd_ready.inc(("q2", p)))
                for g in (8 + 2 * p, 9 + 2 * p):
                    times_cos(g)
            ffn(1)
    return {name: s.marks for name, s in signals.items()}


def shape_constants():
    c = np.zeros((P, NCONST), np.float32)

    def put(name, value):
        a, n = CONSTS[name]
        value = np.asarray(value, np.float32)
        assert value.shape[1] == n, name
        c[:value.shape[0], a:a + n] = value

    put("ident", np.eye(P))
    rot = np.zeros((P, P))
    for q in range(P):
        rot[(q + 16, q) if q % 32 < 16 else (q - 16, q)] = -1.0 if q % 32 < 16 else 1.0
    put("rot1", rot)
    jrev = np.zeros((P, P))
    for q in range(P):
        jrev[GRID_W * (q // GRID_W) + GRID_W - 1 - q % GRID_W, q] = 1.0
    put("jrev", jrev)
    t = np.arange(SEQ)
    row = np.concatenate([t // GRID_W, np.zeros(META, int)]).astype(np.float32)
    col = np.concatenate([t % GRID_W, np.zeros(META, int)]).astype(np.float32)
    inv = np.float32(10000.0) ** (-np.arange(0, 32, 2, dtype=np.float32) / np.float32(32))
    ar, ac = (inv[:, None] * z[None, :] for z in (row, col))
    ang = np.concatenate([ar, ar, ac, ac] * 2, axis=0)
    put("cos1", np.cos(ang))
    put("sin1", np.sin(ang))
    cc = GRID_W - 1 - np.arange(P) % GRID_W
    start = np.clip(cc - NA_KW // 2, 0, GRID_W - NA_KW)[:, None]
    j = np.arange(GRID_W)[None, :]
    put("window", np.where((j >= start) & (j < start + NA_KW), 0.0, NEG))
    a, b = np.arange(P)[:, None], np.arange(P)[None, :]
    put("causal", np.where(b <= a, 0.0, NEG))
    put("causal_t", np.concatenate([np.where(a <= b, 0.0, NEG), np.zeros((P, P))], axis=1))
    s, u = np.arange(P)[:, None], np.arange(SEQ)[None, :]
    put("tri_neg", np.concatenate([-(s + P * k <= u).astype(np.float32) for k in range(2)], axis=1))
    put("eye2", np.concatenate([(s + P * k == u).astype(np.float32) for k in range(2)], axis=1))
    put("head_sum", np.stack([np.arange(P) < HD, np.arange(P) >= HD], axis=1))
    put("ones", np.ones((P, 2)))
    put("sel4", np.repeat(np.eye(M_HEADS), P, axis=1))
    put("sel10", np.repeat(np.eye(10), HD, axis=1))
    inv2 = np.float32(500000.0) ** (-np.arange(0, ROT, 2, dtype=np.float32) / np.float32(ROT))
    ang2 = inv2[:, None] * t[None, :].astype(np.float32)
    put("cos2", np.cos(np.concatenate([ang2, ang2])))
    put("sin2", np.sin(np.concatenate([ang2, ang2])))
    rot2 = np.zeros((ROT, ROT))
    for q in range(ROT):
        rot2[(q + 16, q) if q < 16 else (q - 16, q)] = -1.0 if q < 16 else 1.0
    put("rot2", rot2)
    return c


def cols(x):
    return np.ascontiguousarray(x).reshape(-1, P).T


def pair_heads(w, axis):
    w = np.moveaxis(w, axis, 0)
    w = w.reshape(KV, GROUP, HD, *w.shape[1:])
    w = np.swapaxes(w, 0, 1).reshape(KV * GROUP * HD, *w.shape[3:])
    return np.moveaxis(w, 0, axis)


def by_tile(w):
    k, m = w.shape
    return w.reshape(k // P, P, m // P, P).transpose(2, 0, 1, 3).reshape(-1, P, P)


def by_row(w):
    k, m = w.shape
    return w.reshape(k // P, P, m // P, P).transpose(0, 2, 1, 3).reshape(-1, P, P)


def weight_stream(inp):
    blocks = []
    for i in range(LAYERS):
        w = inp["w_in"][i]
        qa, ka, va, za, qb, kb, vb, zb, ga, gb = np.split(w, np.cumsum([512, 128, 128, 512, 512, 512, 512, 512, 1024]), axis=1)
        blocks += [by_tile(ka), by_tile(pair_heads(qa, 1)), by_tile(qb), by_tile(kb), by_row(va), by_row(vb),
                   by_tile(pair_heads(za, 1)), by_tile(zb), by_tile(ga), by_tile(gb)]
        wa, wn = by_tile(pair_heads(inp["w_o_attn"][i], 0)), by_tile(inp["w_o_na"][i])
        blocks += [wn, wa]
        blocks += [by_tile(inp["w_out"][i])]
    w = inp["a_w_in_2"][0]
    blocks += [by_tile(w[:, 0:1024]), by_row(w[:, 1024:2048]), by_tile(w[:, 2048:3072]), by_tile(inp["a_w_out_2"][0])]
    for l in range(2):
        up = by_tile(inp["f_w_up_2"][l]).reshape(2, FFT, DT, P, P).swapaxes(0, 1)
        blocks += [up.reshape(-1, P, P), by_tile(inp["f_w_down_2"][l])]
        if l == 0:
            w = inp["w_kv_2"]
            blocks += [by_tile(w[:, 0:1024]), by_row(w[:, 1024:2048]), by_tile(inp["b_w_q_2"][0]), by_tile(inp["b_w_o_2"][0])]
    stream = np.concatenate(blocks)
    return np.ascontiguousarray(stream.reshape(-1, CH, P, P).transpose(0, 2, 1, 3)).reshape(-1, P, CH * P)


def parameter_vectors(inp):
    g = inp["a_b_gates_2"][0].reshape(1, 8)
    w = inp["a_w_in_2"][0][:, 3072:3080].reshape(DT, P, 8).transpose(1, 0, 2).reshape(P, 64)
    two = lambda x: np.concatenate([x, x], axis=1).T
    parts = {
        "norm_g": cols(inp["norm_g"]), "qg": two(inp["q_norm_g"]), "kg": two(inp["k_norm_g"]),
        "final_g": cols(inp["final_norm_g"]), "a_norm": cols(inp["a_norm_2"]), "a_h_norm": cols(inp["a_h_norm_2"]),
        "kv_norm": cols(inp["kv_norm_2"]), "k_norm": cols(inp["k_norm_2"]), "b_norm": cols(inp["b_norm_2"]),
        "b_q_norm": cols(inp["b_q_norm_2"]), "f_norm": cols(inp["f_norm_2"]), "conv_w": cols(inp["f_conv_w_2"]),
        "conv_b": cols(inp["f_conv_b_2"]), "b_gates": np.broadcast_to(g, (P, 8)), "w_gates": w,
    }
    assert all(parts[n].shape == (P, k) for n, (_, k) in VECS.items())
    return np.ascontiguousarray(np.concatenate([parts[n] for n in VECS], axis=1))


def kernel(**inputs):
    import concourse.bacc as bacc
    from concourse.bass_utils import run_bass_kernel_spmd

    inp = {k: np.asarray(v) for k, v in inputs.items()}
    tokens = np.concatenate([inp["x"][0], inp["meta_tokens"]], axis=0)
    arrays = {
        "x_t": np.ascontiguousarray(tokens.T.reshape(DT, P, L1).transpose(1, 0, 2)),
        "consts": shape_constants(),
        "vecs": parameter_vectors(inp),
        "rpb": np.ascontiguousarray(inp["na_rpb"]),
        "weights": weight_stream(inp),
    }

    def build(known):
        nc = bacc.Bacc("TRN2", target_bir_lowering=False, num_devices=1)
        args = [nc.dram_tensor(n, a.shape, F32, kind="ExternalInput").ap() for n, a in arrays.items()]
        out = nc.dram_tensor("out", (P, DT, SEQ), F32, kind="ExternalOutput").ap()
        return nc, program(nc, *args, out, known)

    _, marks = build({})
    nc, _ = build(marks)
    r = run_bass_kernel_spmd(nc, [arrays], core_ids=[0])
    got = r.results[0]["out"]
    return got.transpose(2, 1, 0).reshape(1, SEQ, D)
```

```python
from contextlib import ExitStack

import numpy as np

import concourse.bass as bass
from concourse import mybir

F32 = mybir.dt.float32
PART = mybir.dt.float32r
ALU = mybir.AluOpType
ACT = mybir.ActivationFunctionType
AX_X = mybir.AxisListType.X

P = 128
D = 1024
DT = D // P
SEQ = 256
META = 16
L1 = SEQ + META
LAYERS = 2
EPS = 1e-6
NEG = -1e30

GRID_W, NA_KW, RPB_H, RPB_W = 64, 16, 15, 31
HD = 64
GROUP = 4
KV = 2
NA_HEADS = 8
VCOLS = KV * HD + NA_HEADS * HD
M_HEADS = 4
A_HEADS = 8
ROT = 32
FFT = 2816 // P

TT1 = [(0, 128), (128, 128), (256, META)]
TT2 = TT1[:2]

CH = 8
RAW_SLOTS = 4
PART_SLOTS = 4

CONSTS = {}
_at = 0
for _name, _n in [("ident", 128), ("ones", 2), ("rot1", 128), ("jrev", 128), ("cos1", L1), ("sin1", L1), ("window", GRID_W),
                  ("causal", 128), ("tri_neg", 512), ("eye2", 512), ("causal_t", 256), ("head_sum", 2),
                  ("sel4", 512), ("sel10", 5 * 128), ("cos2", 256), ("sin2", 256), ("rot2", 32)]:
    CONSTS[_name] = (_at, _n)
    _at += _n
NCONST = _at
NFIRST = 130
VECS = {}
_at = 0
for _name, _n in [("norm_g", 16), ("qg", 2), ("kg", 2), ("final_g", 8), ("a_norm", 8), ("a_h_norm", 8), ("kv_norm", 8),
                  ("k_norm", 1), ("b_norm", 8), ("b_q_norm", 1), ("f_norm", 16), ("conv_w", 2 * 3 * 2 * FFT),
                  ("conv_b", 2 * 2 * FFT), ("b_gates", 8), ("w_gates", 64)]:
    VECS[_name] = (_at, _n)
    _at += _n
NVEC = _at


class Signal:

    def __init__(self, sem, known):
        self.sem, self.known, self.marks, self.n = sem, known, {}, 0

    def inc(self, key, by=1):
        assert key not in self.marks, key
        self.n += by
        self.marks[key] = self.n
        return self.sem, by

    def at(self, key):
        assert not self.known or key in self.known, key
        return self.sem, self.known.get(key, 1)


Q_COLS = [L1] * (LAYERS - 1) + [SEQ]


def stats_after(i):
    return 1 if i == 0 else 0


def layer_units(i):
    units = [("na", hd, a) for hd in range(NA_HEADS) for a in range(2)]
    if Q_COLS[i] == L1:
        starts = [(c, min(P, GROUP * L1 - c)) for c in range(0, GROUP * L1, P)]
    else:
        starts = [(L1 * j + t, P) for j in range(GROUP) for t in range(0, SEQ, P)]
    return units + [("ga", g, c, n) for c, n in starts for g in range(KV)]


def first_unit(i):
    return sum(len(layer_units(l)) for l in range(i))


def last_unit(i, m):
    if m >= GROUP:
        return 4 * (m - GROUP) + 3
    return max(u for u, (kind, _, c, *_) in enumerate(layer_units(i)) if kind == "ga" and c < L1 * m + Q_COLS[i])


def gated_at(i, u):
    return [m for m in range(DT) if m != GROUP - 1 and last_unit(i, m) + 3 + (m >= GROUP) == u]


def filler(i, u):
    steps = len(layer_units(i)) - 7
    gates = [("gate", n) for n in range(24) if n * steps // 24 == u]
    return gates + ([("yb", u - steps)] if steps <= u < steps + DT else [])


UNITS2 = 2 * A_HEADS


def attention_steps(m):
    return {4: range(0, 3), 5: range(3, 6), 6: range(6, 7), 7: range(7, UNITS2 + 3)}.get(m, range(0))


def rope_at(m=None, step=None):
    if step is not None:
        return {8: [5], 10: [6], 12: [7]}.get(step, [])
    return {3: [0, 1], 5: [2, 3], 7: [4]}.get(m, [])


def tile_list():
    tiles, at = [], 0

    def add(name, engine, blocks):
        nonlocal at
        tiles.append((name, engine, at, blocks))
        at += blocks

    def rows(names, blocks):
        nonlocal at
        for name in names:
            tiles.append((name, "dve", at, blocks))
        at += blocks

    for i in range(LAYERS):
        add(("ka", i), "act", DT)
        for m in range(4):
            add(("qa", i, m), "act", DT)
        for m in range(4):
            add(("qb", i, m), "dve", DT)
        for m in range(4):
            add(("kb", i, m), "dve", DT)
        rows([("va", i, t) for t in range(3)], DT)
        rows([("vb", i, t) for t in range(3)], 4 * DT)
        for u in range(len(layer_units(i)) + 2):
            for kind, n in filler(i, u):
                add((kind, i, n), "dve", DT if kind == "gate" else 4)
            if u >= 2:
                add(("mx", i, u - 2), "act", 0)
        for m in range(DT):
            add(("ya", i, m), "dve", 4)
        for m in range(DT):
            add(("out", i, m), "dve", DT)
    for m in range(4):
        add(("mq", m), "dve", DT)
    for m in range(4):
        add(("mk", m), "dve", DT)
    rows([("mv", t, s) for t in range(2) for s in range(2)], 8 * DT)
    for m in range(DT):
        add(("mo", m), "dve", DT)
    for m in range(DT):
        add(("mout", m), "dve", DT)
    for l in range(2):
        for j in range(FFT):
            add(("uv", l, j), "dve", DT)
            add(("ug", l, j), "dve", DT)
        for m in range(DT):
            add(("down", l, m), "dve", FFT)
        if l == 0:
            for m in range(DT):
                add(("kk", m), "act", DT)
            rows([("vv", t, s) for t in range(2) for s in range(2)], 8 * DT)
            for m in range(DT):
                add(("qq", m), "act", DT)
                for hd in rope_at(m):
                    add(("rope", hd), "dve", 0)
                for u in attention_steps(m):
                    for hd in rope_at(step=u):
                        add(("rope", hd), "dve", 0)
                    if u >= 3:
                        add(("mx2", u - 3), "dve", 0)
            for m in range(DT):
                add(("aout", m), "dve", DT)
    return tiles, at // CH


def program(nc, x_t, consts_d, vecs_d, rpb, weights, out, known):
    ctx = ExitStack()
    with ctx:
        signals = {}

        def sb(name, shape, dt=F32, stack=ctx):
            return stack.enter_context(nc.sbuf_tensor(name, shape, dt))

        def signal(name):
            signals[name] = Signal(ctx.enter_context(nc.semaphore(name)), known.get(name, {}))
            return signals[name]

        acc = ctx.enter_context(nc.psum_tensor("acc", [P, 4, 512], F32))
        misc = ctx.enter_context(nc.psum_tensor("misc", [P, 4, 512], F32))
        raw = sb("raw", [P, RAW_SLOTS, CH * P])
        w_hi = sb("w_hi", [P, PART_SLOTS, CH * P], PART)
        w_lo = sb("w_lo", [P, PART_SLOTS, CH * P], PART)
        cst = sb("cst", [P, NCONST])
        vec = sb("vec", [P, NVEC])
        h = sb("h", [P, DT, L1])
        xt = sb("xt", [P, DT, L1])
        xs_hi = sb("xs_hi", [P, DT, L1], PART)
        xs_lo = sb("xs_lo", [P, DT, L1], PART)
        ys_hi = sb("ys_hi", [P, DT, L1], PART)
        ys_lo = sb("ys_lo", [P, DT, L1], PART)
        var = sb("var", [P, 32])
        rstd = sb("rstd", [P, 32])
        mhalf = sb("mhalf", [P, 32])
        nmax = sb("nmax", [P, 3])
        rsum = sb("rsum", [P, 3])
        rinv = sb("rinv", [P, 3])
        rtok = sb("rtok", [P, 4])
        eps_var = sb("eps_var", [P, 4])
        sq_sum = sb("sq_sum", [P, L1])
        rb_sb = sb("rb_sb", [P, 2 * SEQ])
        fga = sb("fga", [P, DT])
        qscale = sb("qscale", [P, 3])
        gw_hi = sb("gw_hi", [P, 64], PART)
        gw_lo = sb("gw_lo", [P, 64], PART)

        with ExitStack() as first:
            rq = sb("rq", [P, 5, L1], F32, first)
            xg = sb("xg", [P, 5, L1], F32, first)
            qf = sb("qf", [P, 5, L1], F32, first)
            rrow = sb("rrow", [10, L1], F32, first)
            t2 = sb("t2", [P, L1], F32, first)
            qkn = sb("qkn", [P, 8, L1], F32, first)
            v_sb = sb("v_sb", [P, 3, VCOLS], F32, first)
            gates = sb("gates", [P, 24, L1], F32, first)
            o_raw = sb("o_raw", [P, 8, L1], F32, first)
            bias = sb("bias", [P, NA_HEADS, 6 * GRID_W], F32, first)
            probs = sb("probs", [P, 2, L1], F32, first)
            pt = sb("pt", [P, 2, 384], F32, first)
            pm = sb("pm", [META, 128], F32, first)
            pmt = sb("pmt", [META, 128], F32, first)
            z_tanh = xg
            ms = sb("ms", [META, 16], F32, first)
        with ExitStack() as mixers:
            qk2 = sb("qk2", [P, 16, SEQ], F32, mixers)
            v2 = sb("v2", [P, 2, D], F32, mixers)
            og = sb("og", [P, DT, SEQ], F32, mixers)
            num = sb("num", [P, DT, SEQ], F32, mixers)
            dmat = sb("dmat", [P, M_HEADS, 384], F32, mixers)
            sq_sum2 = sb("sq_sum2", [P, SEQ], F32, mixers)
            gate_rows = sb("gate_rows", [8, SEQ], F32, mixers)
            g8 = sb("g8", [P, 2, 8], F32, mixers)
            ab = sb("ab", [P, 2, 4], F32, mixers)
            ln1 = sb("ln1", [P, 2, 4], F32, mixers)
            lf = sb("lf", [P, 2, 4], F32, mixers)
            nf = sb("nf", [P, 2, 4], F32, mixers)
            a_tok = sb("a_tok", [P, 2, 4], F32, mixers)
            floor = sb("floor", [P, 2, 4], F32, mixers)
            den = sb("den", [P, 2, 4], F32, mixers)
            fac = sb("fac", [P, 8], F32, mixers)
            cmax = sb("cmax", [M_HEADS, 2, 128 + SEQ], F32, mixers)
            probs2 = sb("probs2", [P, 3, SEQ], F32, mixers)
            pt2 = sb("pt2", [P, 2, SEQ], F32, mixers)
            rope_t = sb("rope_t", [ROT, 2, SEQ], F32, mixers)
            x_cos = sb("x_cos", [ROT, 16, SEQ], F32, mixers)
        with ExitStack() as ffn_mem:
            a_hi = sb("a_hi", [P, FFT, SEQ], PART, ffn_mem)
            a_lo = sb("a_lo", [P, FFT, SEQ], PART, ffn_mem)
            up = sb("up", [P, 2, 2, SEQ], F32, ffn_mem)
            cv = sb("cv", [P, 2, SEQ], F32, ffn_mem)
            cg = sb("cg", [P, 2, SEQ], F32, ffn_mem)

        def const(name, rows=P):
            a, n = CONSTS[name]
            return cst[0:rows, a:a + n]

        def v(name, i=0, n=1):
            a = VECS[name][0] + i
            return vec[:, a:a + n]

        ident = const("ident")
        qn, kn = qkn[:, 0:4, :], qkn[:, 4:8, :]
        pair = ((xs_hi, xs_lo), (ys_hi, ys_lo))

        inputs_loaded = signal("inputs_loaded")
        h_loaded = signal("h_loaded")
        h2_loaded = signal("h2_loaded")
        first_loaded = signal("first_loaded")
        cst_loaded = signal("cst_loaded")
        bias_loaded = signal("bias_loaded")
        raw_landed = [signal(f"raw_landed{i}") for i in range(RAW_SLOTS)]
        hi_ready = signal("hi_ready")
        lo_ready = signal("lo_ready")
        chunk_used = signal("chunk_used")
        tile_done = signal("tile_done")
        act_evac = signal("act_evac")
        dve_evac = signal("dve_evac")
        sq_ready = signal("sq_ready")
        stats_done = signal("stats_done")
        var_ready = signal("var_ready")
        rstd_ready = signal("rstd_ready")
        bcast_done = signal("bcast_done")
        x_ready = signal("x_ready")
        xhi_ready = signal("xhi_ready")
        xlo_ready = signal("xlo_ready")
        xlo_ready_dve = signal("xlo_ready_dve")
        scores_done = signal("scores_done")
        max_ready = signal("max_ready")
        exp_ready = signal("exp_ready")
        probs_ready = signal("probs_ready")
        turned = signal("turned")
        turned_copied = signal("turned_copied")
        act_step = signal("act_step")
        dve_step = signal("dve_step")
        pool_step = signal("pool_step")
        pe_step = signal("pe_step")
        stored = signal("stored")

        tiles, n_chunks = tile_list()
        assert n_chunks == weights.shape[0]
        index = {name: n for n, (name, *_) in enumerate(tiles)}
        last_chunk = {name: (b + k - 1) // CH for name, _, b, k in tiles}
        ends_tile = {b + k: name for name, _, b, k in tiles if k}

        def bank(name):
            return acc[:, index[name] % 4, :]

        def chunk_free(eng, c):
            name = ends_tile.get((c + 1) * CH)
            eng.wait_ge(*(tile_done.at(name) if name else chunk_used.at(c)))

        block = ctx.enter_context(nc.Block())

        @block.sync
        def _(sp):
            def load_bias(i):
                for r in range(2):
                    for hd in range(NA_HEADS):
                        src = bass.AP(tensor=rpb.tensor, offset=((i * NA_HEADS + hd) * RPB_H + 5 - r) * RPB_W - 48,
                                      ap=[[1, GRID_W], [RPB_W, 6], [1, GRID_W]])
                        sp.dma_start(bias[GRID_W * r:GRID_W * r + GRID_W, hd, :].rearrange("p (d j) -> p d j", d=6),
                                     src).then_inc(*bias_loaded.inc((i, r, hd), 16))

            sp.dma_start(vec[:], vecs_d).then_inc(*inputs_loaded.inc("vec", 16))
            sp.dma_start(h[:, 0:4], x_t[:, 0:4]).then_inc(*h_loaded.inc("h0", 16))
            for c in range(n_chunks):
                if c >= RAW_SLOTS:
                    sp.wait_ge(*lo_ready.at(c - RAW_SLOTS))
                sp.dma_start(raw[:, c % RAW_SLOTS, :], weights[c]).then_inc(*raw_landed[c % RAW_SLOTS].inc(c, 16))
                if c == 0:
                    sp.dma_start(h[:, 4:8], x_t[:, 4:8]).then_inc(*h2_loaded.inc("h4", 16))
                if c == 1:
                    sp.dma_start(cst[:, 0:NFIRST], consts_d[:, 0:NFIRST]).then_inc(*first_loaded.inc("first", 16))
                if c == 5:
                    sp.dma_start(cst[:, NFIRST:], consts_d[:, NFIRST:]).then_inc(*cst_loaded.inc("cst", 16))
                if c == 8:
                    load_bias(0)
                if c == last_chunk[("ya", 0, 0)]:
                    sp.wait_ge(*scores_done.at(2 * NA_HEADS - 1))
                    load_bias(1)
            for m in range(DT):
                sp.wait_ge(*dve_evac.at(("down", 1, m)))
                sp.dma_start(out[:, m], h[:, m, 0:SEQ]).then_inc(*stored.inc(m, 16))
            sp.wait_ge(*stored.at(DT - 1))

        units2 = [(hd, t) for hd in range(A_HEADS) for t in range(2)]
        FB = (2, 0, 3, 1)

        def meta_at(hd):
            return 64 * (hd % 2) + META * (hd // 2)

        def qflat(g):
            return qf[HD * g:HD * g + HD, 1:5, :].rearrange("p j t -> p (j t)")

        @block.tensor
        def _(pe):
            seen = set()

            def once(signal_, key):
                if (id(signal_), key) not in seen:
                    seen.add((id(signal_), key))
                    pe.wait_ge(*signal_.at(key))

            def once_low(key, k):
                if key == "attn":
                    once(dve_evac, ("mx2", 2 * k + 1))
                else:
                    direct = (key[0] if isinstance(key, tuple) else key) in ("x", "a", "kv", "b", "f") or \
                        (key == "mlstm" and k % 2)
                    once(xlo_ready_dve if direct else xlo_ready, (key, k))

            def weight(b, n=P):
                c, j = divmod(b, CH)
                once(lo_ready, c)
                s = c % PART_SLOTS
                return w_hi[:, s, j * P:j * P + n], w_lo[:, s, j * P:j * P + n]

            def acc_free(name):
                n = index[name] - 4
                if n >= 0:
                    before, engine, *_ = tiles[n]
                    pe.wait_ge(*(act_evac if engine == "act" else dve_evac).at(before))

            def parts(o, lhs, rhs, first, last):
                pe.matmul(o, lhs[0], rhs[0], start=first, stop=False)
                pe.matmul(o, lhs[0], rhs[1], start=False, stop=False)
                return pe.matmul(o, lhs[1], rhs[0], start=False, stop=last)

            def tile(name, x_hi, x_lo, key, k0=0, cols=SEQ):
                _, _, b0, blocks = tiles[index[name]]
                acc_free(name)
                o = bank(name)[:, 0:cols]
                for i in range(blocks):
                    w = weight(b0 + i)
                    once_low(key, k0 + i)
                    mm = parts(o, w, (x_hi[:, k0 + i, 0:cols], x_lo[:, k0 + i, 0:cols]), i == 0, i == blocks - 1)
                    if i == blocks - 1:
                        mm.then_inc(*tile_done.inc(name))
                    elif (b0 + i) % CH == CH - 1:
                        mm.then_inc(*chunk_used.inc((b0 + i) // CH))

            def row_tiles(names, x_hi, x_lo, key, tts, width, halves=1, between=None):
                b0 = tiles[index[names[0]]][2]
                for name in names:
                    acc_free(name)
                bk = width // P * halves
                for c0 in range(0, DT * bk, CH):
                    for n, name in enumerate(names):
                        t, s = divmod(n, halves)
                        tok, tn = tts[t]
                        for k in range(c0 // bk, (c0 + CH) // bk):
                            w = weight(b0 + k * bk + s * (width // P), width)
                            once_low(key, k)
                            x = (x_hi[:, k, tok:tok + tn], x_lo[:, k, tok:tok + tn])
                            o = bank(name)[0:tn, 0:width]
                            mm = parts(o, x, w, k == 0, k == DT - 1)
                        if c0 + CH == DT * bk:
                            mm.then_inc(*tile_done.inc(name))
                    if c0 + CH < DT * bk:
                        mm.then_inc(*chunk_used.inc((b0 + c0) // CH))
                    if between:
                        between(c0 // CH)

            def stats(key, tts, n=0):
                pe.wait_ge(*pool_step.at(("sum", key, DT - 1)))
                for t, (t0, tn) in enumerate(tts):
                    c = 4 * n + t
                    mm = pe.matmul(misc[0:tn, 3, c:c + 1], (sq_sum, sq_sum2)[n][:, t0:t0 + tn], const("ones")[:, 0:1], start=True,
                                   stop=True)
                mm.then_inc(*stats_done.inc(key))

            def spread(key, tts, ready=None, col=0):
                pe.wait_ge(*rstd_ready.at(ready or key))
                c0 = SEQ * (col // 2)
                for t, (t0, tn) in enumerate(tts):
                    mm = pe.matmul(misc[:, 2, c0 + t0:c0 + t0 + tn], rtok[0:tn, col + t:col + t + 1].to_broadcast([tn, P]),
                                   ident[0:tn, 0:tn], start=True, stop=True)
                mm.then_inc(*bcast_done.inc(key))

            pe.wait_ge(*inputs_loaded.at("vec"))
            for _ in range(8):
                pe.matmul(misc[:, 0, 0:SEQ], vec[:, 0:P], vec[:, 0:SEQ], start=True, stop=True)
            for i in range(LAYERS):
                key = ("x", i)
                xp, op = pair[i % 2], pair[1 - i % 2]
                units, nq, metas = layer_units(i), Q_COLS[i], Q_COLS[i] > SEQ

                def proj(name):
                    tile(name, *xp, key, cols=L1 if name[0] in ("ka", "kb") else nq)

                def rot(j):
                    pe.wait_ge(*dve_step.at(("xg", i)))
                    if j >= 2:
                        pe.wait_ge(*dve_step.at(("t2", i, j - 2)))
                    n = nq if j else L1
                    pe.matmul(misc[:, j % 2, 0:n], const("rot1"), xg[:, j, 0:n], start=True,
                              stop=True).then_inc(*pe_step.inc(("rot", i, j)))

                def rb(j):
                    pe.wait_ge(*dve_step.at(("rrow", i)))
                    if j >= 2:
                        pe.wait_ge(*dve_step.at(("qf", i, j - 2)))
                    a, _ = CONSTS["sel10"]
                    n = nq if j else L1
                    pe.matmul(misc[:, 2 + j % 2, 0:n], cst[0:10, a + j * P:a + (j + 1) * P], rrow[:, 0:n], start=True,
                              stop=True).then_inc(*pe_step.inc(("rb", i, j)))

                def head_sums(j):
                    pe.wait_ge(*dve_step.at(("qsq", i, j)))
                    for t, (t0, tn) in enumerate(TT1 if metas or j == 0 else TT2):
                        mm = pe.matmul(misc[0:tn, 3, 10 * t + 2 * j:10 * t + 2 * j + 2], qf[:, j, t0:t0 + tn],
                                       const("head_sum"), start=True, stop=True)
                    return mm

                proj(("ka", i))
                for m in range(4):
                    proj(("qa", i, m))
                    if m == stats_after(i):
                        if i == 0:
                            pe.wait_ge(*first_loaded.at("first"))
                        stats(key, TT1)
                    if m == 2 * stats_after(i) + 1:
                        spread(key, TT1)
                    if m == 2:
                        if i == 0:
                            pe.wait_ge(*cst_loaded.at("cst"))
                        pe.wait_ge(*var_ready.at(key))
                        head_sums(0)
                        head_sums(1)
                head_sums(2)
                proj(("qb", i, 0))
                head_sums(3)
                proj(("qb", i, 1))
                head_sums(4).then_inc(*stats_done.inc(("qk", i)))
                rot(0)
                rot(1)
                for m in (2, 3):
                    proj(("qb", i, m))
                proj(("kb", i, 0))
                pe.wait_ge(*rstd_ready.at(("qk", i)))
                for t, (t0, tn) in enumerate(TT1):
                    mm = pe.matmul(misc[0:10, 3, t0:t0 + tn], rstd[0:tn, 10 * t:10 * t + 10], ident[0:tn, 0:tn],
                                   start=True, stop=True)
                mm.then_inc(*pe_step.inc(("rt", i)))
                proj(("kb", i, 1))
                rb(0)
                rb(1)
                proj(("kb", i, 2))
                rot(2)
                rb(2)
                proj(("kb", i, 3))
                rot(3)
                rb(3)
                row_tiles([("va", i, t) for t in range(3)], *xp, key, TT1, P)
                rot(4)
                rb(4)
                pe.wait_ge(*dve_evac.at(("kb", i, 3)))
                pe.wait_ge(*dve_step.at(("t2", i, 4)))
                for hd in range(NA_HEADS if metas else 0):
                    a = HD * (hd % 2)
                    mm = pe.matmul(misc[0:META, hd % 2, META * (hd // 2):META * (hd // 2) + META], qn[a:a + HD, hd // 2, SEQ:L1],
                                   kn[a:a + HD, hd // 2, SEQ:L1], start=True, stop=True)
                if metas:
                    mm.then_inc(*pe_step.inc(("meta_s", i)))
                row_tiles([("vb", i, t) for t in range(3)], *xp, key, TT1, 512)
                pe.wait_ge(*dve_step.at(("qf", i, 4)))
                if metas:
                    pe.wait_ge(*dve_step.at(("meta_p", i)))
                for hd in range(NA_HEADS if metas else 0):
                    mm = pe.matmul(misc[0:META, 2, META * hd:META * hd + META], pm[:, meta_at(hd):meta_at(hd) + META],
                                   ident[0:META, 0:META], start=True, stop=True)
                if metas:
                    mm.then_inc(*pe_step.inc(("meta_t", i)))

                def scores(u):
                    n = first_unit(i) + u
                    if u >= 2:
                        pe.wait_ge(*exp_ready.at(n - 2))
                    o = misc[:, u % 2, 0:L1]
                    if units[u][0] == "na":
                        _, hd, a = units[u]
                        p0 = HD * (hd % 2)
                        if u == 0:
                            pe.wait_ge(*pool_step.at(("bias", i)))
                        pe.matmul(o, qn[p0:p0 + HD, hd // 2, a * P:(a + 1) * P], kn[p0:p0 + HD, hd // 2, :],
                                  start=True, stop=False)
                        b0 = 2 * (1 - a) * GRID_W
                        mm = pe.matmul(o[:, 0:SEQ], const("jrev"), bias[:, hd, b0:b0 + 4 * GRID_W], start=False,
                                       stop=True)
                    else:
                        _, g, c0, cn = units[u]
                        mm = pe.matmul(o[0:cn], qflat(g)[:, c0:c0 + cn], qf[HD * g:HD * g + HD, 0, :], start=True,
                                       stop=True)
                    mm.then_inc(*scores_done.inc(n))

                def turn(u):
                    n = first_unit(i) + u
                    pe.wait_ge(*probs_ready.at(n))
                    if u >= 1:
                        pe.wait_ge(*turned_copied.at(n - 1))
                    q = P if units[u][0] == "na" else units[u][3]
                    for t, (t0, tn) in enumerate(TT1):
                        mm = pe.transpose(misc[0:tn, 2, t * P:t * P + q], probs[0:q, u % 2, t0:t0 + tn], ident[0:q, 0:q])
                    mm.then_inc(*turned.inc(n))

                def mix(u):
                    n = first_unit(i) + u
                    pe.wait_ge(*turned_copied.at(n))
                    acc_free(("mx", i, u))
                    if units[u][0] == "na":
                        _, hd, _ = units[u]
                        q, half, v0 = P, hd % 2, KV * HD + hd * HD
                    else:
                        _, half, _, q = units[u]
                        v0 = half * HD
                    for t, (t0, tn) in enumerate(TT1):
                        mm = pe.matmul(bank(("mx", i, u))[HD * half:HD * half + HD, 0:q],
                                       v_sb[0:tn, t, v0:v0 + HD], pt[0:tn, u % 2, t * P:t * P + q],
                                       start=(t == 0), stop=(t == 2))
                    mm.then_inc(*tile_done.inc(("mx", i, u)))

                scores(0)
                proj(("gate", i, 0))
                if metas:
                    pe.wait_ge(*dve_step.at(("meta_pt", i)))
                for hd in range(NA_HEADS if metas else 0):
                    a = HD * (hd % 2)
                    c0 = KV * HD + hd * HD
                    mm = pe.matmul(misc[a:a + HD, 3, META * (hd // 2):META * (hd // 2) + META],
                                   v_sb[0:META, 2, c0:c0 + HD], pmt[:, META * hd:META * hd + META], start=True, stop=True)
                if metas:
                    mm.then_inc(*pe_step.inc(("meta_o", i)))
                    pe.wait_ge(*act_step.at(("meta_o", i)))
                for u in range(1, len(units) + 2):
                    if u < len(units):
                        scores(u)
                    for kind, m in filler(i, u):
                        if kind == "gate":
                            proj((kind, i, m))
                        else:
                            tile((kind, i, m), *op, ("o", i), 4, nq)
                    if u - 1 < len(units):
                        turn(u - 1)
                    if u >= 2:
                        mix(u - 2)
                for m in range(DT):
                    tile(("ya", i, m), *op, ("o", i), 0, nq)
                for m in range(DT):
                    tile(("out", i, m), *xp, ("mix", i), 0, nq)

            tile(("mq", 0), xs_hi, xs_lo, "a")
            stats("final", TT2)
            stats("a", TT2, 1)
            tile(("mq", 1), xs_hi, xs_lo, "a")
            pe.wait_ge(*dve_step.at("gw_lo"))
            for k in range(DT):
                mm = parts(misc[0:8, 0, 0:SEQ], (gw_hi[:, 8 * k:8 * k + 8], gw_lo[:, 8 * k:8 * k + 8]),
                           (xs_hi[:, k, 0:SEQ], xs_lo[:, k, 0:SEQ]), k == 0, k == DT - 1)
            mm.then_inc(*pe_step.inc("gate_rows"))
            tri, eye2 = const("tri_neg"), const("eye2")
            tile(("mq", 2), xs_hi, xs_lo, "a")
            pe.wait_ge(*dve_step.at("gate_rows"))
            for t in range(2):
                mm = pe.matmul(misc[:, 1, 32 + 8 * t:40 + 8 * t], gate_rows[:, t * P:(t + 1) * P], ident[0:8, 0:8],
                               start=True, stop=True)
            mm.then_inc(*pe_step.inc("gates"))
            spread("final", TT2)
            spread("a", TT2, "final", 2)
            tile(("mq", 3), xs_hi, xs_lo, "a")
            tile(("mk", 0), xs_hi, xs_lo, "a")
            tile(("mk", 1), xs_hi, xs_lo, "a")
            pe.wait_ge(*dve_step.at("lf"))
            pe.matmul(misc[:, 1, 16:20], tri[:, 0:P], lf[:, 0, :], start=True, stop=True)
            pe.matmul(misc[:, 1, 20:24], tri[:, P:2 * P], lf[:, 0, :], start=True, stop=False)
            pe.matmul(misc[:, 1, 20:24], tri[:, 3 * P:4 * P], lf[:, 1, :], start=False, stop=True)
            for t in range(2):
                pe.matmul(misc[0:M_HEADS, 0, 0:SEQ], lf[:, t, :], tri[:, t * SEQ:(t + 1) * SEQ], start=(t == 0), stop=False)
            for t in range(2):
                mm = pe.matmul(misc[0:M_HEADS, 0, 0:SEQ], g8[:, t, 0:4], eye2[:, t * SEQ:(t + 1) * SEQ], start=False,
                               stop=(t == 1))
            mm.then_inc(*pe_step.inc("a_row"))
            tile(("mk", 2), xs_hi, xs_lo, "a")
            tile(("mk", 3), xs_hi, xs_lo, "a")
            top = cmax[:, 0, P:P + SEQ]

            def running_maximum(c):
                if c == 1:
                    pe.wait_ge(*dve_step.at("cmax"))
                    for t in range(2):
                        mm = pe.matmul(misc[:, 1, 24 + 4 * t:28 + 4 * t], top[:, t * P:(t + 1) * P],
                                       ident[0:M_HEADS, 0:M_HEADS], start=True, stop=True)
                    mm.then_inc(*pe_step.inc("m_tok"))

            row_tiles([("mv", t, s) for t in range(2) for s in range(2)], xs_hi, xs_lo, "a", TT2, 512, 2, running_maximum)
            a4, _ = CONSTS["sel4"]
            pe.wait_ge(*dve_evac.at(("mk", 3)))
            one = const("ones")[:, 0:1]
            for s in range(M_HEADS + 1):
                tile(("mo", s), xs_hi, xs_lo, "a")
                if s < M_HEADS:
                    if s:
                        pe.wait_ge(*dve_step.at(("d1", s - 1)))
                    pe.matmul(misc[:, 2, 0:SEQ], cst[0:M_HEADS, a4 + s * P:a4 + (s + 1) * P], top, start=True,
                              stop=True).then_inc(*pe_step.inc(("mb", s)))
                    if s:
                        pe.wait_ge(*dve_step.at(("sd", s - 1)))
                    pe.matmul(misc[:, 0, 0:SEQ], qk2[:, 4 + s, 0:P], qk2[:, s, :], start=True, stop=True)
                    pe.matmul(misc[:, 0, SEQ:384], qk2[:, 4 + s, P:SEQ], qk2[:, s, P:SEQ], start=True,
                              stop=True).then_inc(*pe_step.inc(("mst", s)))
                if s:
                    hd = s - 1
                    pe.wait_ge(*dve_step.at(("sd", hd)))
                    if hd:
                        pe.wait_ge(*act_step.at(("num", hd - 1)))
                    for j in range(2):
                        c0 = hd * SEQ + j * P
                        pe.matmul(misc[:, 3, j * SEQ:(j + 1) * SEQ], v2[:, 0, c0:c0 + P], dmat[:, hd, 0:SEQ],
                                  start=True, stop=False)
                        mm = pe.matmul(misc[:, 3, j * SEQ + P:(j + 1) * SEQ], v2[:, 1, c0:c0 + P],
                                       dmat[:, hd, SEQ:384], start=False, stop=True)
                    mm.then_inc(*pe_step.inc(("num", hd)))
                    pe.matmul(misc[:, 1, hd:hd + 1], dmat[:, hd, 0:P], one, start=True, stop=True)
                    pe.matmul(misc[:, 1, 4 + hd:5 + hd], dmat[:, hd, P:SEQ], one, start=True, stop=False)
                    pe.matmul(misc[:, 1, 4 + hd:5 + hd], dmat[:, hd, SEQ:384], one, start=False, stop=True)
            tile(("mo", 5), xs_hi, xs_lo, "a")
            for hd in range(M_HEADS):
                pe.wait_ge(*pool_step.at(("head_sum", hd)))
                for t in range(2):
                    mm = pe.matmul(misc[:, 1, 8 + 4 * t + hd:9 + 4 * t + hd], xt[:, 2 * hd, t * P:(t + 1) * P], one,
                                   start=True, stop=True)
            mm.then_inc(*pe_step.inc("nss"))
            for m in (6, 7):
                tile(("mo", m), xs_hi, xs_lo, "a")
            pe.wait_ge(*dve_step.at("fac"))
            for hd in range(M_HEADS):
                for t in range(2):
                    mm = pe.matmul(misc[:, FB[hd], t * P:(t + 1) * P], fac[:, 4 * t + hd:4 * t + hd + 1].to_broadcast([P, P]),
                                   ident, start=True, stop=True)
                mm.then_inc(*pe_step.inc(("fb", hd)))
            for m in range(DT):
                tile(("mout", m), ys_hi, ys_lo, "mlstm")

            def ffn(l):
                for j in range(FFT):
                    tile(("uv", l, j), *pair[l], ("f", l))
                    if j == 0:
                        stats(("f", l), TT2)
                    tile(("ug", l, j), *pair[l], ("f", l))
                    if j == 0:
                        spread(("f", l), TT2)
                for m in range(DT):
                    tile(("down", l, m), a_hi, a_lo, ("act", l))

            ffn(0)

            r2 = cst[0:ROT, CONSTS["rot2"][0]:CONSTS["rot2"][0] + ROT]

            def head_stats(g, c, name):
                pe.wait_ge(*dve_step.at(("sq2", g)))
                for t in range(2):
                    mm = pe.matmul(misc[:, 3, c[t]:c[t] + 1], xt[:, g % 8, t * P:(t + 1) * P], one,
                                   start=True, stop=True)
                mm.then_inc(*pe_step.inc(("st2", g)))

            def head_rope(g, o):
                pe.matmul(o[0:ROT, 0:SEQ], r2, qk2[0:ROT, g, :], start=True, stop=True)
                for t in range(2):
                    c = 8 * t + g if g < 8 else 16 + 8 * t + g - 8
                    mm = pe.matmul(o[:, SEQ + t * P:SEQ + (t + 1) * P], rstd[:, c:c + 1].to_broadcast([P, P]), ident,
                                   start=True, stop=True)
                return mm

            def key_ropes(c):
                if 3 <= c <= 6:
                    for g in (2 * c - 6, 2 * c - 5):
                        pe.wait_ge(*rstd_ready.at("k2"))
                        pe.wait_ge(*dve_step.at("xk"))
                        if g >= 2:
                            pe.wait_ge(*dve_step.at(("rope2", g - 2)))
                        head_rope(g, misc[:, g % 2, :]).then_inc(*pe_step.inc(("rope2", g)))

            def query_rope(hd):
                acc_free(("rope", hd))
                pe.wait_ge(*rstd_ready.at(("q2", hd // 2)))
                pe.wait_ge(*dve_step.at(("xq", hd // 2)))
                head_rope(8 + hd, bank(("rope", hd))).then_inc(*tile_done.inc(("rope", hd)))

            def scores2(u):
                hd, t = units2[u]
                n = first_unit(LAYERS) + u
                if u >= 2:
                    pe.wait_ge(*exp_ready.at(n - 2))
                if u == 0:
                    pe.wait_ge(*dve_step.at(("rope2", 7)))
                if t == 0:
                    pe.wait_ge(*dve_evac.at(("rope", hd)))
                keys = (t + 1) * P
                o = misc[:, u % 2, 0:keys]
                pe.matmul(o, qk2[:, 8 + hd, t * P:(t + 1) * P], qk2[:, hd, 0:keys], start=True, stop=False)
                pe.matmul(o[:, t * P:keys], ident, const("causal"), start=False,
                          stop=True).then_inc(*scores_done.inc(n))

            def turn2(u):
                n = first_unit(LAYERS) + u
                pe.wait_ge(*probs_ready.at(n))
                if u >= 1:
                    pe.wait_ge(*turned_copied.at(n - 1))
                for k in range(units2[u][1] + 1):
                    mm = pe.transpose(misc[:, 2, k * P:(k + 1) * P], probs2[:, u % 3, k * P:(k + 1) * P], ident)
                mm.then_inc(*turned.inc(n))

            def mix2(u):
                hd, t = units2[u]
                n = first_unit(LAYERS) + u
                pe.wait_ge(*turned_copied.at(n))
                acc_free(("mx2", u))
                for k in range(t + 1):
                    mm = pe.matmul(bank(("mx2", u))[:, 0:P], v2[:, k, hd * P:(hd + 1) * P],
                                   pt2[:, u % 2, k * P:(k + 1) * P], start=(k == 0), stop=(k == t))
                mm.then_inc(*tile_done.inc(("mx2", u)))

            for m in range(DT):
                tile(("kk", m), xs_hi, xs_lo, "kv")
                if m == 0:
                    stats("kv", TT2)
                elif m == 1:
                    pe.wait_ge(*var_ready.at("kv"))
                if m >= 1:
                    head_stats(m - 1, (m - 1, 8 + m - 1), "k")
            head_stats(7, (7, 15), "k")
            row_tiles([("vv", t, c) for t in range(2) for c in range(2)], xs_hi, xs_lo, "kv", TT2, 512, 2, key_ropes)
            for m in range(DT):
                tile(("qq", m), ys_hi, ys_lo, "b")
                if m == 0:
                    pe.wait_ge(*var_ready.at("k2"))
                for g in range(max(0, m - 1), m):
                    if g >= 2:
                        pe.wait_ge(*var_ready.at(("q2", g // 2 - 1)))
                    head_stats(8 + g, (16 + g, 24 + g), "q")
                for hd in rope_at(m):
                    query_rope(hd)
                for u in attention_steps(m):
                    for hd in rope_at(step=u):
                        query_rope(hd)
                    if u < UNITS2:
                        scores2(u)
                    if u == 7:
                        head_stats(15, (23, 31), "q")
                    if 2 <= u < UNITS2 + 2:
                        turn2(u - 2)
                    if u >= 3:
                        mix2(u - 3)
            for m in range(DT):
                tile(("aout", m), xs_hi, xs_lo, "attn")
            ffn(1)

        @block.scalar
        def _(act):
            at = {"next": 0}

            def split(upto):
                for c in range(at["next"], min(upto + 1, n_chunks)):
                    act.wait_ge(*raw_landed[c % RAW_SLOTS].at(c))
                    if c >= PART_SLOTS:
                        chunk_free(act, c - PART_SLOTS)
                    nc.scalar.activation(w_hi[:, c % PART_SLOTS, :], raw[:, c % RAW_SLOTS, :],
                                         ACT.Copy).then_inc(*hi_ready.inc(c))
                    at["next"] = c + 1

            def done(name):
                split(last_chunk[name] + PART_SLOTS - 1)
                act.wait_ge(*tile_done.at(name))

            def upper(key, dst, cols):
                for m in range(DT):
                    act.wait_ge(*x_ready.at((key, m)))
                    nc.scalar.activation(dst[:, m, 0:cols], xt[:, m, 0:cols], ACT.Copy).then_inc(*xhi_ready.inc((key, m)))

            def input_parts(m, cols, key, gain, dst, sq_key=None):
                nc.scalar.activation(dst[:, m, 0:cols], h[:, m, 0:cols], ACT.Copy, scale=gain).then_inc(*xhi_ready.inc((key, m)))
                if sq_key:
                    nc.scalar.activation(xt[:, m, 0:cols], h[:, m, 0:cols], ACT.Square).then_inc(*sq_ready.inc((sq_key, m)))

            act.wait_ge(*inputs_loaded.at("vec"))
            a, n = VECS["w_gates"]
            nc.scalar.activation(gw_hi[:, :], vec[:, a:a + n], ACT.Copy).then_inc(*act_step.inc("gw_hi"))
            act.wait_ge(*h_loaded.at("h0"))
            for m in range(DT):
                if m == 4:
                    act.wait_ge(*h2_loaded.at("h4"))
                input_parts(m, L1, ("x", 0), v("norm_g", m), xs_hi)
                if m == 3:
                    split(0)
            split(1)
            for m in range(DT):
                nc.scalar.activation(xt[:, m, :], h[:, m, :], ACT.Square).then_inc(*sq_ready.inc((("x", 0), m)))
                if m == 3:
                    split(2)
            for i in range(LAYERS):
                xp, op = pair[i % 2], pair[1 - i % 2]
                units, nq, metas = layer_units(i), Q_COLS[i], Q_COLS[i] > SEQ
                for j, name in enumerate([("ka", i)] + [("qa", i, m) for m in range(4)]):
                    done(name)
                    n = nq if j else L1
                    nc.scalar.activation(rq[:, j, 0:n], bank(name)[:, 0:n], ACT.Copy).then_inc(*act_evac.inc(name))
                for kind in ("qb", "kb"):
                    for m in range(4):
                        split(last_chunk[(kind, i, m)] + PART_SLOTS - 1)
                if metas:
                    act.wait_ge(*dve_step.at(("meta_x", i)))
                    nc.scalar.activation(pm[:, :], pm[:, :], ACT.Exp).then_inc(*act_step.inc(("meta_e", i)))

                def exp(u):
                    n = first_unit(i) + u
                    q = P if units[u][0] == "na" else units[u][3]
                    act.wait_ge(*max_ready.at(n))
                    if u >= 2:
                        act.wait_ge(*turned.at(n - 2))
                    nc.scalar.activation(probs[0:q, u % 2, :], misc[0:q, u % 2, 0:L1], ACT.Exp, bias=nmax[0:q, u % 2:u % 2 + 1],
                                         accum_out=rsum[0:q, u % 2:u % 2 + 1]).then_inc(*exp_ready.inc(n))

                def turn(u):
                    n = first_unit(i) + u
                    q = P if units[u][0] == "na" else units[u][3]
                    act.wait_ge(*turned.at(n))
                    if u >= 2:
                        act.wait_ge(*tile_done.at(("mx", i, u - 2)))
                    pv = pt[:, u % 2, 0:SEQ].rearrange("p (t q) -> p t q", t=2)[:, :, 0:q]
                    nc.scalar.activation(pv, misc[:, 2, 0:SEQ].rearrange("p (t q) -> p t q", t=2)[:, :, 0:q], ACT.Copy)
                    nc.scalar.activation(pt[0:META, u % 2, SEQ:SEQ + q], misc[0:META, 2, SEQ:SEQ + q],
                                         ACT.Copy).then_inc(*turned_copied.inc(n))

                def mixed(u):
                    n = first_unit(i) + u
                    act.wait_ge(*tile_done.at(("mx", i, u)))
                    if units[u][0] == "na":
                        _, hd, a = units[u]
                        half, q = hd % 2, P
                        dst = o_raw[HD * half:HD * half + HD, 4 + hd // 2, a * P:(a + 1) * P]
                    else:
                        _, half, c0, q = units[u]
                        dst = o_raw[HD * half:HD * half + HD, 0:4, :].rearrange("p j t -> p (j t)")[:, c0:c0 + q]
                    nc.scalar.activation(dst, bank(("mx", i, u))[HD * half:HD * half + HD, 0:q],
                                         ACT.Copy).then_inc(*act_evac.inc(("mx", i, u)))

                def gated_upper(m):
                    act.wait_ge(*x_ready.at((("o", i), m)))
                    nc.scalar.activation(op[0][:, m, 0:nq], xt[:, m, 0:nq], ACT.Copy).then_inc(*xhi_ready.inc((("o", i), m)))

                split(last_chunk[("vb", i, 2)] + PART_SLOTS - 1)
                for u in range(len(units) + 2):
                    if u < len(units):
                        exp(u)
                    for kind, m in filler(i, u):
                        split(last_chunk[(kind, i, m)] + PART_SLOTS - 1)
                    if u == 0 and metas:
                        act.wait_ge(*pe_step.at(("meta_o", i)))
                        nc.scalar.activation(o_raw[:, 4:8, SEQ:L1], misc[:, 3, 0:4 * META].rearrange("p (j t) -> p j t", j=4),
                                             ACT.Copy).then_inc(*act_step.inc(("meta_o", i)))
                    if 1 <= u <= len(units):
                        turn(u - 1)
                    if u >= 2:
                        mixed(u - 2)
                    for kind, m in filler(i, u - 1):
                        if kind == "gate":
                            act.wait_ge(*dve_evac.at((kind, i, m)))
                            if 2 <= m < DT:
                                act.wait_ge(*dve_step.at(("zg", i, m - 2)))
                            dst = z_tanh[:, m % 2, 0:nq] if m < DT else gates[:, m, 0:nq]
                            nc.scalar.activation(dst, gates[:, m, 0:nq], ACT.Tanh,
                                                 scale=0.5).then_inc(*act_step.inc(("tanh", i, m)))
                    for m in gated_at(i, u):
                        gated_upper(m)
                gated_upper(3)
                for m in range(DT):
                    split(last_chunk[("ya", i, m)] + PART_SLOTS - 1)
                    act.wait_ge(*x_ready.at((("mix", i), m)))
                    nc.scalar.activation(xp[0][:, m, 0:nq], xt[:, m, 0:nq], ACT.Copy).then_inc(*xhi_ready.inc((("mix", i), m)))
                for m in range(DT):
                    split(last_chunk[("out", i, m)] + PART_SLOTS - 1)
                    act.wait_ge(*dve_evac.at(("out", i, m)))
                    act.wait_ge(*xlo_ready.at((("mix", i), m)))
                    if i == LAYERS - 1:
                        act.wait_ge(*dve_step.at("fga"))
                        input_parts(m, SEQ, "a", fga[:, m:m + 1], op[0], "final")
                        nc.scalar.activation(num[:, m, :], h[:, m, 0:SEQ], ACT.Square,
                                             scale=v("final_g", m)).then_inc(*sq_ready.inc(("a", m)))
                    else:
                        input_parts(m, L1, ("x", i + 1), v("norm_g", 8 * (i + 1) + m), op[0], ("x", i + 1))
            split(last_chunk[("mq", 1)] + PART_SLOTS - 1)
            act.wait_ge(*dve_step.at("ab"))
            nc.scalar.activation(ln1[:], ab[:], ACT.Exp, scale=-1.0).then_inc(*act_step.inc("e1"))
            act.wait_ge(*act_step.at("e1"))
            nc.scalar.activation(ln1[:], ln1[:], ACT.Ln, bias=1.0).then_inc(*act_step.inc("ln1"))
            split(last_chunk[("mk", 3)] + PART_SLOTS - 1)
            split(last_chunk[("mv", 0, 0)] - CH + PART_SLOTS)
            act.wait_ge(*dve_step.at("fm"))
            nc.scalar.activation(floor[:], floor[:], ACT.Exp).then_inc(*act_step.inc("floor"))
            split(last_chunk[("mv", 1, 1)] + PART_SLOTS - 1)
            for s in range(M_HEADS + 1):
                split(last_chunk[("mo", s)] + PART_SLOTS - 1)
                if s < M_HEADS:
                    act.wait_ge(*dve_step.at(("d1", s)))
                    nc.scalar.activation(dmat[:, s, 0:SEQ], dmat[:, s, 0:SEQ], ACT.Exp, bias=a_tok[:, 0, s:s + 1])
                    nc.scalar.activation(dmat[:, s, SEQ:384], dmat[:, s, SEQ:384], ACT.Exp,
                                         bias=a_tok[:, 1, s:s + 1]).then_inc(*act_step.inc(("dexp", s)))
                if s:
                    hd = s - 1
                    act.wait_ge(*pe_step.at(("num", hd)))
                    nc.scalar.activation(num[:, 2 * hd:2 * hd + 2, :], misc[:, 3, :].rearrange("p (j t) -> p j t", j=2),
                                         ACT.Copy).then_inc(*act_step.inc(("num", hd)))
            for m in range(DT):
                split(last_chunk[("mo", m)] + PART_SLOTS - 1)
                act.wait_ge(*dve_evac.at(("mo", m)))
                nc.scalar.activation(og[:, m, :], og[:, m, :], ACT.Sigmoid).then_inc(*act_step.inc(("so", m)))
            upper("mlstm", ys_hi, SEQ)

            def residual(kind, before, sq_key, inputs):
                for m in range(DT):
                    split(last_chunk[kind + (m,)] + PART_SLOTS - 1)
                    act.wait_ge(*dve_evac.at(kind + (m,)))
                    if before is not None:
                        act.wait_ge(*(xlo_ready_dve if m % 2 else xlo_ready).at((before, m)))
                    for key, gain, at, dst in inputs:
                        input_parts(m, SEQ, key, v(gain, at + m), dst, sq_key if key == sq_key else None)

            def ffn(l):
                for j in range(FFT + 2):
                    for c, (kind, dst) in enumerate((("uv", cv), ("ug", cg))):
                        if j < FFT:
                            split(last_chunk[(kind, l, j)] + PART_SLOTS - 1)
                        if 1 <= j <= FFT:
                            k = j - 1
                            act.wait_ge(*dve_evac.at((kind, l, k)))
                            if k >= 2:
                                act.wait_ge(*xlo_ready.at((("act", l), k - 2)))
                            w = v("conv_w", ((l * 3 + 2) * 2 + c) * FFT + k)
                            b = v("conv_b", (l * 2 + c) * FFT + k)
                            nc.scalar.activation(dst[:, k % 2, :], up[:, k % 2, c, :], ACT.Identity, bias=b,
                                                 scale=w).then_inc(*act_step.inc((kind, l, k)))
                    if j >= 2:
                        k = j - 2
                        act.wait_ge(*dve_step.at(("conv", "ug", l, k)))
                        nc.scalar.activation(cg[:, k % 2, :], cg[:, k % 2, :], ACT.Silu).then_inc(*act_step.inc(("sg", l, k)))
                        act.wait_ge(*pool_step.at(("prod", l, k)))
                        nc.scalar.activation(a_hi[:, k, :], cv[:, k % 2, :], ACT.Copy).then_inc(*xhi_ready.inc((("act", l), k)))
                if l == 0:
                    residual(("down", 0), None, "kv", (("kv", "kv_norm", 0, xs_hi), ("b", "b_norm", 0, ys_hi)))
                else:
                    for m in range(DT):
                        split(last_chunk[("down", 1, m)] + PART_SLOTS - 1)

            residual(("mout",), "mlstm", ("f", 0), ((("f", 0), "f_norm", 0, xs_hi),))
            ffn(0)

            def raw_head(kind, base, m):
                done((kind, m))
                nc.scalar.activation(qk2[:, base + m, :], bank((kind, m))[:, 0:SEQ],
                                     ACT.Copy).then_inc(*act_evac.inc((kind, m)))

            for m in range(DT):
                raw_head("kk", 0, m)
            split(last_chunk[("vv", 1, 1)] + PART_SLOTS - 1)

            def upper2(u):
                hd, t = units2[u]
                act.wait_ge(*tile_done.at(("mx2", u)))
                nc.scalar.activation(xs_hi[:, hd, t * P:(t + 1) * P], bank(("mx2", u))[:, 0:P],
                                     ACT.Copy).then_inc(*xhi_ready.inc(("attn", u)))

            for m in range(DT):
                raw_head("qq", 8, m)
                for u in attention_steps(m):
                    n = first_unit(LAYERS) + u
                    if 2 <= u < UNITS2 + 2:
                        k = u - 2
                        keys = (units2[k][1] + 1) * P
                        act.wait_ge(*turned.at(n - 2))
                        if k >= 2:
                            act.wait_ge(*tile_done.at(("mx2", k - 2)))
                        nc.scalar.activation(pt2[:, k % 2, 0:keys], misc[:, 2, 0:keys],
                                             ACT.Copy).then_inc(*turned_copied.inc(n - 2))
                    if u < UNITS2:
                        keys = (units2[u][1] + 1) * P
                        act.wait_ge(*max_ready.at(n))
                        if u >= 3:
                            act.wait_ge(*turned.at(n - 3))
                        b = u % 3
                        nc.scalar.activation(probs2[:, b, 0:keys], misc[:, u % 2, 0:keys], ACT.Exp, bias=nmax[:, b:b + 1],
                                             accum_out=rsum[:, b:b + 1]).then_inc(*exp_ready.inc(n))
                    if u >= 3:
                        upper2(u - 3)
            residual(("aout",), None, ("f", 1), ((("f", 1), "f_norm", 8, ys_hi),))
            ffn(1)

        @block.vector
        def _(dve):
            at = {"next": 0}

            def split(upto):
                for c in range(at["next"], min(upto + 1, n_chunks)):
                    dve.wait_ge(*hi_ready.at(c))
                    nc.vector.tensor_tensor(w_lo[:, c % PART_SLOTS, :], raw[:, c % RAW_SLOTS, :],
                                            w_hi[:, c % PART_SLOTS, :].bitcast(F32),
                                            ALU.subtract).then_inc(*lo_ready.inc(c))
                    at["next"] = c + 1

            def done(name):
                split(last_chunk[name] + PART_SLOTS - 2)
                dve.wait_ge(*tile_done.at(name))

            def step(ins, key):
                ins.then_inc(*dve_step.inc(key))
                dve.wait_ge(*dve_step.at(key))

            def variance(key, tts):
                dve.wait_ge(*stats_done.at(key))
                if len(tts) == 3:
                    step(nc.vector.tensor_scalar(var[0:META, 2:3], misc[0:META, 3, 2:3], 1.0 / D, EPS, ALU.mult, ALU.add),
                         ("var", key))
                nc.vector.tensor_scalar(var[:, 0:2], misc[:, 3, 0:2], 1.0 / D, EPS, ALU.mult,
                                        ALU.add).then_inc(*var_ready.inc(key))
                dve.wait_ge(*var_ready.at(key))
                step(nc.vector.tensor_scalar(eps_var[:, 0:3], var[:, 0:3], EPS, None, ALU.mult), ("eps_var", key))

            def factors(key, n):
                dve.wait_ge(*bcast_done.at(key))
                step(nc.vector.tensor_copy(rb_sb[:, 0:n], misc[:, 2, 0:n]), ("rb_sb", key))

            def low_part(m, cols, key, gain, upper_, dst):
                dve.wait_ge(*xhi_ready.at((key, m)))
                nc.vector.scalar_tensor_tensor(dst[:, m, 0:cols], h[:, m, 0:cols], gain, upper_[:, m, 0:cols].bitcast(F32),
                                               ALU.mult, ALU.subtract).then_inc(*xlo_ready_dve.inc((key, m)))

            nc.vector.memset(mhalf[:], -0.5)
            nc.vector.memset(var[:], 1.0)
            nc.vector.memset(rstd[:], 1.0)
            nc.vector.memset(rtok[:], 1.0).then_inc(*dve_step.inc("mhalf"))
            dve.wait_ge(*inputs_loaded.at("vec"))
            for i in range(LAYERS):
                nc.vector.tensor_scalar(qscale[:, i:i + 1], v("qg", i), HD ** -0.5, None,
                                        ALU.mult).then_inc(*dve_step.inc(("qscale", i)))
            nc.vector.tensor_scalar(qscale[:, 2:3], v("b_q_norm"), P ** -0.5, None, ALU.mult).then_inc(*dve_step.inc("qscale2"))
            nc.vector.tensor_tensor(fga[:, :], v("final_g", 0, DT), v("a_norm", 0, DT), ALU.mult).then_inc(*dve_step.inc("fga"))
            dve.wait_ge(*act_step.at("gw_hi"))
            a, n = VECS["w_gates"]
            nc.vector.tensor_tensor(gw_lo[:, :], vec[:, a:a + n], gw_hi[:, :].bitcast(F32),
                                    ALU.subtract).then_inc(*dve_step.inc("gw_lo"))
            for m in range(DT):
                low_part(m, L1, ("x", 0), v("norm_g", m), xs_hi, xs_lo)
                if m == 3:
                    split(0)
            split(1)
            for i in range(LAYERS):
                key = ("x", i)
                op = pair[1 - i % 2]
                units, nq, metas = layer_units(i), Q_COLS[i], Q_COLS[i] > SEQ
                split(last_chunk[("ka", i)] + PART_SLOTS - 1)
                for j, name in enumerate([("ka", i)] + [("qa", i, m) for m in range(4)]):
                    split(last_chunk[name] + PART_SLOTS - 2)
                    dve.wait_ge(*act_evac.at(name))
                    n = nq if j else L1
                    nc.vector.tensor_tensor(qf[:, j, 0:n], rq[:, j, 0:n], rq[:, j, 0:n],
                                            ALU.mult).then_inc(*dve_step.inc(("qsq", i, j)))
                    if j == stats_after(i) + 1:
                        variance(key, TT1)
                    if j == 2 * stats_after(i) + 2:
                        factors(key, L1)
                nc.vector.tensor_scalar(xg[:, 0, :], rq[:, 0, :], v("kg", i), None, ALU.mult)
                nc.vector.tensor_scalar(xg[:, 1:5, 0:nq], rq[:, 1:5, 0:nq], qscale[:, i:i + 1], None,
                                        ALU.mult).then_inc(*dve_step.inc(("xg", i)))

                def head_tile(kind, m):
                    done((kind, i, m))
                    dst, scale = (qn, HD ** -0.5) if kind == "qb" else (kn, 1.0)
                    n = nq if kind == "qb" else L1
                    nc.vector.scalar_tensor_tensor(dst[:, m, 0:n], bank((kind, i, m))[:, 0:n], scale, rb_sb[:, 0:n],
                                                   ALU.mult, ALU.mult).then_inc(*dve_evac.inc((kind, i, m)))

                def rope(j):
                    n = nq if j else L1
                    dve.wait_ge(*pe_step.at(("rot", i, j)))
                    step(nc.vector.tensor_tensor(t2[:, 0:n], misc[:, j % 2, 0:n], const("sin1")[:, 0:n], ALU.mult), ("t2", i, j))
                    dve.wait_ge(*pool_step.at(("t1", i, j)))
                    step(nc.vector.tensor_tensor(t2[:, 0:n], rq[:, j, 0:n], t2[:, 0:n], ALU.add), ("t3", i, j))
                    dve.wait_ge(*pe_step.at(("rb", i, j)))
                    step(nc.vector.tensor_tensor(qf[:, j, 0:n], t2[:, 0:n], misc[:, 2 + j % 2, 0:n], ALU.mult), ("qf", i, j))

                head_tile("qb", 0)
                head_tile("qb", 1)
                dve.wait_ge(*stats_done.at(("qk", i)))
                last = 30 if metas else 22
                step(nc.vector.tensor_scalar(var[0:META, 20:last], misc[0:META, 3, 20:last], 1.0 / HD, eps_var[0:META, 2:3],
                                             ALU.mult, ALU.add), ("var", "qk", i))
                for t in range(2):
                    ins = nc.vector.tensor_scalar(var[:, 10 * t:10 * t + 10], misc[:, 3, 10 * t:10 * t + 10], 1.0 / HD,
                                                  eps_var[:, t:t + 1], ALU.mult, ALU.add)
                ins.then_inc(*var_ready.inc(("qk", i)))
                for m in (2, 3):
                    head_tile("qb", m)
                head_tile("kb", 0)
                dve.wait_ge(*pe_step.at(("rt", i)))
                nc.vector.tensor_copy(rrow[:, :], misc[0:10, 3, 0:L1]).then_inc(*dve_step.inc(("rrow", i)))
                head_tile("kb", 1)
                if i == 0:
                    dve.wait_ge(*cst_loaded.at("cst"))
                rope(0)
                rope(1)
                head_tile("kb", 2)
                rope(2)
                head_tile("kb", 3)
                rope(3)
                for t in range(3):
                    done(("va", i, t))
                    tn = TT1[t][1]
                    nc.vector.tensor_scalar(v_sb[0:tn, t, 0:P], bank(("va", i, t))[0:tn, 0:P], rtok[0:tn, t:t + 1], None,
                                            ALU.mult).then_inc(*dve_evac.inc(("va", i, t)))
                rope(4)
                if metas:
                    dve.wait_ge(*pe_step.at(("meta_s", i)))
                    s3 = misc[0:META, 0:2, 0:64].rearrange("p b (h k) -> p b h k", h=4)
                    p3 = pm[:, :].rearrange("p (b h k) -> p b h k", b=2, h=4)
                    m3, z3 = (ms[:, c:c + 8].rearrange("p (b h) -> p b h", b=2) for c in (0, 8))
                    step(nc.vector.tensor_reduce(m3, s3, AX_X, ALU.max), ("meta_m", i))
                    nc.vector.tensor_tensor(p3, s3, m3.unsqueeze(3).to_broadcast([META, 2, 4, META]),
                                            ALU.subtract).then_inc(*dve_step.inc(("meta_x", i)))
                if metas:
                    dve.wait_ge(*act_step.at(("meta_e", i)))
                    step(nc.vector.tensor_reduce(z3, p3, AX_X, ALU.add), ("meta_z", i))
                    step(nc.vector.reciprocal(ms[:, 0:8], ms[:, 8:16]), ("meta_r", i))
                    nc.vector.tensor_tensor(p3, p3, m3.unsqueeze(3).to_broadcast([META, 2, 4, META]),
                                            ALU.mult).then_inc(*dve_step.inc(("meta_p", i)))
                for t in range(3):
                    done(("vb", i, t))
                    tn = TT1[t][1]
                    nc.vector.tensor_scalar(v_sb[0:tn, t, P:VCOLS], bank(("vb", i, t))[0:tn, :], rtok[0:tn, t:t + 1], None,
                                            ALU.mult).then_inc(*dve_evac.inc(("vb", i, t)))
                if metas:
                    dve.wait_ge(*pe_step.at(("meta_t", i)))
                    nc.vector.tensor_copy(pmt[:, :], misc[0:META, 2, 0:128]).then_inc(*dve_step.inc(("meta_pt", i)))

                def gated(m):
                    dve.wait_ge(*dve_step.at(("zg", i, m)))
                    if metas:
                        dve.wait_ge(*act_step.at(("meta_o", i)))
                    dve.wait_ge(*act_evac.at(("mx", i, last_unit(i, m))))
                    nc.vector.scalar_tensor_tensor(xt[:, m, 0:nq], o_raw[:, m, 0:nq], 0.25, gates[:, m, 0:nq], ALU.mult,
                                                   ALU.mult).then_inc(*x_ready.inc((("o", i), m)))

                def y_tile(kind, at_, m):
                    dve.wait_ge(*act_step.at(("tanh", i, at_ + m)))
                    dve.wait_ge(*tile_done.at((kind, i, m)))
                    nc.vector.scalar_tensor_tensor(gates[:, at_ + m, 0:nq], gates[:, at_ + m, 0:nq], 1.0,
                                                   bank((kind, i, m))[:, 0:nq], ALU.add,
                                                   ALU.mult).then_inc(*dve_evac.inc((kind, i, m)))

                for u in range(len(units) + 2):
                    if u < len(units):
                        n = first_unit(i) + u
                        q = P if units[u][0] == "na" else units[u][3]
                        b = u % 2
                        dve.wait_ge(*scores_done.at(n))
                        nc.vector.tensor_reduce(nmax[0:q, b:b + 1], misc[0:q, b, 0:L1], AX_X, ALU.max,
                                                negate=True).then_inc(*max_ready.inc(n))
                    if u < len(units):
                        dve.wait_ge(*exp_ready.at(n))
                        step(nc.vector.reciprocal(rinv[0:q, b:b + 1], rsum[0:q, b:b + 1]), ("rinv", n))
                        nc.vector.tensor_scalar(probs[0:q, b, :], probs[0:q, b, :], rinv[0:q, b:b + 1], None,
                                                ALU.mult).then_inc(*probs_ready.inc(n))
                    for kind, m in filler(i, u):
                        if kind == "gate":
                            done((kind, i, m))
                            nc.vector.tensor_tensor(gates[:, m, 0:nq], bank((kind, i, m))[:, 0:nq], rb_sb[:, 0:nq],
                                                    ALU.mult).then_inc(*dve_evac.inc((kind, i, m)))
                        else:
                            split(last_chunk[(kind, i, m)] + PART_SLOTS - 2)
                            y_tile(kind, 16, m)
                    for kind, m in filler(i, u - 1):
                        if kind == "gate" and m < DT:
                            dve.wait_ge(*act_step.at(("tanh", i, m)))
                            nc.vector.scalar_tensor_tensor(gates[:, m, 0:nq], z_tanh[:, m % 2, 0:nq], 1.0, gates[:, m, 0:nq], ALU.add,
                                                           ALU.mult).then_inc(*dve_step.inc(("zg", i, m)))
                    for m in gated_at(i, u):
                        gated(m)
                gated(3)
                split(last_chunk[("ya", i, 0)] + PART_SLOTS - 2)
                for m in range(DT):
                    y_tile("ya", 8, m)
                    dve.wait_ge(*dve_evac.at(("ya", i, m)))
                    dve.wait_ge(*xlo_ready.at((("o", i), m)))
                    nc.vector.tensor_tensor(xt[:, m, 0:nq], gates[:, 8 + m, 0:nq], gates[:, 16 + m, 0:nq],
                                            ALU.add).then_inc(*x_ready.inc((("mix", i), m)))
                    if m % 2:
                        split(last_chunk[("ya", i, m)] + PART_SLOTS - 1)
                for m in range(DT):
                    dve.wait_ge(*tile_done.at(("out", i, m)))
                    nc.vector.tensor_tensor(h[:, m, 0:nq], h[:, m, 0:nq], bank(("out", i, m))[:, 0:nq],
                                            ALU.add).then_inc(*dve_evac.inc(("out", i, m)))
                    if m < DT - 1:
                        split(last_chunk[("out", i, m)] + PART_SLOTS - 1)
                    if i < LAYERS - 1:
                        low_part(m, L1, ("x", i + 1), v("norm_g", 8 * (i + 1) + m), *op)
                    else:
                        low_part(m, SEQ, "a", fga[:, m:m + 1], *op)
                split(last_chunk[("out", i, DT - 1)] + PART_SLOTS - 1)
            dve.wait_ge(*stats_done.at("a"))
            step(nc.vector.tensor_scalar(var[:, 0:2], misc[:, 3, 0:2], 1.0 / D, EPS, ALU.mult, ALU.add), "var1")
            step(nc.vector.tensor_scalar(eps_var[:, 0:2], var[:, 0:2], EPS, None, ALU.mult), "eps_var1")
            for t in range(2):
                ins = nc.vector.tensor_scalar(var[:, 2 + t:3 + t], misc[:, 3, 4 + t:5 + t], 1.0 / D, eps_var[:, t:t + 1],
                                              ALU.mult, ALU.add)
            ins.then_inc(*var_ready.inc("final"))

            split(last_chunk[("mq", 1)] + PART_SLOTS - 1)
            dve.wait_ge(*pe_step.at("gate_rows"))
            nc.vector.tensor_copy(gate_rows[:], misc[0:8, 0, 0:SEQ]).then_inc(*dve_step.inc("gate_rows"))
            dve.wait_ge(*rstd_ready.at("final"))
            dve.wait_ge(*pe_step.at("gates"))
            for t in range(2):
                step(nc.vector.scalar_tensor_tensor(g8[:, t, :], misc[:, 1, 32 + 8 * t:40 + 8 * t], rtok[:, 2 + t:3 + t],
                                                    v("b_gates", 0, 8), ALU.mult, ALU.add), ("g8", t))
            nc.vector.scalar_tensor_tensor(ab[:], g8[:, :, 4:8], -1.0, g8[:, :, 4:8], ALU.mult, ALU.max).then_inc(*dve_step.inc("ab"))
            nc.vector.memset(cmax[:], 0.0).then_inc(*dve_step.inc("cmax0"))
            dve.wait_ge(*act_step.at("ln1"))
            nc.vector.scalar_tensor_tensor(lf[:], g8[:, :, 4:8], 0.0, ln1[:], ALU.min,
                                           ALU.subtract).then_inc(*dve_step.inc("lf"))
            factors("a", 2 * SEQ)
            rb12 = rb_sb[:, SEQ:2 * SEQ]
            for m in range(4):
                done(("mq", m))
                nc.vector.scalar_tensor_tensor(qk2[:, m, :], bank(("mq", m))[:, 0:SEQ], P ** -0.5, rb12, ALU.mult,
                                               ALU.mult).then_inc(*dve_evac.inc(("mq", m)))

            def key_tile(m):
                done(("mk", m))
                nc.vector.tensor_tensor(qk2[:, 4 + m, :], bank(("mk", m))[:, 0:SEQ], rb12,
                                        ALU.mult).then_inc(*dve_evac.inc(("mk", m)))

            key_tile(0)
            key_tile(1)
            dve.wait_ge(*pe_step.at("a_row"))
            step(nc.vector.tensor_copy(nf[:], misc[:, 1, 16:24].rearrange("p (t g) -> p t g", t=2)), "nf")
            nc.vector.tensor_tensor(a_tok[:], g8[:, :, 0:4], nf[:], ALU.add).then_inc(*dve_step.inc("a_tok"))
            step(nc.vector.tensor_scalar(cmax[:, 0, P:], misc[0:M_HEADS, 0, 0:SEQ], 0.0, None, ALU.max), "m0")
            b = 0
            for r in range(8):
                d = 1 << r
                step(nc.vector.tensor_tensor(cmax[:, 1 - b, P:], cmax[:, b, P:], cmax[:, b, P - d:P + SEQ - d], ALU.max),
                     ("m", r) if r < 7 else "cmax")
                b = 1 - b
                if r == 4:
                    key_tile(2)
                    split(last_chunk[("mk", 3)] + PART_SLOTS - 2)
                elif r == 6:
                    key_tile(3)
            first_v = last_chunk[("mv", 0, 0)] - CH + 1
            split(first_v + 3)
            dve.wait_ge(*pe_step.at("m_tok"))
            nc.vector.tensor_tensor(floor[:], nf[:], misc[:, 1, 24:32].rearrange("p (t g) -> p t g", t=2),
                                    ALU.subtract).then_inc(*dve_step.inc("fm"))
            dve.wait_ge(*xlo_ready_dve.at(("a", 7)))
            for m in range(DT):
                nc.vector.scalar_tensor_tensor(h[:, m, 0:SEQ], h[:, m, 0:SEQ], v("final_g", m), rb_sb[:, 0:SEQ], ALU.mult,
                                               ALU.mult).then_inc(*dve_step.inc(("final", m)))
                split(first_v + min(m + 4, CH + 1))
            split(last_chunk[("mv", 1, 1)] + PART_SLOTS - 2)
            for t in range(2):
                for s in range(2):
                    if (t, s) == (1, 0):
                        split(last_chunk[("mv", 1, 1)] + PART_SLOTS - 1)
                    dve.wait_ge(*tile_done.at(("mv", t, s)))
                    nc.vector.tensor_scalar(v2[:, t, 512 * s:512 * s + 512], bank(("mv", t, s)), rtok[:, 2 + t:3 + t], None,
                                            ALU.mult).then_inc(*dve_evac.inc(("mv", t, s)))
            ct = const("causal_t")

            def o_tile(m):
                done(("mo", m))
                nc.vector.tensor_tensor(og[:, m, :], bank(("mo", m))[:, 0:SEQ], rb12, ALU.mult).then_inc(*dve_evac.inc(("mo", m)))

            def gate_sums(m):
                dve.wait_ge(*act_step.at(("so", m)))
                dve.wait_ge(*dve_step.at(("nsq", m // 2)))
                nc.vector.scalar_tensor_tensor(num[:, m, :], num[:, m, :], v("a_h_norm", m), og[:, m, :], ALU.mult,
                                               ALU.mult).then_inc(*dve_step.inc(("hn", m)))

            for s in range(M_HEADS + 1):
                o_tile(s)
                if s < M_HEADS:
                    dve.wait_ge(*pe_step.at(("mb", s)))
                    nc.vector.scalar_tensor_tensor(dmat[:, s, 0:SEQ], misc[:, 2, 0:SEQ], -1.0, ct, ALU.mult, ALU.add)
                    nc.vector.scalar_tensor_tensor(dmat[:, s, SEQ:384], misc[:, 2, P:SEQ], -1.0, ct[:, 0:P], ALU.mult,
                                                   ALU.add).then_inc(*dve_step.inc(("d1", s)))
                    dve.wait_ge(*act_step.at(("dexp", s)))
                    dve.wait_ge(*pe_step.at(("mst", s)))
                    nc.vector.tensor_tensor(dmat[:, s, :], dmat[:, s, :], misc[:, 0, 0:384],
                                            ALU.mult).then_inc(*dve_step.inc(("sd", s)))
                if s:
                    hd = s - 1
                    dve.wait_ge(*act_step.at(("num", hd)))
                    nc.vector.tensor_tensor(xt[:, 2 * hd:2 * hd + 2, 0:SEQ], num[:, 2 * hd:2 * hd + 2, :],
                                            num[:, 2 * hd:2 * hd + 2, :], ALU.mult).then_inc(*dve_step.inc(("nsq", hd)))
            o_tile(5)
            for m in range(3):
                gate_sums(m)
            dve.wait_ge(*pe_step.at("nss"))
            dve.wait_ge(*act_step.at("floor"))
            sums = misc[:, 1, 0:8].rearrange("p (t g) -> p t g", t=2)
            step(nc.vector.scalar_tensor_tensor(den[:], sums, -1.0, floor[:], ALU.mult, ALU.max), "-den")
            step(nc.vector.tensor_tensor(den[:], sums, den[:], ALU.max), "den")
            step(nc.vector.reciprocal(den[:], den[:]), "rden")
            f3 = fac[:, :].rearrange("p (t g) -> p t g", t=2)
            v3 = var[:, 0:8].rearrange("p (t g) -> p t g", t=2)
            step(nc.vector.tensor_tensor(f3, den[:], den[:], ALU.mult), "rden2")
            step(nc.vector.tensor_tensor(f3, f3, misc[:, 1, 8:16].rearrange("p (t g) -> p t g", t=2), ALU.mult), "nvar")
            nc.vector.tensor_scalar(v3, f3, 1.0 / 256, EPS, ALU.mult, ALU.add).then_inc(*var_ready.inc("mlstm"))
            o_tile(6)
            gate_sums(3)
            gate_sums(4)
            dve.wait_ge(*rstd_ready.at("mlstm"))
            nc.vector.tensor_tensor(f3, rstd[:, 0:8].rearrange("p (t g) -> p t g", t=2), den[:],
                                    ALU.mult).then_inc(*dve_step.inc("fac"))
            gate_sums(5)
            o_tile(7)
            gate_sums(6)
            for m in range(DT):
                if m == 3:
                    gate_sums(7)
                dve.wait_ge(*pe_step.at(("fb", m // 2)))
                dve.wait_ge(*dve_step.at(("hn", m)))
                nc.vector.tensor_tensor(xt[:, m, 0:SEQ], num[:, m, :], misc[:, FB[m // 2], 0:SEQ],
                                        ALU.mult).then_inc(*x_ready.inc(("mlstm", m)))
                for k in {2: [1], 4: [3], 6: [5], 7: [7]}.get(m, []):
                    dve.wait_ge(*xhi_ready.at(("mlstm", k)))
                    nc.vector.tensor_tensor(ys_lo[:, k, 0:SEQ], xt[:, k, 0:SEQ], ys_hi[:, k, 0:SEQ].bitcast(F32),
                                            ALU.subtract).then_inc(*xlo_ready_dve.inc(("mlstm", k)))

            def residual(kind, inputs, before=None):
                for m in range(DT):
                    split(last_chunk[kind + (m,)] + PART_SLOTS - 2)
                    dve.wait_ge(*tile_done.at(kind + (m,)))
                    if before:
                        dve.wait_ge(*dve_step.at((before, m)))
                    nc.vector.tensor_tensor(h[:, m, 0:SEQ], h[:, m, 0:SEQ], bank(kind + (m,))[:, 0:SEQ],
                                            ALU.add).then_inc(*dve_evac.inc(kind + (m,)))
                    if m < DT - 1:
                        split(last_chunk[kind + (m,)] + PART_SLOTS - 1)
                    for key, gain, at_, (hi, lo) in inputs:
                        low_part(m, SEQ, key, v(gain, at_ + m), hi, lo)
                split(last_chunk[kind + (DT - 1,)] + PART_SLOTS - 1)

            def ffn(l):
                split(last_chunk[("uv", l, 0)] + PART_SLOTS - 1)
                variance(("f", l), TT2)
                factors(("f", l), SEQ)
                for j in range(FFT + 1):
                    for c, (kind, dst) in enumerate((("uv", cv), ("ug", cg))):
                        if j < FFT:
                            done((kind, l, j))
                            if j >= 2:
                                dve.wait_ge(*dve_step.at(("conv", kind, l, j - 2)))
                                dve.wait_ge(*act_step.at((kind, l, j - 2)))
                            nc.vector.tensor_tensor(up[:, j % 2, c, :], bank((kind, l, j))[:, 0:SEQ], rb_sb[:, 0:SEQ],
                                                    ALU.mult).then_inc(*dve_evac.inc((kind, l, j)))
                        if j >= 1:
                            k = j - 1
                            dve.wait_ge(*act_step.at((kind, l, k)))
                            u, y = up[:, k % 2, c, :], dst[:, k % 2, :]
                            w = [v("conv_w", ((l * 3 + s) * 2 + c) * FFT + k) for s in range(2)]
                            step(nc.vector.scalar_tensor_tensor(y[:, 1:SEQ], u[:, 0:SEQ - 1], w[1], y[:, 1:SEQ], ALU.mult,
                                                                ALU.add), ("conv1", kind, l, k))
                            nc.vector.scalar_tensor_tensor(y[:, 2:SEQ], u[:, 0:SEQ - 2], w[0], y[:, 2:SEQ], ALU.mult,
                                                           ALU.add).then_inc(*dve_step.inc(("conv", kind, l, k)))
                if l == 0:
                    residual(("down", 0), (("kv", "kv_norm", 0, pair[0]), ("b", "b_norm", 0, pair[1])))
                else:
                    residual(("down", 1), ())

            residual(("mout",), ((("f", 0), "f_norm", 0, pair[0]),), "final")
            ffn(0)
            split(last_chunk[("kk", 0)] + PART_SLOTS - 1)
            variance("kv", TT2)

            def head_squares(kind, g):
                name = (kind, g % 8)
                split(last_chunk[name] + PART_SLOTS - 2)
                dve.wait_ge(*act_evac.at(name))
                nc.vector.tensor_tensor(xt[:, g % 8, 0:SEQ], qk2[:, g, :], qk2[:, g, :], ALU.mult).then_inc(*dve_step.inc(("sq2", g)))

            def head_variance(c, n, key):
                for t in range(2):
                    a = c + 8 * t
                    ins = nc.vector.tensor_scalar(var[:, a:a + n], misc[:, 3, a:a + n], 1.0 / P, eps_var[:, t:t + 1], ALU.mult,
                                                  ALU.add)
                ins.then_inc(*var_ready.inc(key))

            def rope2(g, o):
                ta = rope_t[:, g % 2, 0:SEQ]
                step(nc.vector.tensor_tensor(ta, o[0:ROT, 0:SEQ], const("sin2", ROT), ALU.mult), ("ra", g))
                dve.wait_ge(*pool_step.at(("xc", g)))
                x2 = qk2[0:ROT, g, :]
                step(nc.vector.tensor_tensor(x2, ta, x_cos[:, g, :], ALU.add), ("rs", g))
                return nc.vector.tensor_tensor(qk2[:, g, :], qk2[:, g, :], o[:, SEQ:2 * SEQ], ALU.mult)

            for m in range(DT):
                head_squares("kk", m)
            dve.wait_ge(*rstd_ready.at("kv"))
            dve.wait_ge(*pe_step.at(("st2", 7)))
            head_variance(0, 8, "k2")
            dve.wait_ge(*dve_step.at(("sq2", 7)))
            nc.vector.tensor_scalar(qk2[:, 0:8, :], qk2[:, 0:8, :], v("k_norm"), None, ALU.mult).then_inc(*dve_step.inc("xk"))
            dve.wait_ge(*dve_step.at("xk"))
            first_v = last_chunk[("vv", 0, 0)] - CH + 1
            for c in range(3, 7):
                split(first_v + c + PART_SLOTS - 1)
                for g in (2 * c - 6, 2 * c - 5):
                    dve.wait_ge(*pe_step.at(("rope2", g)))
                    step(rope2(g, misc[:, g % 2, :]), ("rope2", g))
            split(last_chunk[("vv", 1, 1)] + PART_SLOTS - 2)
            for t in range(2):
                for s in range(2):
                    if (t, s) == (1, 0):
                        split(last_chunk[("vv", 1, 1)] + PART_SLOTS - 1)
                    dve.wait_ge(*tile_done.at(("vv", t, s)))
                    nc.vector.tensor_scalar(v2[:, t, 512 * s:512 * s + 512], bank(("vv", t, s)), rtok[:, t:t + 1], None,
                                            ALU.mult).then_inc(*dve_evac.inc(("vv", t, s)))

            def query_rope(hd):
                dve.wait_ge(*tile_done.at(("rope", hd)))
                rope2(8 + hd, bank(("rope", hd))).then_inc(*dve_evac.inc(("rope", hd)))

            def query_factors(p):
                dve.wait_ge(*dve_step.at(("sq2", 9 + 2 * p)))
                x2 = qk2[:, 8 + 2 * p:10 + 2 * p, :]
                nc.vector.tensor_scalar(x2, x2, qscale[:, 2:3], None, ALU.mult).then_inc(*dve_step.inc(("xq", p)))
                dve.wait_ge(*pe_step.at(("st2", 9 + 2 * p)))
                head_variance(16 + 2 * p, 2, ("q2", p))

            for m in range(DT):
                head_squares("qq", 8 + m)
                if m in (2, 4, 6):
                    query_factors(m // 2 - 1)
                for hd in rope_at(m):
                    query_rope(hd)
                for u in attention_steps(m):
                    for hd in rope_at(step=u):
                        query_rope(hd)
                    if u < UNITS2:
                        n = first_unit(LAYERS) + u
                        keys = (units2[u][1] + 1) * P
                        b = u % 3
                        dve.wait_ge(*scores_done.at(n))
                        nc.vector.tensor_reduce(nmax[:, b:b + 1], misc[:, u % 2, 0:keys], AX_X, ALU.max,
                                                negate=True).then_inc(*max_ready.inc(n))
                        dve.wait_ge(*exp_ready.at(n))
                        step(nc.vector.reciprocal(rinv[:, b:b + 1], rsum[:, b:b + 1]), ("rinv", n))
                        nc.vector.tensor_scalar(probs2[:, b, 0:keys], probs2[:, b, 0:keys], rinv[:, b:b + 1], None,
                                                ALU.mult).then_inc(*probs_ready.inc(n))
                    if u >= 3:
                        hd, t = units2[u - 3]
                        part = slice(t * P, (t + 1) * P)
                        dve.wait_ge(*xhi_ready.at(("attn", u - 3)))
                        nc.vector.tensor_tensor(xs_lo[:, hd, part], bank(("mx2", u - 3))[:, 0:P], xs_hi[:, hd, part].bitcast(F32),
                                                ALU.subtract).then_inc(*dve_evac.inc(("mx2", u - 3)))
                    if u == 7:
                        query_factors(3)
            residual(("aout",), ((("f", 1), "f_norm", 8, pair[1]),))
            ffn(1)

        @block.gpsimd
        def _(pool):
            def root(key, dst, c0, c1):
                pool.wait_ge(*var_ready.at(key))
                nc.gpsimd.tensor_tensor(dst[:, c0:c1], var[:, c0:c1], mhalf[:, c0:c1], ALU.pow).then_inc(*rstd_ready.inc(key))

            def lower(key, dst, upper_, cols, order=range(DT)):
                for m in order:
                    pool.wait_ge(*xhi_ready.at((key, m)))
                    nc.gpsimd.tensor_tensor(dst[:, m, 0:cols], xt[:, m, 0:cols], upper_[:, m, 0:cols].bitcast(F32),
                                            ALU.subtract).then_inc(*xlo_ready.inc((key, m)))

            def add_square(key, m, cols, src=xt, n=0):
                pool.wait_ge(*sq_ready.at((key, m)))
                if m >= 2:
                    pool.wait_ge(*pool_step.at(("sum", key, m - 1)))
                if m >= 1:
                    o = (sq_sum, sq_sum2)[n][:, 0:cols]
                    nc.gpsimd.tensor_tensor(o, src[:, 0, 0:cols] if m == 1 else o, src[:, m, 0:cols],
                                            ALU.add).then_inc(*pool_step.inc(("sum", key, m)))

            pool.wait_ge(*dve_step.at("mhalf"))
            for m in range(DT):
                add_square(("x", 0), m, L1)
            for i in range(LAYERS):
                xp, op = pair[i % 2], pair[1 - i % 2]
                nq = Q_COLS[i]
                root(("x", i), rtok, 0, 3)
                root(("qk", i), rstd, 0, 30)
                if i == 0:
                    pool.wait_ge(*cst_loaded.at("cst"))
                pool.wait_ge(*dve_step.at(("xg", i)))
                for j in range(5):
                    n = nq if j else L1
                    nc.gpsimd.tensor_tensor(rq[:, j, 0:n], xg[:, j, 0:n], const("cos1")[:, 0:n], ALU.mult).then_inc(*pool_step.inc(("t1", i, j)))
                pool.wait_ge(*bias_loaded.at((i, 1, NA_HEADS - 1)))
                b3 = bias[:, :, :].rearrange("p h (d j) -> p (h d) j", j=GRID_W)
                nc.gpsimd.tensor_tensor(b3, b3, const("window").unsqueeze(1).to_broadcast([P, 6 * NA_HEADS, GRID_W]),
                                        ALU.add).then_inc(*pool_step.inc(("bias", i)))
                lower(("o", i), op[1], op[0], nq, (4, 5, 6, 7, 0, 1, 2, 3))
                lower(("mix", i), xp[1], xp[0], nq)
                for m in range(DT):
                    if i < LAYERS - 1:
                        add_square(("x", i + 1), m, L1)
                    else:
                        add_square("final", m, SEQ)
                        add_square("a", m, SEQ, num, 1)
            root("final", rtok, 0, 4)
            for hd in range(M_HEADS):
                pool.wait_ge(*dve_step.at(("nsq", hd)))
                nc.gpsimd.tensor_tensor(xt[:, 2 * hd, 0:SEQ], xt[:, 2 * hd, 0:SEQ], xt[:, 2 * hd + 1, 0:SEQ],
                                        ALU.add).then_inc(*pool_step.inc(("head_sum", hd)))
            root("mlstm", rstd, 0, 8)
            lower("mlstm", ys_lo, ys_hi, SEQ, range(0, DT, 2))

            def ffn(l):
                for m in range(DT):
                    add_square(("f", l), m, SEQ)
                root(("f", l), rtok, 0, 2)
                for j in range(FFT):
                    pool.wait_ge(*act_step.at(("sg", l, j)))
                    nc.gpsimd.tensor_tensor(cv[:, j % 2, :], cv[:, j % 2, :], cg[:, j % 2, :],
                                            ALU.mult).then_inc(*pool_step.inc(("prod", l, j)))
                    pool.wait_ge(*xhi_ready.at((("act", l), j)))
                    nc.gpsimd.tensor_tensor(a_lo[:, j, :], cv[:, j % 2, :], a_hi[:, j, :].bitcast(F32),
                                            ALU.subtract).then_inc(*xlo_ready.inc((("act", l), j)))

            def times_cos(g):
                nc.gpsimd.tensor_tensor(x_cos[:, g, :], qk2[0:ROT, g, :], const("cos2", ROT),
                                        ALU.mult).then_inc(*pool_step.inc(("xc", g)))

            ffn(0)
            for m in range(DT):
                add_square("kv", m, SEQ)
            root("kv", rtok, 0, 2)
            root("k2", rstd, 0, 16)
            pool.wait_ge(*dve_step.at("xk"))
            for g in range(8):
                times_cos(g)
            for p in range(4):
                pool.wait_ge(*var_ready.at(("q2", p)))
                for t in range(2):
                    a = 16 + 8 * t + 2 * p
                    ins = nc.gpsimd.tensor_tensor(rstd[:, a:a + 2], var[:, a:a + 2], mhalf[:, a:a + 2], ALU.pow)
                ins.then_inc(*rstd_ready.inc(("q2", p)))
                for g in (8 + 2 * p, 9 + 2 * p):
                    times_cos(g)
            ffn(1)
    return {name: s.marks for name, s in signals.items()}


def shape_constants():
    c = np.zeros((P, NCONST), np.float32)

    def put(name, value):
        a, n = CONSTS[name]
        value = np.asarray(value, np.float32)
        assert value.shape[1] == n, name
        c[:value.shape[0], a:a + n] = value

    put("ident", np.eye(P))
    rot = np.zeros((P, P))
    for q in range(P):
        rot[(q + 16, q) if q % 32 < 16 else (q - 16, q)] = -1.0 if q % 32 < 16 else 1.0
    put("rot1", rot)
    jrev = np.zeros((P, P))
    for q in range(P):
        jrev[GRID_W * (q // GRID_W) + GRID_W - 1 - q % GRID_W, q] = 1.0
    put("jrev", jrev)
    t = np.arange(SEQ)
    row = np.concatenate([t // GRID_W, np.zeros(META, int)]).astype(np.float32)
    col = np.concatenate([t % GRID_W, np.zeros(META, int)]).astype(np.float32)
    inv = np.float32(10000.0) ** (-np.arange(0, 32, 2, dtype=np.float32) / np.float32(32))
    ar, ac = (inv[:, None] * z[None, :] for z in (row, col))
    ang = np.concatenate([ar, ar, ac, ac] * 2, axis=0)
    put("cos1", np.cos(ang))
    put("sin1", np.sin(ang))
    cc = GRID_W - 1 - np.arange(P) % GRID_W
    start = np.clip(cc - NA_KW // 2, 0, GRID_W - NA_KW)[:, None]
    j = np.arange(GRID_W)[None, :]
    put("window", np.where((j >= start) & (j < start + NA_KW), 0.0, NEG))
    a, b = np.arange(P)[:, None], np.arange(P)[None, :]
    put("causal", np.where(b <= a, 0.0, NEG))
    put("causal_t", np.concatenate([np.where(a <= b, 0.0, NEG), np.zeros((P, P))], axis=1))
    s, u = np.arange(P)[:, None], np.arange(SEQ)[None, :]
    put("tri_neg", np.concatenate([-(s + P * k <= u).astype(np.float32) for k in range(2)], axis=1))
    put("eye2", np.concatenate([(s + P * k == u).astype(np.float32) for k in range(2)], axis=1))
    put("head_sum", np.stack([np.arange(P) < HD, np.arange(P) >= HD], axis=1))
    put("ones", np.ones((P, 2)))
    put("sel4", np.repeat(np.eye(M_HEADS), P, axis=1))
    put("sel10", np.repeat(np.eye(10), HD, axis=1))
    inv2 = np.float32(500000.0) ** (-np.arange(0, ROT, 2, dtype=np.float32) / np.float32(ROT))
    ang2 = inv2[:, None] * t[None, :].astype(np.float32)
    put("cos2", np.cos(np.concatenate([ang2, ang2])))
    put("sin2", np.sin(np.concatenate([ang2, ang2])))
    rot2 = np.zeros((ROT, ROT))
    for q in range(ROT):
        rot2[(q + 16, q) if q < 16 else (q - 16, q)] = -1.0 if q < 16 else 1.0
    put("rot2", rot2)
    return c


def cols(x):
    return np.ascontiguousarray(x).reshape(-1, P).T


def pair_heads(w, axis):
    w = np.moveaxis(w, axis, 0)
    w = w.reshape(KV, GROUP, HD, *w.shape[1:])
    w = np.swapaxes(w, 0, 1).reshape(KV * GROUP * HD, *w.shape[3:])
    return np.moveaxis(w, 0, axis)


def by_tile(w):
    k, m = w.shape
    return w.reshape(k // P, P, m // P, P).transpose(2, 0, 1, 3).reshape(-1, P, P)


def by_row(w):
    k, m = w.shape
    return w.reshape(k // P, P, m // P, P).transpose(0, 2, 1, 3).reshape(-1, P, P)


def weight_stream(inp):
    blocks = []
    for i in range(LAYERS):
        w = inp["w_in"][i]
        qa, ka, va, za, qb, kb, vb, zb, ga, gb = np.split(w, np.cumsum([512, 128, 128, 512, 512, 512, 512, 512, 1024]), axis=1)
        blocks += [by_tile(ka), by_tile(pair_heads(qa, 1)), by_tile(qb), by_tile(kb), by_row(va), by_row(vb),
                   by_tile(pair_heads(za, 1)), by_tile(zb), by_tile(ga), by_tile(gb)]
        wa, wn = by_tile(pair_heads(inp["w_o_attn"][i], 0)), by_tile(inp["w_o_na"][i])
        blocks += [wn, wa]
        blocks += [by_tile(inp["w_out"][i])]
    w = inp["a_w_in_2"][0]
    blocks += [by_tile(w[:, 0:1024]), by_row(w[:, 1024:2048]), by_tile(w[:, 2048:3072]), by_tile(inp["a_w_out_2"][0])]
    for l in range(2):
        up = by_tile(inp["f_w_up_2"][l]).reshape(2, FFT, DT, P, P).swapaxes(0, 1)
        blocks += [up.reshape(-1, P, P), by_tile(inp["f_w_down_2"][l])]
        if l == 0:
            w = inp["w_kv_2"]
            blocks += [by_tile(w[:, 0:1024]), by_row(w[:, 1024:2048]), by_tile(inp["b_w_q_2"][0]), by_tile(inp["b_w_o_2"][0])]
    stream = np.concatenate(blocks)
    return np.ascontiguousarray(stream.reshape(-1, CH, P, P).transpose(0, 2, 1, 3)).reshape(-1, P, CH * P)


def parameter_vectors(inp):
    g = inp["a_b_gates_2"][0].reshape(1, 8)
    w = inp["a_w_in_2"][0][:, 3072:3080].reshape(DT, P, 8).transpose(1, 0, 2).reshape(P, 64)
    two = lambda x: np.concatenate([x, x], axis=1).T
    parts = {
        "norm_g": cols(inp["norm_g"]), "qg": two(inp["q_norm_g"]), "kg": two(inp["k_norm_g"]),
        "final_g": cols(inp["final_norm_g"]), "a_norm": cols(inp["a_norm_2"]), "a_h_norm": cols(inp["a_h_norm_2"]),
        "kv_norm": cols(inp["kv_norm_2"]), "k_norm": cols(inp["k_norm_2"]), "b_norm": cols(inp["b_norm_2"]),
        "b_q_norm": cols(inp["b_q_norm_2"]), "f_norm": cols(inp["f_norm_2"]), "conv_w": cols(inp["f_conv_w_2"]),
        "conv_b": cols(inp["f_conv_b_2"]), "b_gates": np.broadcast_to(g, (P, 8)), "w_gates": w,
    }
    assert all(parts[n].shape == (P, k) for n, (_, k) in VECS.items())
    return np.ascontiguousarray(np.concatenate([parts[n] for n in VECS], axis=1))


def kernel(**inputs):
    import concourse.bacc as bacc
    from concourse.bass_utils import run_bass_kernel_spmd

    inp = {k: np.asarray(v) for k, v in inputs.items()}
    tokens = np.concatenate([inp["x"][0], inp["meta_tokens"]], axis=0)
    arrays = {
        "x_t": np.ascontiguousarray(tokens.T.reshape(DT, P, L1).transpose(1, 0, 2)),
        "consts": shape_constants(),
        "vecs": parameter_vectors(inp),
        "rpb": np.ascontiguousarray(inp["na_rpb"]),
        "weights": weight_stream(inp),
    }

    def build(known):
        nc = bacc.Bacc("TRN2", target_bir_lowering=False, num_devices=1)
        args = [nc.dram_tensor(n, a.shape, F32, kind="ExternalInput").ap() for n, a in arrays.items()]
        out = nc.dram_tensor("out", (P, DT, SEQ), F32, kind="ExternalOutput").ap()
        return nc, program(nc, *args, out, known)

    _, marks = build({})
    nc, _ = build(marks)
    r = run_bass_kernel_spmd(nc, [arrays], core_ids=[0])
    got = r.results[0]["out"]
    return got.transpose(2, 1, 0).reshape(1, SEQ, D)
```
